# Optimizing a Trainium2 kernel written in Bass

```python
import math
import jax, jax.numpy as jnp
from jax import lax
import numpy as np

D_MODEL = 1024
BATCH = 1
SEQ = 1024
DEPTH = 2
DEC_BATCH = 8
DEC_SEQ = 16
PAST_LEN = 512

CHUNK = 64
Q_BLOCK = 128
N_A_LAYERS = DEPTH // 2
N_B_LAYERS = DEPTH - N_A_LAYERS
GLA_HEADS = 4
GLA_DK = D_MODEL // 2
GLA_DV = D_MODEL
GLA_DKH = GLA_DK // GLA_HEADS
GLA_DVH = GLA_DV // GLA_HEADS
GATE_RANK = 16
GATE_TAU = 16.0
A_IN = 2 * GLA_DK + 2 * GLA_DV + GATE_RANK
DIFF_HEADS = 8
DIFF_HD = D_MODEL // (2 * DIFF_HEADS)
DIFF_QK = DIFF_HEADS * 2 * DIFF_HD
DIFF_V = DIFF_HEADS * 2 * DIFF_HD
ROPE_DIMS = DIFF_HD // 4
ROPE_THETA = 500000.0
D_FF = 4 * D_MODEL
DEEPNORM_ALPHA = (2 * DEPTH) ** 0.25
DEEPNORM_BETA = (8 * DEPTH) ** -0.25
LN_EPS = 1e-5
RMS_EPS = 1e-5

kernel_name = 'yoco_gla_diffattn_stream_step'

def layer_norm(x, g, b):
    xf = x.astype(jnp.float32)
    mu = jnp.mean(xf, -1, keepdims=True)
    var = jnp.mean(jnp.square(xf - mu), -1, keepdims=True)
    return ((xf - mu) * lax.rsqrt(var + LN_EPS) * g + b).astype(x.dtype)

def rms_norm(x, g):
    xf = x.astype(jnp.float32)
    return (xf * lax.rsqrt(jnp.mean(xf * xf, -1, keepdims=True) + RMS_EPS) * g).astype(x.dtype)

def partial_rope(x, pos):
    inv = 1.0 / (ROPE_THETA ** (jnp.arange(0, ROPE_DIMS, 2, dtype=jnp.float32) / ROPE_DIMS))
    ang = pos.astype(jnp.float32)[:, None] * inv[None, :]
    cos = jnp.cos(ang)[:, None, None, :]
    sin = jnp.sin(ang)[:, None, None, :]
    xr = x[..., :ROPE_DIMS].astype(jnp.float32)
    x1, x2 = xr[..., :ROPE_DIMS // 2], xr[..., ROPE_DIMS // 2:]
    rot = jnp.concatenate([x1 * cos - x2 * sin, x2 * cos + x1 * sin], -1)
    return jnp.concatenate([rot.astype(x.dtype), x[..., ROPE_DIMS:]], -1)

def gla_project(x, w_in, w_gate_up, b_gate):
    B, T, _ = x.shape
    h = x @ w_in
    q, k, v, r, gl = jnp.split(h, [GLA_DK, 2 * GLA_DK, 2 * GLA_DK + GLA_DV, 2 * GLA_DK + 2 * GLA_DV], axis=-1)
    logit = (gl @ w_gate_up + b_gate).astype(jnp.float32)
    log_a = (jax.nn.log_sigmoid(logit) / GATE_TAU).reshape(B, T, GLA_HEADS, GLA_DKH)
    q = q.reshape(B, T, GLA_HEADS, GLA_DKH) * (GLA_DKH ** -0.5)
    k = k.reshape(B, T, GLA_HEADS, GLA_DKH)
    v = v.reshape(B, T, GLA_HEADS, GLA_DVH)
    return q, k, v, log_a, r

def gla_block(S, q, k, v, log_a):
    C = q.shape[1]
    b = jnp.cumsum(log_a, axis=1)
    qf = q.astype(jnp.float32) * jnp.exp(b)
    kf = k.astype(jnp.float32) * jnp.exp(-b)
    vf = v.astype(jnp.float32)
    inter = jnp.einsum('bchk,bhkv->bchv', qf, S)
    att = jnp.einsum('bihk,bjhk->bhij', qf, kf)
    att = jnp.where(jnp.tril(jnp.ones((C, C), dtype=bool)), att, 0.0)
    intra = jnp.einsum('bhij,bjhv->bihv', att, vf)
    b_last = b[:, -1]
    k_tail = k.astype(jnp.float32) * jnp.exp(b_last[:, None] - b)
    S_new = S * jnp.exp(b_last)[..., None] + jnp.einsum('bjhk,bjhv->bhkv', k_tail, vf)
    return S_new, inter + intra

def gla_prompt(q, k, v, log_a):
    B, T = q.shape[:2]
    n = T // CHUNK

    def to_blocks(a):
        return a.reshape(B, n, CHUNK, *a.shape[2:]).swapaxes(0, 1)

    S0 = jnp.zeros((B, GLA_HEADS, GLA_DKH, GLA_DVH), jnp.float32)

    def step(S, inp):
        return gla_block(S, *inp)

    S_fin, o = lax.scan(step, S0, (to_blocks(q), to_blocks(k), to_blocks(v), to_blocks(log_a)))
    return o.swapaxes(0, 1).reshape(B, T, GLA_HEADS, GLA_DVH), S_fin

def gla_output(o, r, g_norm, w_o):
    B, T = o.shape[:2]
    o = rms_norm(o, g_norm).reshape(B, T, GLA_DV).astype(r.dtype)
    return (o * jax.nn.silu(r)) @ w_o

def shared_kv(h, w_kv, pos):
    B, T, _ = h.shape
    kv = h @ w_kv
    k, v = jnp.split(kv, [DIFF_QK], axis=-1)
    k = partial_rope(k.reshape(B, T, DIFF_HEADS, 2, DIFF_HD), pos)
    v = v.reshape(B, T, DIFF_HEADS, 2 * DIFF_HD)
    return k, v

def diff_query(x, w_q, pos):
    B, T, _ = x.shape
    q = (x @ w_q).reshape(B, T, DIFF_HEADS, 2, DIFF_HD)
    return partial_rope(q, pos) * (DIFF_HD ** -0.5)

def diff_lambda(lam, lambda_init):
    lam = lam.astype(jnp.float32)
    return jnp.exp(jnp.sum(lam[0] * lam[1])) - jnp.exp(jnp.sum(lam[2] * lam[3])) + lambda_init

def diff_attn_prompt(q, k, v, lam):
    T = q.shape[1]
    chunk_id = jnp.arange(T) // CHUNK
    outs = []
    for i in range(T // Q_BLOCK):
        qs, qe = i * Q_BLOCK, (i + 1) * Q_BLOCK
        s = jnp.einsum('bqhcd,bkhcd->bhcqk', q[:, qs:qe], k[:, :qe]).astype(jnp.float32)
        mask = chunk_id[None, :qe] <= chunk_id[qs:qe, None]
        p = jax.nn.softmax(jnp.where(mask, s, -jnp.inf), axis=-1)
        a = (p[:, :, 0] - lam * p[:, :, 1]).astype(v.dtype)
        outs.append(jnp.einsum('bhqk,bkhv->bqhv', a, v[:, :qe]))
    return jnp.concatenate(outs, axis=1)

def diff_attn_sample(q, k_new, v_new, cache_k, cache_v, lam):
    P = cache_k.shape[1]
    s_past = jnp.einsum('bqhcd,bkhcd->bhcqk', q, cache_k)
    s_new = jnp.einsum('bqhcd,bkhcd->bhcqk', q, k_new)
    s = jnp.concatenate([s_past, s_new], axis=-1).astype(jnp.float32)
    p = jax.nn.softmax(s, axis=-1)
    a = (p[:, :, 0] - lam * p[:, :, 1]).astype(v_new.dtype)
    return (jnp.einsum('bhqk,bkhv->bqhv', a[..., :P], cache_v)
            + jnp.einsum('bhqk,bkhv->bqhv', a[..., P:], v_new))

def diff_output(o, g_norm, lambda_init, w_o):
    B, T = o.shape[:2]
    o = rms_norm(o, g_norm) * (1.0 - lambda_init)
    return o.reshape(B, T, DIFF_V) @ w_o

def sqrelu_mlp(x, w_up, w_down):
    return jnp.square(jax.nn.relu(x @ w_up)) @ w_down

def run_trunk(x, pos, state_gla, cache_k, cache_v, w_in_a, w_gate_up_a, b_gate_a, g_norm_a, w_o_a,
              w_kv, w_q_b, lam_b, g_norm_b, w_o_b, w_up, w_down, ln_g, ln_b):
    gla_states = []
    k_sh = v_sh = None
    for layer in range(DEPTH):
        if layer < N_A_LAYERS:
            i = layer
            q, k, v, log_a, r = gla_project(x, w_in_a[i], w_gate_up_a[i], b_gate_a[i])
            if state_gla is None:
                o, s_fin = gla_prompt(q, k, v, log_a)
            else:
                s_fin, o = gla_block(state_gla[i].astype(jnp.float32), q, k, v, log_a)
            gla_states.append(s_fin.astype(x.dtype))
            mix = gla_output(o, r, g_norm_a[i], w_o_a[i])
        else:
            j = layer - N_A_LAYERS
            lambda_init = 0.8 - 0.6 * math.exp(-0.3 * layer)
            lam = diff_lambda(lam_b[j], lambda_init)
            q = diff_query(x, w_q_b[j], pos)
            if cache_k is None:
                o = diff_attn_prompt(q, k_sh, v_sh, lam)
            else:
                o = diff_attn_sample(q, k_sh, v_sh, cache_k, cache_v, lam)
            mix = diff_output(o, g_norm_b[j], lambda_init, w_o_b[j])
        x = layer_norm(DEEPNORM_ALPHA * x + mix.astype(x.dtype), ln_g[layer, 0], ln_b[layer, 0])
        x = layer_norm(DEEPNORM_ALPHA * x + sqrelu_mlp(x, w_up[layer], w_down[layer]).astype(x.dtype),
                       ln_g[layer, 1], ln_b[layer, 1])
        if layer == N_A_LAYERS - 1:
            k_sh, v_sh = shared_kv(x, w_kv, pos)
    return x, jnp.stack(gla_states), k_sh, v_sh

def setup_inputs(seed: int = 0) -> dict:
    key = jax.random.key(seed)
    ks = jax.random.split(key, 19)

    def nrm(k, shape, scale):
        return jax.random.normal(k, shape, jnp.float32) * scale

    return {
        'x_prompt': nrm(ks[0], (BATCH, SEQ, D_MODEL), 1.0),
        'x_sample': nrm(ks[1], (DEC_BATCH, DEC_SEQ, D_MODEL), 1.0),
        'state_gla': nrm(ks[2], (N_A_LAYERS, DEC_BATCH, GLA_HEADS, GLA_DKH, GLA_DVH), 0.5),
        'cache_k': nrm(ks[3], (DEC_BATCH, PAST_LEN, DIFF_HEADS, 2, DIFF_HD), 1.0),
        'cache_v': nrm(ks[4], (DEC_BATCH, PAST_LEN, DIFF_HEADS, 2 * DIFF_HD), 1.0),
        'w_in_a': nrm(ks[5], (N_A_LAYERS, D_MODEL, A_IN), D_MODEL ** -0.5),
        'w_gate_up_a': nrm(ks[6], (N_A_LAYERS, GATE_RANK, GLA_DK), GATE_RANK ** -0.5),
        'b_gate_a': nrm(ks[7], (N_A_LAYERS, GLA_DK), 0.1),
        'g_norm_a': 1.0 + nrm(ks[8], (N_A_LAYERS, GLA_DVH), 0.01),
        'w_o_a': nrm(ks[9], (N_A_LAYERS, GLA_DV, D_MODEL), GLA_DV ** -0.5 * DEEPNORM_BETA),
        'w_kv': nrm(ks[10], (D_MODEL, DIFF_QK + DIFF_V), D_MODEL ** -0.5),
        'w_q_b': nrm(ks[11], (N_B_LAYERS, D_MODEL, DIFF_QK), D_MODEL ** -0.5),
        'lam_b': nrm(ks[12], (N_B_LAYERS, 4, DIFF_HD), 0.1),
        'g_norm_b': 1.0 + nrm(ks[13], (N_B_LAYERS, 2 * DIFF_HD), 0.01),
        'w_o_b': nrm(ks[14], (N_B_LAYERS, DIFF_V, D_MODEL), DIFF_V ** -0.5 * DEEPNORM_BETA),
        'w_up': nrm(ks[15], (DEPTH, D_MODEL, D_FF), D_MODEL ** -0.5),
        'w_down': nrm(ks[16], (DEPTH, D_FF, D_MODEL), D_FF ** -0.5 * DEEPNORM_BETA),
        'ln_g': 1.0 + nrm(ks[17], (DEPTH, 2, D_MODEL), 0.01),
        'ln_b': nrm(ks[18], (DEPTH, 2, D_MODEL), 0.01),
    }

def reference(x_prompt, x_sample, state_gla, cache_k, cache_v, w_in_a, w_gate_up_a, b_gate_a, g_norm_a,
              w_o_a, w_kv, w_q_b, lam_b, g_norm_b, w_o_b, w_up, w_down, ln_g, ln_b):
    pos_prompt = jnp.arange(x_prompt.shape[1])
    pos_sample = cache_k.shape[1] + jnp.arange(x_sample.shape[1])
    y_prompt, gla_prompt_state, k_prompt, v_prompt = run_trunk(
        x_prompt, pos_prompt, None, None, None, w_in_a, w_gate_up_a, b_gate_a, g_norm_a, w_o_a,
        w_kv, w_q_b, lam_b, g_norm_b, w_o_b, w_up, w_down, ln_g, ln_b)
    y_sample, gla_sample_state, k_sample, v_sample = run_trunk(
        x_sample, pos_sample, state_gla, cache_k, cache_v, w_in_a, w_gate_up_a, b_gate_a, g_norm_a, w_o_a,
        w_kv, w_q_b, lam_b, g_norm_b, w_o_b, w_up, w_down, ln_g, ln_b)
    return (y_prompt, y_sample, gla_prompt_state, k_prompt, v_prompt, gla_sample_state, k_sample, v_sample)


_drawn_inputs = setup_inputs


def setup_inputs(seed=0):
    import zlib

    import numpy as np

    out = dict(_drawn_inputs(seed))
    spreads = {}
    factors = {'g_norm_a': 8.0, 'g_norm_b': 64.0, 'ln_g': 2.794, 'ln_b': 4.163}
    for name, (base, spread) in spreads.items():
        noise = np.random.default_rng([zlib.crc32(name.encode()), seed]).standard_normal(out[name].shape)
        drawn = base * np.exp(spread * noise) if base else spread * noise
        out[name] = __import__('jax').numpy.asarray(drawn.astype(out[name].dtype))
    for name, factor in factors.items():
        out[name] = (out[name] * factor).astype(out[name].dtype)
    return out
```

```python
from contextlib import ExitStack

import numpy as np
import concourse.bass as bass
from concourse import mybir

F32 = mybir.dt.float32
F32R = mybir.dt.float32r
ALU = mybir.AluOpType
ACT = mybir.ActivationFunctionType
AX = mybir.AxisListType

P = 128
D = 1024
KT = D // P
TILES = 9
PT = TILES - 1
TOK = TILES * P
GROUP = 3
NG = TILES // GROUP
GW = GROUP * P
H_A, DK, DV = 4, 128, 256
CH = 64
H_B, HD, VD = 8, 64, 128
STREAMS, SEQ_S = 8, 16
PAST = 512
FF = 4 * D
FC = 512
NFC = FF // FC
ROT = HD // 4 // 2
ALPHA = float(4 ** 0.25)
LAMBDA_INIT = 0.8 - 0.6 * float(np.exp(-0.3))
EPS = 1e-5
PASSES = ((0, 0), (0, 1), (1, 0))
NEG = -1.0e30

C_ID = 0
C_MP = C_ID + P
C_MS = C_MP + P
C_SEL = C_MS + P
C_ROW = C_SEL + 64
C_COS = C_ROW + STREAMS
C_SIN = C_COS + TILES * ROT
C_ONE = C_SIN + TILES * ROT
C_NH = C_ONE + CH
C_SG = C_NH + 10
C_END = C_SG + 2


def constants():
    c = np.zeros((P, C_END), np.float32)
    r = np.arange(P)
    c[:, C_ID:C_ID + P] = np.eye(P)
    j, i = r[:, None], r[None, :]
    c[:, C_MP:C_MP + P] = (j // CH == i // CH) & (j <= i)
    c[:, C_MS:C_MS + P] = (j // SEQ_S == i // SEQ_S) & (j <= i)
    c[:, C_SEL:C_SEL + 64] = (r[:, None] // 32 == np.arange(64)[None, :] // 16) & (
        r[:, None] % 16 == np.arange(64)[None, :] % 16)
    c[:, C_ROW:C_ROW + STREAMS] = r[:, None] // SEQ_S == np.arange(STREAMS)[None, :]
    inv = 1.0 / (500000.0 ** (np.arange(0, 2 * ROT, 2, dtype=np.float32) / (2 * ROT)))
    for t in range(TILES):
        pos = (t * P + r) if t < PT else PAST + r % SEQ_S
        ang = pos.astype(np.float32)[:, None] * inv.astype(np.float32)[None, :]
        c[:, C_COS + t * ROT:C_COS + (t + 1) * ROT] = np.cos(ang)
        c[:, C_SIN + t * ROT:C_SIN + (t + 1) * ROT] = np.sin(ang)
    c[:, C_ONE:C_ONE + CH] = 1.0
    c[:, C_NH:C_NH + 8] = -0.5
    c[:, C_NH + 8:C_NH + 10] = -1.0
    c[:, C_SG] = (r // 16 % 2 == 0)
    c[:, C_SG + 1] = (r // 16 % 2 == 1)
    m = np.zeros((1, 2 * P), np.float32)
    m[0, :CH] = 1.0
    m[0, P + CH:] = NEG
    return c, m


def encoder_step(nc, x_prompt, x_sample, state_gla, cache_k, cache_v, w_in, w_gate, b_gate, g_norm_a,
                 w_o_a, w_kv, w_q, lam, g_norm_b, w_o_b, w_up, w_down, ln_g, ln_b, consts, maskrow,
                 y_prompt, y_sample, gla_prompt, k_prompt, v_prompt, gla_sample, k_sample, v_sample):
    ctx = ExitStack()

    base = 16512

    def at(name, offset, shape, dt=F32):
        return nc.alloc_sbuf_tensor_at(name, shape, dt, offset=offset)

    O_W = base
    O_RAW = O_W + 4 * 2 * 1024 * 4
    O_XT = O_RAW + 4 * 1024 * 4
    O_Q = O_XT + 2 * KT * TOK * 4
    O_V = O_Q + TILES * D * 4
    O_TMP = O_V + TILES * D * 4
    O_C = O_TMP + 11264
    wsplit = at("wsplit", O_W, [P, 4, 2, 1024], F32R)
    raw = at("raw", O_RAW, [P, 4, 1024])
    XTR = [at(f"xt{i}", O_XT, [P, 2, KT, TOK], F32R) for i in range(5)]
    cst = at("cst", O_C, [P, C_END])
    mrow = at("mrow", O_C + 2720, [1, 2 * P])
    stats = at("stats", O_C + 2720 + 1024, [P, 192])
    xin = at("xin", O_V, [P, TILES, D])
    X = at("x_res", O_Q, [P, TILES, D])
    qkT = at("qkT", O_Q, [P, 2, H_A, TOK])
    vO = at("vO", O_V, [P, TILES, D])
    glT = [vO[0:16, 2 * GROUP + g, 512:512 + GW] for g in range(NG)]
    hT = at("hT", O_V, [P, 2, 4, TOK], F32R)
    gm = at("gm", O_TMP, [P, GW])
    gna = at("gna", O_TMP + 1536, [P, GW])
    gb = at("gb", O_TMP + 2 * 1536, [P, GW])
    geb = at("geb", O_TMP + 3 * 1536, [P, GW])
    genb = at("genb", O_TMP + 4 * 1536, [P, GW])
    wglr = at("wglr", O_TMP + 5 * 1536, [P, KT, 16])
    wgls = at("wgls", O_TMP + 5 * 1536 + 512, [P, 2, KT, 16], F32R)
    wgu = at("wgu", O_TMP + 5 * 1536, [16, H_A * DK])
    sie = at("sie", O_TMP, [P, 2, 512])
    sio = at("sio", O_TMP + 4096, [P, 2, 512])
    rin = at("rin", O_TMP, [P, 2, D])
    lng = at("lng", O_TMP, [P, 2, D])
    hsq = at("hsq", O_TMP + 8192, [P, 2, GW])
    gna_g = at("gna_g", O_TMP + 10240, [P, DV])
    kvs = at("kvs", O_V, [P, 6, 512])
    rtmp = at("rtmp", O_V + 12288, [P, 2, 4, 8, ROT])
    kqd = at("kqd", O_XT, [P, 2, 4, 2, 2, HD])
    vin = at("vin", O_XT + 8192, [P, PT, P])
    KD = at("KD", O_XT + 12288, [P, 2, 2, 2, PT * P], F32R)
    QS = at("QS", O_XT + 45056, [P, 2, 2, PT * P], F32R)
    vsp = [at("vsp0", O_XT + 61440, [P, 2, PT, P], F32R), at("vsp1", O_TMP, [P, 2, PT, P], F32R)]
    PR = at("PR", O_V, [P, 2, 2, PT * P])
    AT = at("AT", O_V + 16384, [P, 2, 2, PT, P], F32R)
    osb = at("osb", O_V + 32768, [P, 2, P])
    osq = at("osq", O_V + 33792, [P, P])
    oraw = at("oraw", O_V + 34304, [P, 2, P])
    gnb = at("gnb", O_TMP + 8192, [P, VD])
    lamt = at("lamt", O_TMP + 8704, [P, 4, HD])
    lamp = at("lamp", O_TMP + 9728, [P, 2, HD])
    Kc = at("Kc", O_XT, [P, 2, 4, D])
    Vc = at("Vc", O_XT + 32768, [P, 2, 4, D])
    vS = at("vS", O_XT + 65536, [P, D])
    KTn = at("KTn", O_XT + 69632, [P, H_B, P])
    Qbd = at("Qbd", O_V, [P, 2, H_B, P])
    KTb = at("KTb", O_V + 8192, [P, 2, 4, 512])
    kqS = at("kqS", O_V + 8192, [P, 2, D])
    PS = at("PS", O_V + 24576, [P, 2, 640])
    ATs = at("ATs", O_V + 29696, [P, 2, 5, 64])
    oTs = at("oTs", O_V + 32256, [P, H_B, P])
    QTs = at("QTs", O_TMP, [P, H_B, P])
    oS = at("oS", O_TMP + 4096, [P, D])
    CM = at("CM", O_TMP + 9216, [P, 2, 64])
    sqS = at("sqS", O_TMP + 9728, [P, P])
    oin = at("oin", O_V, [P, PT, D])
    nlam = stats[:, 176:177]
    sgl = stats[:, 177:178]
    lam2 = stats[:, 178:180]
    mx = stats[:, 0:4].rearrange("p (a b) -> p a b", a=2)
    nmx = stats[:, 4:8].rearrange("p (a b) -> p a b", a=2)
    ls = stats[:, 8:16].rearrange("p (a b) -> p a b", a=4)
    rl = stats[:, 16:24].rearrange("p (a b) -> p a b", a=4)
    gf = stats[:, 24:28]
    oss = stats[:, 28:32]
    rq = stats[:, 32:36]
    oms = stats[:, 36:40]
    ors = stats[:, 40:44]
    of = stats[:, 44:48]
    ssS = stats[:, 48:56]
    msS = stats[:, 56:64]
    rsS = stats[:, 64:72]
    coef = stats[:, 72:74]
    bg = stats[:, 0:4]
    nbg = stats[:, 4:8]
    elast = stats[:, 8:8 + H_A * 24].rearrange("p (h c) -> p h c", h=H_A)
    ss = stats[:, 104:112].rearrange("p (a b) -> p a b", a=4)
    ms = stats[:, 112:120].rearrange("p (a b) -> p a b", a=4)
    rs4 = stats[:, 120:128].rearrange("p (a b) -> p a b", a=4)
    bst = stats[:, 128:164].rearrange("p (t s) -> p t s", t=3)
    mv = stats[:, 164:170].rearrange("p (t s) -> p t s", t=3)
    rstd = stats[:, 170:173]
    nmr = stats[:, 173:176]
    ktT = at("ktT", O_XT, [P, 2, P])
    kts = at("kts", O_XT + 1024, [P, 2, P])
    attm = at("attm", O_XT + 2048, [P, 2, P])
    S = at("S", O_XT + 3072, [P, 2, H_A, DV])
    sq = at("sq", O_XT + 3072 + 8192, [P, 2, DV])
    ktS = at("ktS", O_XT + 13312, [P, H_A, P])
    attS = at("attS", O_XT + 15360, [P, H_A, P])
    oT = at("oT", O_XT + 17408, [P, 8, P])
    ktb = at("ktb", O_XT + 21504, [P, STREAMS, H_A * P])
    Ss = at("Ss", O_XT + 37888, [P, STREAMS, H_A, DV])

    ident = cst[:, C_ID:C_ID + P]
    neg1 = cst[:, C_NH + 8:C_NH + 10]

    gate_scr = nc.dram_tensor("gate_scr", (TILES, P, D), F32, kind="Internal").ap()
    q_scr = nc.dram_tensor("q_scr", (TILES, P, D), F32, kind="Internal").ap()
    o_scr = nc.dram_tensor("o_scr", (PT, P, D), F32, kind="Internal").ap()
    kv_dst = [[k_prompt[0].rearrange("(t p) h c d -> t p (h c d)", p=P)[t] for t in range(PT)]
              + [k_sample.rearrange("b s h c d -> (b s) (h c d)")],
              [v_prompt[0].rearrange("(t p) h v -> t p (h v)", p=P)[t] for t in range(PT)]
              + [v_sample.rearrange("b s h v -> (b s) (h v)")],
              [q_scr[t] for t in range(TILES)]]
    y_dst = [y_prompt[0, t * P:(t + 1) * P, :] for t in range(PT)] + [y_sample.rearrange("b s d -> (b s) d")]
    x_scr = [x_prompt[0, t * P:(t + 1) * P, :] for t in range(PT)] + [
        x_sample.rearrange("b s d -> (b s) d")]

    ps = ctx.enter_context(nc.psum_tensor("ps", [P, 8, 512], F32))

    def sem(name):
        return ctx.enter_context(nc.semaphore(name))

    c_in = sem("c_in")
    bg_in = sem("bg_in")
    mr_in = sem("mr_in")
    wgu_in = sem("wgu_in")
    x_in = [sem(f"x_in{t}") for t in range(TILES)]
    raw_in = [sem(f"raw_in{s}") for s in range(4)]
    hi_done = sem("hi_done")
    lo_done = sem("lo_done")
    w_used = sem("w_used")
    t_full = sem("t_full")
    t_hi = sem("t_hi")
    t_free = sem("t_free")
    g_full = sem("g_full")
    g_free = sem("g_free")
    gl_raw = sem("gl_raw")
    gl_hi = sem("gl_hi")
    gl_lo = sem("gl_lo")
    m_done = sem("m_done")
    lg_done = sem("lg_done")
    b_done = sem("b_done")
    eb_done = sem("eb_done")
    qk_done = sem("qk_done")
    la_done = sem("la_done")
    e_read = sem("e_read")
    re_done = sem("re_done")
    rr_done = sem("rr_done")
    ro_done = sem("ro_done")
    r_out = [sem("r_out0"), sem("r_out1")]
    r_back = [sem("r_back0"), sem("r_back1")]
    kt_pre = sem("kt_pre")
    pe_kt = sem("pe_kt")
    pe_at = sem("pe_at")
    kt_tok = sem("kt_tok")
    pe_kv = sem("pe_kv")
    at_m = sem("at_m")
    s_upd = sem("s_upd")
    pe_i0 = sem("pe_i0")
    pe_o = sem("pe_o")
    o_sq = sem("o_sq")
    o_ms = sem("o_ms")
    o_rs = sem("o_rs")
    o_evac = sem("o_evac")
    ss_in = sem("ss_in")
    ktS_done = sem("ktS_done")
    peS_kt = sem("peS_kt")
    ktb_done = sem("ktb_done")
    peS_at = sem("peS_at")
    attS_done = sem("attS_done")
    peS_oT = sem("peS_oT")
    oT_done = sem("oT_done")
    peS_kv = sem("peS_kv")
    Ss_done = sem("Ss_done")
    st_out = sem("st_out")
    gated = sem("gated")
    gna_in = sem("gna_in")
    sts = sem("sts")
    y_out = sem("y_out")
    x_res_in = sem("x_res_in")
    lng_in = sem("lng_in")
    ln_var = sem("ln_var")
    ln_rstd = sem("ln_rstd")
    ln_nmr = sem("ln_nmr")
    ln_norm = sem("ln_norm")
    ln_gain = sem("ln_gain")
    ln_done = sem("ln_done")
    ln_st = sem("ln_st")
    up_r = sem("up_r")
    up_h = sem("up_h")
    up_sq = sem("up_sq")
    rope = sem("rope")
    kv_done = sem("kv_done")
    h_in0 = sem("h_in0")
    h_in1 = sem("h_in1")
    h_v = sem("h_v")
    p_full = sem("p_full")
    p_hi = sem("p_hi")
    p_free = sem("p_free")
    v_hi = sem("v_hi")
    v_lo = sem("v_lo")
    s_full = sem("s_full")
    mx_done = sem("mx_done")
    nmx_done = sem("nmx_done")
    ex_done = sem("ex_done")
    g_done = sem("g_done")
    cb_done = sem("cb_done")
    a_full = sem("a_full")
    a_hi = sem("a_hi")
    a_free = sem("a_free")
    o_full = sem("o_full")
    osq_done = sem("osq_done")
    f_done = sem("f_done")
    ob_done = sem("ob_done")
    lam_in = sem("lam_in")
    lam_p = sem("lam_p")
    lam_e = sem("lam_e")
    nl_done = sem("nl_done")
    gnb_in = sem("gnb_in")
    o_out0 = sem("o_out0")
    o_out1 = sem("o_out1")
    S_in = sem("S_in")
    S_tr = sem("S_tr")
    S_cp = sem("S_cp")
    S_qb = sem("S_qb")
    S_z = sem("S_z")
    kc_in0 = sem("kc_in0")
    kc_in1 = sem("kc_in1")
    k_tr = sem("k_tr")
    k_ev0 = sem("k_ev0")
    k_ev1 = sem("k_ev1")
    s2_full = sem("s2_full")
    s2_mx = sem("s2_mx")
    s2_ex = sem("s2_ex")
    s2_l = sem("s2_l")
    s2_co = sem("s2_co")
    s2_cm = sem("s2_cm")
    s2_at = sem("s2_at")
    s2_atc = sem("s2_atc")
    s2_pv = sem("s2_pv")
    s2_ot = sem("s2_ot")
    s2_fin = sem("s2_fin")
    s2_finsq = sem("s2_finsq")
    s2_fms = sem("s2_fms")
    s2_frs = sem("s2_frs")
    s2_fo = sem("s2_fo")
    ps_z = sem("ps_z")
    o_back = sem("o_back")
    att_done = sem("att_done")
    att_small = sem("att_small")
    o_free = sem("o_free")
    up_done = sem("up_done")
    chain_v = sem("chain_v")
    kv_out = [sem(f"kv_out{i}") for i in range(6)]
    h_kq = [h_in0, h_in1]
    o_out = [o_out0, o_out1]
    kc_in = [kc_in0, kc_in1]

    TU_X0 = 0
    TU_GL = TU_X0 + 2 * TILES
    TU_Q = TU_GL + NG
    TU_LOG = TU_Q + 8 * NG
    TU_O1 = TU_LOG + H_A * NG
    TU_L = [0] * 3
    TU_L[0] = TU_O1 + 2 * TILES
    TU_UP = [0, 0]
    TU_UP[0] = TU_L[0] + 2 * TILES
    TU_L[1] = TU_UP[0] + NFC * 4 * NG
    TU_O2 = TU_L[1] + 2 * TILES
    TU_L[2] = TU_O2 + 2 * TILES
    TU_UP[1] = TU_L[2] + 2 * TILES
    GU_V = 0
    GU_R = GU_V + 2 * TILES
    GU_O = GU_R + 2 * TILES
    GU_MLP = [GU_O + 2 * TILES, 0]
    GU_KVQ = GU_MLP[0] + NFC * 2 * TILES
    GU_O2 = GU_KVQ + 6 * TILES
    GU_MLP[1] = GU_O2 + 2 * TILES
    G_QK, G_V, G_R, G_O = 0, 8, 16, 24
    G_MLP = [32, 0]
    G_KVQ = G_MLP[0] + 8 * NFC
    G_O2 = G_KVQ + 24
    G_MLP[1] = G_O2 + 8
    G_TOTAL = G_MLP[1] + 8 * NFC

    def a_banks(s):
        return (s % PT + 4) // 4

    a_count = [0]
    for step in range(H_B * PT):
        a_count.append(a_count[-1] + a_banks(step))

    def after_norm(lay):
        seq = [("tr", t, half) for t in range(GROUP) for half in range(2)]
        seq += [("up", 0, 0), ("up", 1, 0)]
        seq += [("tr", t, half) for t in range(GROUP, 2 * GROUP) for half in range(2)]
        seq += [("up", 0, 1), ("up", 1, 1)]
        seq += [("tr", t, half) for t in range(2 * GROUP, TILES) for half in range(2)]
        seq += [("up", 0, 2), ("up", 1, 2)] + [("up", m, n) for m in (2, 3) for n in range(NG)]
        return [(TU_L[2 * lay] + i, *e) for i, e in enumerate(seq)]
    LOG_AT = {2 * i: (i // NG, i % NG) for i in range(H_A * NG)}

    block = ctx.enter_context(nc.Block())

    @block.sync
    def _(sp):
        def load(g, src, n):
            if g >= 4:
                sp.wait_ge(lo_done, g - 3)
            sp.dma_start(raw[:, g % 4, :].rearrange("p (k n) -> p k n", n=n),
                         src.rearrange("(k p) n -> p k n", p=P)).then_inc(raw_in[g % 4], 16)

        def load_p(g, w, u):
            for j in range(4):
                load(g + j, w[j * 256:(j + 1) * 256, u * 512:(u + 1) * 512], 512)

        for t in range(3):
            sp.dma_start(xin[:, t, :], x_scr[t]).then_inc(x_in[t], 16)
            if t == 0:
                sp.dma_start(cst[:], consts).then_inc(c_in, 16)
        for m in range(4):
            load(m, w_in[0, :, m * P:(m + 1) * P], P)
            if m < 3:
                for t in (3 + 2 * m, 4 + 2 * m):
                    sp.dma_start(xin[:, t, :], x_scr[t]).then_inc(x_in[t], 16)
        sp.dma_start(wglr[:], w_in[0, :, 3072:3088].rearrange("(k p) n -> p k n", p=P)).then_inc(gl_raw, 16)
        sp.dma_start(bg, b_gate).then_inc(bg_in, 16)
        sp.dma_start(gna_g[:], g_norm_a[0:1, :].broadcast_to([P, DV])).then_inc(gna_in, 16)
        sp.dma_start(mrow[:], maskrow).then_inc(mr_in, 16)
        for m in range(4, 8):
            load(m, w_in[0, :, m * P:(m + 1) * P], P)
        sp.wait_ge(t_free, TU_Q)
        sp.dma_start(wgu[:], w_gate[0]).then_inc(wgu_in, 16)
        for u in range(2):
            load_p(G_V + 4 * u, w_in[0, :, 1024:2048], u)
        n = 0
        for u in range(2):
            load_p(G_R + 4 * u, w_in[0, :, 2048:3072], u)
        for u in range(2):
            if u == 1:
                load_p(G_O, w_o_a[0], 0)
            for t in range(TILES):
                sp.wait_ge(ro_done, n + 1)
                sp.dma_start(gate_scr[t, :, u * 512:(u + 1) * 512], sio[:, n % 2, :]).then_inc(r_out[n % 2], 16)
                n += 1
        sp.wait_ge(w_used, G_O)
        for b in range(STREAMS):
            sp.dma_start(Ss[:, b], state_gla[0, b].rearrange("h k v -> k h v")).then_inc(ss_in, 16)
        sp.wait_ge(s_upd, 2 * PT * H_A)
        sp.dma_start(gla_prompt[0, 0].rearrange("h k v -> k h v"), S[:, 0]).then_inc(st_out, 16)
        for b in range(STREAMS):
            sp.wait_ge(Ss_done, 2 * (b + 1))
            sp.dma_start(gla_sample[0, b].rearrange("h k v -> k h v"), Ss[:, b]).then_inc(st_out, 16)
        for n2 in range(2):
            sp.wait_ge(r_out[n2], 16 * TILES)
        for t in range(TILES):
            if t >= 2:
                sp.wait_ge(gated, t - 1)
            else:
                sp.wait_ge(ro_done, 2 * TILES)
            sp.dma_start(rin[:, t % 2, :], gate_scr[t]).then_inc(r_back[t % 2], 16)
        sp.wait_ge(st_out, 16 * (1 + STREAMS))
        sp.wait_ge(g_free, GU_O)
        def norm_params(n):
            if n:
                sp.wait_ge(ln_done, TILES * n)
            for i, w in enumerate((ln_g, ln_b)):
                sp.dma_start(lng[:, i, :], w[n // 2, n % 2:n % 2 + 1, :].broadcast_to([P, D])).then_inc(lng_in, 16)

        def mlp_loads(lay, c):
            g = G_MLP[lay] + 8 * c
            col = w_up[lay, :, bass.ds(c * FC, FC)] if not isinstance(c, int) else w_up[lay, :, c * FC:(c + 1) * FC]
            row = w_down[lay, bass.ds(c * FC, FC), :] if not isinstance(c, int) else w_down[lay, c * FC:(c + 1) * FC, :]
            for m in range(4):
                load_at(g + m, m, col[:, m * P:(m + 1) * P], P)
            for q in range(4):
                nh, kp = q // 2, q % 2
                load_at(g + 4 + q, q, row[kp * 256:(kp + 1) * 256, nh * 512:(nh + 1) * 512], 512)

        def load_at(g, slot, src, n):
            sp.wait_ge(lo_done, g - 3)
            sp.dma_start(raw[:, slot, :].rearrange("p (k n) -> p k n", n=n),
                         src.rearrange("(k p) n -> p k n", p=P)).then_inc(raw_in[slot], 16)

        sp.wait_ge(Ss_done, 2 * STREAMS)
        for t in range(TILES):
            sp.dma_start(X[:, t, :], x_scr[t]).then_inc(x_res_in, 16)
        sp.wait_ge(gated, TILES)
        norm_params(0)
        load_p(G_O + 4, w_o_a[0], 1)
        mlp_loads(0, 0)
        norm_params(1)
        for c in range(1, NFC):
            mlp_loads(0, c)
        n = 0
        for u in range(6):
            w, col = (w_kv, u * 512) if u < 4 else (w_q[0], (u - 4) * 512)
            load_p(G_KVQ + 4 * u, w[:, col:col + 512], 0)
            if u:
                for t in range(TILES):
                    sp.wait_ge(kv_done, n + 1)
                    sp.dma_start(kv_dst[(u - 1) // 2][t][:, (u - 1) % 2 * 512:(u - 1) % 2 * 512 + 512],
                                 kvs[:, n % 6, :]).then_inc(kv_out[n % 6], 16)
                    n += 1
        for t in range(TILES):
            sp.wait_ge(kv_done, n + 1)
            sp.dma_start(kv_dst[2][t][:, 512:1024], kvs[:, n % 6, :]).then_inc(kv_out[n % 6], 16)
            n += 1
        load_p(G_O2, w_o_b[0], 0)
        sp.dma_start(lamt[:], lam[0:1].broadcast_to([P, 4, HD])).then_inc(lam_in, 16)
        sp.dma_start(gnb[:], g_norm_b[0:1, :].broadcast_to([P, VD])).then_inc(gnb_in, 16)
        for i in range(6):
            sp.wait_ge(kv_out[i], 16 * TILES)

        def pair_in(i):
            h, mat, part = i // 4, i % 4 // 2, i % 2
            src = k_prompt[0].rearrange("(t p) h c d -> p t h c d", p=P)[:, :, h] if mat == 0 else \
                q_scr[0:PT].rearrange("t p (h c d) -> p t h c d", h=H_B, c=2)[:, :, h]
            if i >= 2:
                sp.wait_ge(p_full, 2 * i - 2)
            for dup in range(2):
                for t in range(4):
                    sp.dma_start(kqd[:, i % 2, t, :, dup, :], src[:, 4 * part + t]).then_inc(h_kq[i % 2], 16)

        def values_in(h):
            if h:
                sp.wait_ge(v_lo, h)
            sp.dma_start(vin[:], v_prompt[0].rearrange("(t p) h v -> p t h v", p=P)[:, :, h]).then_inc(h_v, 16)

        def out_o(s):
            sp.wait_ge(ob_done, s + 1)
            h, i = s // PT, s % PT
            sp.dma_start(o_scr[i, :, h * P:(h + 1) * P], osb[:, s % 2, :]).then_inc(o_out[s % 2], 16)

        for i in range(2):
            pair_in(i)
        values_in(0)
        for i in range(2, 6):
            pair_in(i)
        values_in(1)
        for h in range(H_B):
            for i in range(PT):
                if i in (0, 2) and h + 1 < H_B:
                    pair_in(4 * (h + 1) + i // 2 + 2)
                if i in (4, 6) and h + 2 < H_B:
                    pair_in(4 * (h + 2) + i // 2 - 2)
                if i == 3 and h + 2 < H_B:
                    values_in(h + 2)
                out_o(h * PT + i)

        sp.wait_ge(att_done, 1)
        for i, src in enumerate((kv_dst[0][PT], q_scr[PT])):
            sp.dma_start(kqS[:, i, :], src).then_inc(S_in, 16)
        sp.dma_start(vS[:], kv_dst[1][PT]).then_inc(S_in, 16)

        def cache_in(b):
            if b >= 2:
                sp.wait_ge(s2_pv, 2 * (b - 1))
            sp.dma_start(Kc[:, b % 2], cache_k[b].rearrange("(t p) h c d -> p t (h c d)", p=P)).then_inc(kc_in[b % 2], 16)
            sp.dma_start(Vc[:, b % 2], cache_v[b].rearrange("(t p) h v -> p t (h v)", p=P)).then_inc(kc_in[b % 2], 16)
        for b in range(STREAMS):
            cache_in(b)
        for i in range(2):
            sp.wait_ge(o_out[i], 16 * H_B * PT // 2)
        sp.wait_ge(s2_fin, 1)
        for t in range(PT):
            sp.dma_start(oin[:, t, :], o_scr[t]).then_inc(o_back, 16)
        load_p(G_O2 + 4, w_o_b[0], 1)
        sp.wait_ge(t_free, TU_O2 + 2 * TILES)
        norm_params(2)
        mlp_loads(1, 0)
        norm_params(3)
        for c in range(1, NFC):
            mlp_loads(1, c)
        for t in range(TILES):
            sp.wait_ge(ln_done, 3 * TILES + t + 1)
            sp.dma_start(y_dst[t], X[:, t, :]).then_inc(y_out, 16)
        sp.wait_ge(y_out, 16 * TILES)

    @block.gpsimd
    def _(pool):
        def split_lo(g):
            pool.wait_ge(hi_done, g + 1)
            nc.gpsimd.tensor_tensor(wsplit[:, g % 4, 1, :], raw[:, g % 4, :],
                                    wsplit[:, g % 4, 0, :].bitcast(F32), ALU.subtract).then_inc(lo_done, 1)

        def power(p):
            pool.wait_ge(o_ms, p + 1)
            nc.gpsimd.tensor_tensor(rs4[:, p % 4, :], ms[:, p % 4, :], cst[:, C_NH:C_NH + 2],
                                    ALU.pow).then_inc(o_rs, 1)

        pool.wait_ge(c_in, 16)
        for g in range(4):
            split_lo(g)
        pool.wait_ge(gl_hi, 1)
        nc.gpsimd.tensor_tensor(wgls[:, 1], wglr[:], wgls[:, 0].bitcast(F32), ALU.subtract).then_inc(gl_lo, 1)
        for g in range(4, G_O + 4):
            split_lo(g)
        for p in range(2 * PT + 2):
            power(p)

        def norm(n, grp):
            for t in range(grp * GROUP, (grp + 1) * GROUP):
                i = n * TILES + t
                pool.wait_ge(ln_var, i + 1)
                nc.gpsimd.tensor_tensor(rstd[:, i % 3:i % 3 + 1], mv[:, i % 3, 1:2], cst[:, C_NH:C_NH + 1],
                                        ALU.pow).then_inc(ln_rstd, 1)
            for t in range(grp * GROUP, (grp + 1) * GROUP):
                i = n * TILES + t
                pool.wait_ge(ln_norm, i + 1)
                if t == 0:
                    pool.wait_ge(lng_in, 32 * (n + 1))
                nc.gpsimd.tensor_tensor(X[:, t, :], X[:, t, :], lng[:, 0, :], ALU.mult).then_inc(ln_gain, 1)

        def product_norm(n, g):
            norm(n, 0)
            norm(n, 1)
            for j in range(4):
                split_lo(g + 4 + j)
            norm(n, 2)

        def mlp(lay):
            g = G_MLP[lay]
            for j in range(8 * NFC - 4):
                split_lo(g + 4 + j)
            norm(2 * lay + 1, 0)
            for j in range(4):
                if g + 8 * NFC + j < G_TOTAL:
                    split_lo(g + 8 * NFC + j)
            norm(2 * lay + 1, 1)
            norm(2 * lay + 1, 2)

        for j in range(4):
            split_lo(G_O + 4 + j)
        product_norm(0, G_O + 4)
        mlp(0)
        for g in range(G_KVQ + 4, G_O2 + 4):
            split_lo(g)

        def v_low(h):
            pool.wait_ge(v_hi, h + 1)
            nc.gpsimd.tensor_tensor(vsp[h % 2][:, 1], vin[:], vsp[h % 2][:, 0].bitcast(F32),
                                    ALU.subtract).then_inc(v_lo, 1)

        pp = [0]

        def small(fn, *a, done=None):
            ins = fn(*a)
            if done is None:
                pp[0] += 1
                ins.then_inc(att_small, 1)
                pool.wait_ge(att_small, pp[0])
            else:
                ins.then_inc(done, 1)
        tt, ts = nc.gpsimd.tensor_tensor, nc.gpsimd.tensor_scalar

        def balance(s):
            r = s % 4
            pool.wait_ge(ex_done, 2 * s + 2)
            small(tt, rl[:, r, :], ls[:, r, :], neg1, ALU.pow)
            small(tt, gf[:, r:r + 1], ls[:, r, 0:1], rl[:, r, 1:2], ALU.mult)
            small(tt, gf[:, r:r + 1], gf[:, r:r + 1], nlam, ALU.mult, done=g_done)

        def factor(s):
            r = s % 4
            pool.wait_ge(osq_done, s + 1)
            small(tt, rq[:, r:r + 1], rl[:, r, 0:1], rl[:, r, 0:1], ALU.mult)
            small(tt, oms[:, r:r + 1], oss[:, r:r + 1], rq[:, r:r + 1], ALU.mult)
            small(ts, oms[:, r:r + 1], oms[:, r:r + 1], 1.0 / VD, EPS, ALU.mult, ALU.add)
            small(tt, ors[:, r:r + 1], oms[:, r:r + 1], cst[:, C_NH:C_NH + 1], ALU.pow)
            small(tt, of[:, r:r + 1], ors[:, r:r + 1], rl[:, r, 0:1], ALU.mult, done=f_done)

        pool.wait_ge(nl_done, 1)
        v_low(0)
        balance(0)
        for s in range(H_B * PT):
            if s % PT == 2 and s // PT + 1 < H_B:
                v_low(s // PT + 1)
            if s + 1 < H_B * PT:
                balance(s + 1)
            if s:
                factor(s - 1)
        factor(H_B * PT - 1)

        pool.wait_ge(att_done, 1)
        nc.gpsimd.memset(Qbd[:], 0.0).then_inc(S_z, 1)
        nc.gpsimd.memset(PS[:, :, 512:640], 0.0).then_inc(ps_z, 1)
        pool.wait_ge(S_z, 1)
        pool.wait_ge(ps_z, 1)
        pool.wait_ge(S_cp, 4)

        def queries(b):
            if b >= 2:
                pool.wait_ge(s2_full, 2 * (b - 1))
            for c in range(2):
                for hh in range(4):
                    col = 32 * hh + 16 * c
                    nc.gpsimd.tensor_copy(Qbd[c * HD:(c + 1) * HD, b % 2, hh::4, col:col + 16],
                                          QTs[c * HD:(c + 1) * HD, hh::4, b * 16:b * 16 + 16]).then_inc(S_qb, 1)
                pool.wait_ge(S_qb, 8 * b + 4 * (c + 1))

        def coefficient(w):
            pool.wait_ge(s2_ex, 2 * w + 2)
            r = w % 2
            small(tt, ls[:, r, 0:1], ls[:, r, 0:1], ls[:, r, 1:2], ALU.add)
            small(tt, coef[:, r:r + 1], ls[:, r, 0:1], neg1[:, 0:1], ALU.pow)
            small(tt, coef[:, r:r + 1], coef[:, r:r + 1], sgl, ALU.mult, done=s2_co)

        def clear_new(w):
            pool.wait_ge(s2_at, w - 1)
            nc.gpsimd.memset(PS[:, w % 2, 512:640], 0.0).then_inc(ps_z, 1)
            pool.wait_ge(ps_z, w)

        queries(0)
        queries(1)
        for w in range(2 * STREAMS):
            if w >= 2:
                clear_new(w)
            coefficient(w)
            if w % 2 and w // 2 + 2 < STREAMS:
                queries(w // 2 + 2)
        pool.wait_ge(s2_fms, 1)
        nc.gpsimd.tensor_tensor(rsS, msS, cst[:, C_NH:C_NH + 8], ALU.pow).then_inc(s2_frs, 1)
        for j in range(4):
            split_lo(G_O2 + 4 + j)
        product_norm(2, G_O2 + 4)
        mlp(1)

    @block.scalar
    def _(act):
        def split_hi(g):
            act.wait_ge(raw_in[g % 4], 16 * (g // 4 + 1))
            if g >= 4:
                act.wait_ge(w_used, g - 3)
            nc.scalar.activation(wsplit[:, g % 4, 0, :], raw[:, g % 4, :], ACT.Copy).then_inc(hi_done, 1)

        def transposed_hi(u, xt, t, half):
            act.wait_ge(t_full, u + 1)
            nc.scalar.activation(xt[:, 0, 4 * half:4 * half + 4, t * P:(t + 1) * P],
                                 ps[:, 6 + u % 2, :].rearrange("p (k n) -> p k n", n=P),
                                 ACT.Copy).then_inc(t_hi, 1)

        n_hi = 0
        for g in range(4):
            split_hi(g)
        for t in range(TILES):
            for half in range(2):
                transposed_hi(TU_X0 + 2 * t + half, XTR[0], t, half)
                n_hi += 1
        act.wait_ge(gl_raw, 16)
        nc.scalar.activation(wgls[:, 0], wglr[:], ACT.Copy).then_inc(gl_hi, 1)
        act.wait_ge(c_in, 16)
        act.wait_ge(bg_in, 16)
        nc.scalar.mul(nbg, bg, -1.0).then_inc(la_done, 1)
        for g in range(4, 12):
            split_hi(g)
        for step in range(24):
            if step in LOG_AT:
                i = step // 2
                act.wait_ge(m_done, 2 * i + 2)
                if i == 0:
                    act.wait_ge(la_done, 1)
                h = LOG_AT[step][0]
                nc.scalar.activation(gna[:], gna[:], ACT.Exp, bias=nbg[:, h:h + 1]).then_inc(e_read, 1)
                act.wait_ge(e_read, i + 1)
                nc.scalar.activation(gna[:], gna[:], ACT.Ln, bias=1.0).then_inc(lg_done, 1)
                act.wait_ge(b_done, i + 1)
                if i:
                    act.wait_ge(qk_done, 3 * i)
                nc.scalar.activation(geb[:], gb[:], ACT.Exp, scale=1.0 / 16).then_inc(eb_done, 1)
                nc.scalar.activation(genb[:], gb[:], ACT.Exp, scale=-1.0 / 16).then_inc(eb_done, 1)
            if step % 12 >= 8:
                split_hi(12 + 4 * (step // 12) + step % 12 - 8)
        n = 0
        for u in range(2):
            for grp in range(NG):
                for t in range(GROUP):
                    use = GU_R + n
                    act.wait_ge(g_full, use + 1)
                    if n >= 2:
                        act.wait_ge(ro_done, n - 1)
                    nc.scalar.activation(sie[:, n % 2, :], ps[:, use % 6, :], ACT.Exp,
                                         scale=-1.0).then_inc(re_done, 1)
                    n += 1
            for j in range(4):
                g = 20 + 4 * u + j
                split_hi(g)

        def decayed(s):
            t, h = s // H_A, s % H_A
            if s >= 2:
                act.wait_ge(pe_kt, s - 1)
            for c in range(2):
                last = nc.scalar.mul(ktT[:, s % 2, c * CH:(c + 1) * CH],
                                     qkT[:, 1, h, t * P + c * CH:t * P + (c + 1) * CH],
                                     elast[:, h, 2 * t + c:2 * t + c + 1])
            last.then_inc(kt_pre, 1)

        def to_tokens(s):
            act.wait_ge(pe_kt, s + 1)
            if s >= 2:
                act.wait_ge(pe_kv, 2 * (s - 1))
            nc.scalar.activation(kts[:, s % 2, :], ps[:, 0, 0:P], ACT.Copy).then_inc(kt_tok, 1)

        def squares(p):
            t, hp = p // 2, p % 2
            act.wait_ge(pe_o, 4 * t + 2 * hp + 2)
            if p >= 4:
                act.wait_ge(o_ms, p - 3)
            for k in range(2):
                if p or k:
                    act.wait_ge(o_sq, 2 * p + k)
                nc.scalar.activation(sq[:, k, :], ps[:, 4 + 2 * (t % 2) + hp, k * DV:(k + 1) * DV],
                                     ACT.Square, accum_out=ss[:, p % 4, k:k + 1]).then_inc(o_sq, 1)

        act.wait_ge(qk_done, 3 * H_A * NG)
        act.wait_ge(w_used, G_O)
        steps = PT * H_A
        decayed(0)
        decayed(1)
        to_tokens(0)
        for s in range(steps):
            if s + 2 < steps:
                decayed(s + 2)
            if s + 1 < steps:
                to_tokens(s + 1)
            if s % 2 == 1:
                squares(s // 2)
        act.wait_ge(peS_kt, 4)
        for b in range(STREAMS):
            last = nc.scalar.mul(ktb[:, b, :], ps[:, 0, :], cst[:, C_ROW + b:C_ROW + b + 1])
        last.then_inc(ktb_done, 1)
        act.wait_ge(peS_oT, 1)
        for i in range(2):
            last = nc.scalar.activation(oT[:, 4 * i:4 * i + 4, :],
                                        ps[:, 4 + i, :].rearrange("p (k n) -> p k n", n=P), ACT.Copy)
        last.then_inc(oT_done, 1)
        for p in (2 * PT, 2 * PT + 1):
            act.wait_ge(pe_o, 4 * PT + 2 * (p - 2 * PT) + 2)
            act.wait_ge(o_ms, p - 3)
            for k in range(2):
                act.wait_ge(o_sq, 2 * p + k)
                nc.scalar.activation(sq[:, k, :], ps[:, 6 + p - 2 * PT, k * DV:(k + 1) * DV],
                                     ACT.Square, accum_out=ss[:, p % 4, k:k + 1]).then_inc(o_sq, 1)
        act.wait_ge(Ss_done, 2 * STREAMS)
        act.wait_ge(st_out, 16 * (1 + STREAMS))
        for t in range(TILES):
            for half in range(2):
                transposed_hi(TU_O1 + 2 * t + half, XTR[1], t, half)

        def norm(n, grp):
            for t in range(grp * GROUP, (grp + 1) * GROUP):
                i = n * TILES + t
                act.wait_ge(ln_nmr, i + 1)
                nc.scalar.activation(X[:, t, :], X[:, t, :], ACT.Identity, bias=nmr[:, i % 3:i % 3 + 1],
                                     scale=rstd[:, i % 3:i % 3 + 1]).then_inc(ln_norm, 1)

        def hidden(lay, k, m, ng):
            act.wait_ge(up_r, 96 * lay + k + 1)
            nc.scalar.activation(hsq[:, k % 2, :], hsq[:, k % 2, :], ACT.Square).then_inc(up_sq, 1)
            act.wait_ge(up_sq, 96 * lay + k + 1)
            nc.scalar.activation(hT[:, 0, m, ng * GW:(ng + 1) * GW], hsq[:, k % 2, :], ACT.Copy).then_inc(up_h, 1)

        def residual_norm(lay, g):
            n = 2 * lay
            norm(n, 0)
            k = 0
            for i, (u, kind, p, q) in enumerate(after_norm(lay)):
                if i == 2 * GROUP:
                    norm(n, 1)
                    for j in range(4):
                        split_hi(g + 4 + j)
                if kind == "tr":
                    transposed_hi(u, XTR[2 if lay == 0 else 4], p, q)
                    if (p, q) == (2 * GROUP - 1, 1):
                        norm(n, 2)
                else:
                    hidden(lay, k, p, q)
                    k += 1
                    if q == NG - 1:
                        split_hi(G_MLP[lay] + 4 + p)

        def mlp(lay):
            g = G_MLP[lay]
            for c in range(NFC):
                if c:
                    for m in range(4):
                        for ng in range(NG):
                            k = 12 * c + 3 * m + ng
                            hidden(lay, k, m, ng)
                        split_hi(g + 8 * c + 4 + m)
                if c < NFC - 1:
                    for j in range(4):
                        split_hi(g + 8 * c + 8 + j)
            for j in range(4):
                if j == 2:
                    norm(2 * lay + 1, 0)
                if g + 8 * NFC + j < G_TOTAL:
                    split_hi(g + 8 * NFC + j)

        for j in range(4):
            split_hi(G_O + 4 + j)
        residual_norm(0, G_O + 4)
        mlp(0)
        for grp in range(NG):
            if grp:
                norm(1, grp)
            for t in range(grp * GROUP, (grp + 1) * GROUP):
                for half in range(2):
                    transposed_hi(TU_L[1] + 2 * t + half, XTR[3], t, half)
        for g in range(G_KVQ + 4, G_O2 + 4):
            split_hi(g)

        act.wait_ge(lam_p, 2)
        nc.scalar.activation(lam2, lam2, ACT.Exp).then_inc(lam_e, 1)

        def prepare(h, j):
            i = 8 * h + j
            act.wait_ge(p_full, i + 1)
            c, part = j % 2, j % 4 // 2
            if j < 4:
                dst = KD[:, h % 2, 0, c, part * 512:(part + 1) * 512]
            else:
                dst = QS[:, h % 2, c, part * 512:(part + 1) * 512]
            nc.scalar.activation(dst, ps[:, 4, :], ACT.Copy).then_inc(p_hi, 1)

        def v_high(h):
            act.wait_ge(h_v, 16 * (h + 1))
            if h >= 2:
                act.wait_ge(o_full, PT * (h - 1))
            nc.scalar.activation(vsp[h % 2][:, 0], vin[:], ACT.Copy).then_inc(v_hi, 1)

        def exponentials(s):
            i = s % PT
            w = (i + 1) * P
            act.wait_ge(nmx_done, s + 1)
            if s >= 2:
                act.wait_ge(a_full, a_count[s - 1])
            if s >= 4:
                act.wait_ge(f_done, s - 3)
            for c in range(2):
                nc.scalar.activation(PR[:, s % 2, c, 0:w], ps[:, 2 * c:2 * c + 2, :].rearrange("p a n -> p (a n)")[:, 0:w],
                                     ACT.Exp, bias=nmx[:, s % 2, c:c + 1], scale=HD ** -0.5,
                                     accum_out=ls[:, s % 4, c:c + 1]).then_inc(ex_done, 1)

        def weights_hi(s):
            for b in range(a_banks(s)):
                use = a_count[s] + b
                act.wait_ge(a_full, use + 1)
                if s >= 2 and b == 0:
                    act.wait_ge(o_full, s - 1)
                n = min(4, s % PT + 1 - 4 * b)
                nc.scalar.activation(AT[:, s % 2, 0, 4 * b:4 * b + n, :],
                                     ps[:, 5 + use % 2, 0:n * P].rearrange("p (k n) -> p k n", n=P),
                                     ACT.Copy).then_inc(a_hi, 1)

        def out_square(s):
            act.wait_ge(o_full, s + 1)
            if s:
                act.wait_ge(osq_done, s)
            nc.scalar.activation(osq[:], ps[:, 7, 0:P], ACT.Square,
                                 accum_out=oss[:, s % 4:s % 4 + 1]).then_inc(osq_done, 1)
            if s >= 2:
                act.wait_ge(ob_done, s - 1)
            nc.scalar.activation(oraw[:, s % 2, :], ps[:, 7, 0:P], ACT.Copy).then_inc(o_free, 1)

        for j in range(8):
            prepare(0, j)
        v_high(0)
        exponentials(0)
        for s in range(H_B * PT):
            h = s // PT
            if h + 1 < H_B:
                prepare(h + 1, s % PT)
                if s % PT == 1:
                    v_high(h + 1)
            if s + 1 < H_B * PT:
                exponentials(s + 1)
            weights_hi(s)
            if s:
                out_square(s - 1)
        out_square(H_B * PT - 1)

        def exps2(w):
            act.wait_ge(s2_mx, w + 1)
            if w < 2:
                act.wait_ge(ps_z, 1)
            else:
                act.wait_ge(s2_at, w - 1)
                act.wait_ge(ps_z, w)
                act.wait_ge(s2_co, w - 1)
            b = w // 2
            nc.scalar.activation(PS[:, w % 2, 0:512], ps[:, 2 * (w % 2), :], ACT.Exp, bias=nmx[:, w % 2, 0:1],
                                 scale=HD ** -0.5, accum_out=ls[:, w % 2, 0:1]).then_inc(s2_ex, 1)
            nc.scalar.activation(PS[:, w % 2, 512 + 16 * b:528 + 16 * b], ps[:, 2 * (w % 2) + 1, 0:16], ACT.Exp,
                                 bias=nmx[:, w % 2, 0:1], scale=HD ** -0.5,
                                 accum_out=ls[:, w % 2, 1:2]).then_inc(s2_ex, 1)

        def weights2(w):
            act.wait_ge(s2_at, w + 1)
            if w >= 2:
                act.wait_ge(s2_pv, w - 1)
            nc.scalar.activation(ATs[:, w % 2], ps[:, 6, 0:320].rearrange("p (k n) -> p k n", k=5),
                                 ACT.Copy).then_inc(s2_atc, 1)

        def cache_keys(w):
            for hh in (0, 2):
                act.wait_ge(k_tr, 4 * w + hh + 1)
                if w >= 2:
                    act.wait_ge(s2_full, w - 1)
                nc.scalar.activation(KTb[:, w % 2, hh, :], ps[:, 4, :], ACT.Copy).then_inc(k_ev0, 1)

        act.wait_ge(S_cp, 4)
        cache_keys(0)
        for w in range(2 * STREAMS):
            if w + 1 < 2 * STREAMS:
                cache_keys(w + 1)
            exps2(w)
            weights2(w)
        for h in range(H_B):
            act.wait_ge(s2_fin, 1)
            if h:
                act.wait_ge(s2_finsq, h)
            nc.scalar.activation(sqS[:], ps[:, h // 4, (h % 4) * P:(h % 4 + 1) * P], ACT.Square,
                                 accum_out=ssS[:, h:h + 1]).then_inc(s2_finsq, 1)
        for t in range(TILES):
            for half in range(2):
                transposed_hi(TU_O2 + 2 * t + half, XTR[0], t, half)
        for j in range(4):
            split_hi(G_O2 + 4 + j)
        residual_norm(1, G_O2 + 4)
        mlp(1)
        for grp in (1, 2):
            norm(3, grp)

    @block.tensor
    def _(pe):
        tf = [0]

        def t_bank(u):
            if u >= 2:
                pe.wait_ge(t_free, u - 1)
            return 6 + u % 2

        def transposes(u, src, t, half):
            b = t_bank(u)
            for k in range(4):
                last = nc.tensor.transpose(ps[:, b, k * P:(k + 1) * P],
                                           src[:, t, (4 * half + k) * P:(4 * half + k + 1) * P], ident)
            last.then_inc(t_full, 1)

        def quarter_cols(g, u, xt, ng, M=P, w=None):
            b = t_bank(u)
            for k in range(KT):
                for i, (a, c) in enumerate(PASSES):
                    st = wsplit[:, g % 4, a, k * P:(k + 1) * P] if w is None else w[:, a, k, :]
                    last = nc.tensor.matmul(ps[0:M, b, 0:GW], st, xt[:, c, k, ng * GW:(ng + 1) * GW],
                                            start=(k == 0 and i == 0), stop=(k == KT - 1 and i == 2))
            last.then_inc(t_full, 1)

        def product(g, use, xt, before=None):
            for grp in range(NG):
                for j in range(4):
                    if before:
                        before(4 * grp + j)
                    pe.wait_ge(lo_done, g + j + 1)
                    for t in range(GROUP):
                        u = use + grp * GROUP + t
                        if j == 0 and u >= 6:
                            pe.wait_ge(g_free, u - 5)
                        tok = (grp * GROUP + t) * P
                        for k in range(2):
                            for i, (a, c) in enumerate(PASSES):
                                last = nc.tensor.matmul(
                                    ps[:, u % 6, :], xt[:, a, 2 * j + k, tok:tok + P],
                                    wsplit[:, (g + j) % 4, c, k * 512:(k + 1) * 512],
                                    start=(j == 0 and k == 0 and i == 0), stop=(j == 3 and k == 1 and i == 2))
                        if j == 3:
                            last.then_inc(g_full, 1)
                    if grp == NG - 1:
                        if j == 3:
                            pe.wait_ge(g_full, use + TILES)
                            pe.sem_inc(w_used, 1)
                        else:
                            last.then_inc(w_used, 1)

        pe.wait_ge(c_in, 16)
        for t in range(TILES):
            pe.wait_ge(x_in[t], 16)
            for half in range(2):
                transposes(TU_X0 + 2 * t + half, xin, t, half)
        pe.wait_ge(t_free, TU_GL)
        pe.wait_ge(gl_lo, 1)
        for ng in range(NG):
            quarter_cols(0, TU_GL + ng, XTR[0], ng, M=16, w=wgls)
        for m in range(8):
            pe.wait_ge(lo_done, m + 1)
            for ng in range(NG):
                quarter_cols(m, TU_Q + 3 * m + ng, XTR[0], ng)
            pe.wait_ge(t_full, TU_Q + 3 * m + 3)
            pe.sem_inc(w_used, 1)

        def logits(v_step):
            def f(step):
                step += 12 * v_step
                if step not in LOG_AT:
                    return
                h, ng = LOG_AT[step]
                u = TU_LOG + step // 2
                b = t_bank(u)
                if step == 0:
                    pe.wait_ge(wgu_in, 16)
                nc.tensor.matmul(ps[:, b, 0:GW], wgu[:, h * DK:(h + 1) * DK], glT[ng],
                                 start=True, stop=True).then_inc(t_full, 1)
            return f
        for u in range(2):
            product(G_V + 4 * u, GU_V + TILES * u, XTR[0], before=logits(u))
        for u in range(2):
            product(G_R + 4 * u, GU_R + TILES * u, XTR[0])

        pe.wait_ge(g_free, GU_O)
        pe.wait_ge(t_free, TU_O1)
        pe.wait_ge(qk_done, 3 * H_A * NG)

        def scores(s):
            t, h = s // H_A, s % H_A
            pe.wait_ge(kt_pre, s + 1)
            if s:
                pe.wait_ge(kt_tok, s)
                pe.wait_ge(at_m, s)
            nc.tensor.transpose(ps[:, 0, 0:P], ktT[:, s % 2, :], ident).then_inc(pe_kt, 1)
            nc.tensor.matmul(ps[:, 1, 0:P], qkT[:, 1, h, t * P:(t + 1) * P], qkT[:, 0, h, t * P:(t + 1) * P],
                             start=True, stop=True).then_inc(pe_at, 1)

        def outputs(s):
            t, h = s // H_A, s % H_A
            pe.wait_ge(kt_tok, s + 1)
            for c in range(2):
                if s:
                    pe.wait_ge(s_upd, 2 * (s - 1) + c + 1)
                nc.tensor.matmul(ps[:, 2 + c, 0:DV], kts[c * CH:(c + 1) * CH, s % 2, :],
                                 vO[c * CH:(c + 1) * CH, t, h * DV:(h + 1) * DV],
                                 start=True, stop=True).then_inc(pe_kv, 1)
            pe.wait_ge(at_m, s + 1)
            if t >= 2 and h % 2 == 0:
                pe.wait_ge(o_evac, 2 * (t - 2) + h // 2 + 1)
            o = ps[:, 4 + 2 * (t % 2) + h // 2, (h % 2) * DV:(h % 2 + 1) * DV]
            nc.tensor.matmul(o, attm[:, s % 2, :], vO[:, t, h * DV:(h + 1) * DV], start=True, stop=True)
            q = qkT[:, 0, h, t * P:(t + 1) * P]
            if t:
                pe.wait_ge(s_upd, 2 * (s - 4) + 2)
                nc.tensor.matmul(o[0:CH], q[:, 0:CH], S[:, 0, h, :], start=False, stop=True,
                                 skip_group_check=True).then_inc(pe_i0, 1)
            pe.wait_ge(s_upd, 2 * s + 1)
            nc.tensor.matmul(o[CH:P], q[:, CH:P], S[:, 1, h, :], start=False, stop=True,
                             skip_group_check=True).then_inc(pe_o, 1)

        steps = PT * H_A
        scores(0)
        for s in range(steps):
            if s + 1 < steps:
                scores(s + 1)
            outputs(s)

        pe.wait_ge(ktS_done, 4)
        pe.wait_ge(kt_tok, steps)
        pe.wait_ge(at_m, steps)
        tok = slice(PT * P, TOK)
        for h in range(H_A):
            nc.tensor.transpose(ps[:, 0, h * P:(h + 1) * P], ktS[:, h, :], ident).then_inc(peS_kt, 1)
            last = nc.tensor.matmul(ps[:, 1, h * P:(h + 1) * P], qkT[:, 1, h, tok], qkT[:, 0, h, tok],
                                    start=True, stop=True)
        last.then_inc(peS_at, 1)
        pe.wait_ge(ss_in, 16 * STREAMS)
        pe.wait_ge(o_evac, 2 * PT - 2)
        for i in range(8):
            h, vh = i // 2, i % 2
            for b in range(STREAMS):
                last = nc.tensor.matmul(ps[:, 4 + i // 4, (i % 4) * P + b * 16:(i % 4) * P + b * 16 + 16],
                                        Ss[:, b, h, vh * P:(vh + 1) * P],
                                        qkT[:, 0, h, PT * P + b * 16:PT * P + b * 16 + 16],
                                        start=True, stop=True)
        last.then_inc(peS_oT, 1)
        pe.wait_ge(attS_done, 1)
        pe.wait_ge(oT_done, 1)
        pe.wait_ge(o_evac, 2 * PT)
        for h in range(H_A):
            o = ps[:, 6 + h // 2, (h % 2) * DV:(h % 2 + 1) * DV]
            nc.tensor.matmul(o, attS[:, h, :], vO[:, PT, h * DV:(h + 1) * DV], start=True, stop=True)
            for vh in range(2):
                last = nc.tensor.matmul(o[:, vh * P:(vh + 1) * P], oT[:, 2 * h + vh, :], ident,
                                        start=False, stop=True, skip_group_check=True)
            last.then_inc(pe_o, 1)
        pe.wait_ge(ktb_done, 1)
        for b in range(STREAMS):
            for hp in range(2):
                i = 2 * b + hp
                if i >= 4:
                    pe.wait_ge(Ss_done, i - 3)
                for k in range(2):
                    h = 2 * hp + k
                    last = nc.tensor.matmul(ps[:, i % 4, k * DV:(k + 1) * DV], ktb[:, b, h * P:(h + 1) * P],
                                            vO[:, PT, h * DV:(h + 1) * DV], start=True, stop=True)
                last.then_inc(peS_kv, 1)
        for t in range(TILES):
            pe.wait_ge(gated, t + 1)
            for half in range(2):
                transposes(TU_O1 + 2 * t + half, vO, t, half)

        def down(g, use, c):
            for nh in range(2):
                for grp in range(NG):
                    for kp in range(2):
                        q = 2 * nh + kp
                        pe.wait_ge(lo_done, g + q + 1)
                        for t in range(GROUP):
                            v = nh * TILES + grp * GROUP + t
                            if kp == 0:
                                pe.wait_ge(g_free, use + v - 5)
                            tok = (grp * GROUP + t) * P
                            for k in range(2):
                                for i, (a, b) in enumerate(PASSES):
                                    last = nc.tensor.matmul(
                                        ps[:, v % 6, :], hT[:, a, 2 * kp + k, tok:tok + P],
                                        wsplit[:, q, b, k * 512:(k + 1) * 512],
                                        start=(kp == 0 and k == 0 and i == 0),
                                        stop=(kp == 1 and k == 1 and i == 2))
                            if kp == 1:
                                last.then_inc(g_full, 1)
                        if grp == NG - 1:
                            if kp == 0:
                                last.then_inc(w_used, 1)
                            else:
                                pe.wait_ge(g_full, use + nh * TILES + TILES)
                                pe.sem_inc(w_used, 1)

        def up(lay, k, u, m, ng, xt, g):
            if ng == 0:
                pe.wait_ge(lo_done, g + m + 1)
            quarter_cols(m, u, xt, ng)
            if ng == NG - 1:
                pe.wait_ge(t_full, u + 1)
                pe.sem_inc(w_used, 1)

        def product_norm(lay, g, use, xt_in, xt_out):
            seq = after_norm(lay)

            def first_group(step):
                if 8 <= step < 11:
                    for u, _, t, half in seq[2 * (step - 8):2 * (step - 8) + 2]:
                        if half == 0:
                            pe.wait_ge(ln_done, 2 * lay * TILES + t + 1)
                        transposes(u, X, t, half)
            product(g, use, xt_in)
            product(g + 4, use + TILES, xt_in, before=first_group)
            k = 0
            for u, kind, p, q in seq[2 * GROUP:]:
                if kind == "tr":
                    if q == 0:
                        pe.wait_ge(ln_done, 2 * lay * TILES + p + 1)
                    transposes(u, X, p, q)
                else:
                    if p == 0 and q < NG:
                        pe.wait_ge(t_free, seq[0][0] + {0: 6, 1: 14, 2: 22}[q])
                    up(lay, k, u, p, q, xt_out, G_MLP[lay])
                    k += 1

        def mlp(lay, xt):
            for c in range(NFC):
                if c:
                    for m in range(4):
                        for ng in range(NG):
                            k = 12 * c + 3 * m + ng
                            up(lay, k, TU_UP[lay] + k, m, ng, xt, G_MLP[lay] + 8 * c)
                pe.wait_ge(up_done, 96 * lay + 12 * (c + 1))
                down(G_MLP[lay] + 8 * c + 4, GU_MLP[lay] + 2 * TILES * c, c)

        pe.wait_ge(t_free, TU_O1 + 2 * TILES)
        product_norm(0, G_O, GU_O, XTR[1], XTR[2])
        mlp(0, XTR[2])
        def next_group(step):
            if step % 4 == 0:
                grp = step // 4
                for t in range(grp * GROUP, (grp + 1) * GROUP):
                    pe.wait_ge(ln_done, TILES + t + 1)
                    for half in range(2):
                        transposes(TU_L[1] + 2 * t + half, X, t, half)
                pe.wait_ge(t_free, TU_L[1] + 2 * GROUP * (grp + 1))
        for u in range(6):
            product(G_KVQ + 4 * u, GU_KVQ + TILES * u, XTR[3], before=next_group if u == 0 else None)

        pe.wait_ge(g_free, GU_O2)
        pe.wait_ge(t_free, TU_O2)

        def prepare(h, j):
            i = 8 * h + j
            pair = 4 * h + j // 2
            if j % 2 == 0:
                pe.wait_ge(h_kq[pair % 2], 128 * (pair // 2 + 1))
            if i:
                pe.wait_ge(p_free, i)
            for k in range(4):
                last = nc.tensor.transpose(ps[:, 4, k * P:(k + 1) * P],
                                           kqd[:, pair % 2, k, j % 2].rearrange("p a d -> p (a d)"), ident)
            last.then_inc(p_full, 1)

        def scores(s):
            h, i = s // PT, s % PT
            w = (i + 1) * P
            if i == 0:
                pe.wait_ge(p_free, 8 * (h + 1))
            for c in range(2):
                if s:
                    pe.wait_ge(ex_done, 2 * (s - 1) + c + 1)
                for b in range((w + 511) // 512):
                    n = min(512, w - 512 * b)
                    o = ps[:, 2 * c + b, 0:n]
                    q = QS[:, h % 2, c, i * P:(i + 1) * P]
                    diag = 512 * b + n == w
                    nc.tensor.matmul(o, q, KD[:, h % 2, 0, c, 512 * b:512 * b + n], start=True, stop=False)
                    last = nc.tensor.matmul(o, q, KD[:, h % 2, 1, c, 512 * b:512 * b + n], start=False,
                                            stop=True)
                    if diag:
                        last = nc.tensor.matmul(ps[:, 2 * c + b, n - P:n], mrow[:, 0:P], mrow[:, P:2 * P],
                                                start=False, stop=True, skip_group_check=True)
                last.then_inc(s_full, 1)

        def weights(s):
            i = s % PT
            pe.wait_ge(cb_done, s + 1)
            for b in range(a_banks(s)):
                use = a_count[s] + b
                if use >= 2:
                    pe.wait_ge(a_free, use - 1)
                for kt in range(4 * b, min(4 * b + 4, i + 1)):
                    last = nc.tensor.transpose(ps[:, 5 + use % 2, (kt - 4 * b) * P:(kt - 4 * b + 1) * P],
                                               PR[:, s % 2, 0, kt * P:(kt + 1) * P], ident)
                last.then_inc(a_full, 1)

        def values(s):
            h, i = s // PT, s % PT
            pe.wait_ge(a_free, a_count[s + 1])
            pe.wait_ge(v_lo, h + 1)
            if s:
                pe.wait_ge(o_free, s)
            for kt in range(i + 1):
                for n, (a, b) in enumerate(PASSES):
                    last = nc.tensor.matmul(ps[:, 7, 0:P], AT[:, s % 2, a, kt, :], vsp[h % 2][:, b, kt, :],
                                            start=(kt == 0 and n == 0), stop=(kt == i and n == 2))
            last.then_inc(o_full, 1)

        pe.wait_ge(mr_in, 16)
        for j in range(8):
            prepare(0, j)
        scores(0)
        for s in range(H_B * PT):
            if s // PT + 1 < H_B:
                prepare(s // PT + 1, s % PT)
            if s + 1 < H_B * PT:
                scores(s + 1)
            weights(s)
            if s:
                values(s - 1)
        values(H_B * PT - 1)

        pe.wait_ge(S_in, 48)
        pe.wait_ge(att_done, 1)
        for i in range(2):
            for z in range(2):
                for k in range(4):
                    last = nc.tensor.transpose(ps[:, 2 * i + z, k * P:(k + 1) * P],
                                               kqS[:, i, (4 * z + k) * P:(4 * z + k + 1) * P], ident)
                last.then_inc(S_tr, 1)
        pe.wait_ge(S_cp, 4)

        def cache_keys(w):
            b, z = w // 2, w % 2
            if z == 0:
                pe.wait_ge(kc_in[b % 2], 32 * (b // 2 + 1))
            for hh in range(4):
                ev = (k_ev0, k_ev1)[hh % 2]
                n = 2 * w + hh // 2
                if n:
                    pe.wait_ge(ev, n)
                for kt in range(4):
                    last = nc.tensor.transpose(ps[:, 4 + hh % 2, kt * P:(kt + 1) * P],
                                               Kc[:, b % 2, kt, (4 * z + hh) * P:(4 * z + hh + 1) * P], ident)
                last.then_inc(k_tr, 1)

        def scores2(w):
            b, z = w // 2, w % 2
            pe.wait_ge(S_qb, 8 * (b + 1))
            pe.wait_ge(k_ev0, 2 * w + 2)
            pe.wait_ge(k_ev1, 2 * w + 2)
            if w >= 2:
                pe.wait_ge(s2_ex, 2 * w - 2)
            bank = 2 * (w % 2)
            for hh in range(4):
                q = Qbd[:, b % 2, 4 * z + hh, :]
                nc.tensor.matmul(ps[:, bank, :], q, KTb[:, w % 2, hh, :], start=(hh == 0), stop=(hh == 3))
            for hh in range(4):
                q = Qbd[:, b % 2, 4 * z + hh, :]
                last = nc.tensor.matmul(ps[:, bank + 1, 0:16], q, KTn[:, 4 * z + hh, 16 * b:16 * b + 16],
                                        start=(hh == 0), stop=(hh == 3))
            last.then_inc(s2_full, 1)

        def weights2(w):
            pe.wait_ge(s2_ex, 2 * w + 2)
            pe.wait_ge(s2_cm, w + 1)
            if w:
                pe.wait_ge(s2_atc, w)
            for kt in range(5):
                last = nc.tensor.matmul(ps[:, 6, kt * 64:(kt + 1) * 64], PS[:, w % 2, kt * P:(kt + 1) * P],
                                        CM[:, w % 2, :], start=True, stop=True)
            last.then_inc(s2_at, 1)

        def values2(w):
            b, z = w // 2, w % 2
            pe.wait_ge(s2_atc, w + 1)
            if w:
                pe.wait_ge(s2_ot, w)
            for hh in range(4):
                cols = slice((4 * z + hh) * P, (4 * z + hh + 1) * P)
                for kt in range(5):
                    v = Vc[:, b % 2, kt, cols] if kt < 4 else vS[:, cols]
                    last = nc.tensor.matmul(ps[:, 7, hh * 16:(hh + 1) * 16], v, ATs[:, w % 2, kt, hh * 16:(hh + 1) * 16],
                                            start=(kt == 0), stop=(kt == 4))
            last.then_inc(s2_pv, 1)

        cache_keys(0)
        for w in range(2 * STREAMS):
            if w + 1 < 2 * STREAMS:
                cache_keys(w + 1)
            scores2(w)
            weights2(w)
            values2(w)
        pe.wait_ge(s2_ot, 2 * STREAMS)
        for h in range(H_B):
            last = nc.tensor.transpose(ps[:, h // 4, (h % 4) * P:(h % 4 + 1) * P], oTs[:, h, :], ident)
        last.then_inc(s2_fin, 1)
        pe.wait_ge(o_back, 16 * PT)
        pe.wait_ge(s2_fo, 1)
        for t in range(TILES):
            for half in range(2):
                u = TU_O2 + 2 * t + half
                if t < PT:
                    transposes(u, oin, t, half)
                else:
                    transposes(u, oS[:].unsqueeze(1), 0, half)
        pe.wait_ge(t_free, TU_O2 + 2 * TILES)
        product_norm(1, G_O2, GU_O2, XTR[0], XTR[4])
        mlp(1, XTR[4])

    @block.vector
    def _(dve):
        def transposed_lo(u, xt, t, half, n_hi):
            dve.wait_ge(t_hi, n_hi)
            dst = slice(t * P, (t + 1) * P)
            nc.vector.tensor_tensor(xt[:, 1, 4 * half:4 * half + 4, dst],
                                    ps[:, 6 + u % 2, :].rearrange("p (k n) -> p k n", n=P),
                                    xt[:, 0, 4 * half:4 * half + 4, dst].bitcast(F32),
                                    ALU.subtract).then_inc(t_free, 1)

        hi = 0
        for t in range(TILES):
            for half in range(2):
                hi += 1
                transposed_lo(TU_X0 + 2 * t + half, XTR[0], t, half, hi)
        for ng in range(NG):
            u = TU_GL + ng
            dve.wait_ge(t_full, u + 1)
            if ng == 0:
                dve.wait_ge(t_free, TU_GL)
            nc.vector.tensor_copy(glT[ng], ps[0:16, 6 + u % 2, 0:GW]).then_inc(t_free, 1)
        for m in range(8):
            for ng in range(NG):
                u = TU_Q + 3 * m + ng
                dve.wait_ge(t_full, u + 1)
                dst = qkT[:, m // 4, m % 4, ng * GW:(ng + 1) * GW]
                if m < 4:
                    nc.vector.tensor_scalar(dst, ps[:, 6 + u % 2, 0:GW], float(DK) ** -0.5, None,
                                            ALU.mult).then_inc(t_free, 1)
                else:
                    nc.vector.tensor_copy(dst, ps[:, 6 + u % 2, 0:GW]).then_inc(t_free, 1)
        chain = 0
        for step in range(24):
            if step in LOG_AT:
                h, ng = LOG_AT[step]
                i = step // 2
                u = TU_LOG + i
                dve.wait_ge(t_full, u + 1)
                if i:
                    dve.wait_ge(b_done, i)
                nc.vector.tensor_scalar(gm[:], ps[:, 6 + u % 2, 0:GW], bg[:, h:h + 1], 0.0, ALU.add,
                                        ALU.min).then_inc(m_done, 1)
                dve.wait_ge(m_done, 2 * i + 1)
                nc.vector.scalar_tensor_tensor(gna[:], gm[:], 2.0, ps[:, 6 + u % 2, 0:GW], ALU.mult,
                                               ALU.subtract).then_inc(m_done, 1)
                dve.wait_ge(m_done, 2 * i + 2)
                dve.sem_inc(t_free, 1)
                dve.wait_ge(lg_done, i + 1)
                nc.vector.tensor_tensor(gm[:], gm[:], gna[:], ALU.subtract).then_inc(sts, 1)
                dve.wait_ge(sts, i + 1)
                if i:
                    dve.wait_ge(eb_done, 2 * i)
                pos, nscan = ng * GW, 0
                while pos < (ng + 1) * GW:
                    w = CH if pos < PT * P else SEQ_S
                    o = pos - ng * GW
                    last = nc.vector.tensor_tensor_scan(gb[:, o:o + w], cst[:, C_ONE:C_ONE + w], gm[:, o:o + w],
                                                        0.0, ALU.mult, ALU.add)
                    pos += w
                last.then_inc(b_done, 1)
                dve.wait_ge(eb_done, 2 * i + 2)
                q = qkT[:, 0, h, ng * GW:(ng + 1) * GW]
                k = qkT[:, 1, h, ng * GW:(ng + 1) * GW]
                nc.vector.tensor_tensor(q, q, geb[:], ALU.mult).then_inc(qk_done, 1)
                nc.vector.tensor_tensor(k, k, genb[:], ALU.mult).then_inc(qk_done, 1)
                if ng < 2:
                    nc.vector.tensor_copy(elast[:, h, 6 * ng:6 * ng + 6], geb[:, CH - 1::CH]).then_inc(qk_done, 1)
                else:
                    nc.vector.tensor_copy(elast[:, h, 12:16], geb[:, CH - 1:4 * CH:CH])
                    nc.vector.tensor_copy(elast[:, h, 16:24], geb[:, 4 * CH + SEQ_S - 1::SEQ_S]).then_inc(qk_done, 1)
            if step % 4 == 3:
                for t in range(GROUP):
                    use = GU_V + (step // 4) * GROUP + t
                    dve.wait_ge(g_full, use + 1)
                    if step == 11 or step == 23:
                        dve.wait_ge(t_full, 0 + TU_LOG + min(H_A * NG, 12))  if 0 else None
                    tile = use % TILES
                    nc.vector.tensor_copy(vO[:, tile, (use // TILES) * 512:(use // TILES + 1) * 512],
                                          ps[:, use % 6, :]).then_inc(g_free, 1)
        for n in range(2 * TILES):
            use = GU_R + n
            dve.wait_ge(re_done, n + 1)
            nc.vector.tensor_scalar(sie[:, n % 2, :], sie[:, n % 2, :], 1.0, None, ALU.add).then_inc(rr_done, 1)
            dve.wait_ge(rr_done, 2 * n + 1)
            nc.vector.reciprocal(sie[:, n % 2, :], sie[:, n % 2, :]).then_inc(rr_done, 1)
            dve.wait_ge(rr_done, 2 * n + 2)
            if n >= 2:
                dve.wait_ge(r_out[n % 2], 16 * (n // 2))
            nc.vector.tensor_tensor(sio[:, n % 2, :], ps[:, use % 6, :], sie[:, n % 2, :],
                                    ALU.mult).then_inc(ro_done, 1)
            dve.wait_ge(ro_done, n + 1)
            dve.sem_inc(g_free, 1)

        def mask(s):
            dve.wait_ge(pe_at, s + 1)
            if s >= 2:
                dve.wait_ge(pe_o, s - 1)
            nc.vector.tensor_tensor(attm[:, s % 2, :], ps[:, 1, 0:P], cst[:, C_MP:C_MP + P],
                                    ALU.mult).then_inc(at_m, 1)

        def update(s):
            t, h = s // H_A, s % H_A
            dve.wait_ge(pe_kv, 2 * s + 1)
            if t:
                dve.wait_ge(pe_o, s - 3)
                nc.vector.scalar_tensor_tensor(S[:, 1, h, :], S[:, 0, h, :], elast[:, h, 2 * t:2 * t + 1],
                                               ps[:, 2, 0:DV], ALU.mult, ALU.add).then_inc(s_upd, 1)
            else:
                nc.vector.tensor_copy(S[:, 1, h, :], ps[:, 2, 0:DV]).then_inc(s_upd, 1)
            dve.wait_ge(pe_kv, 2 * s + 2)
            dve.wait_ge(s_upd, 2 * s + 1)
            if t:
                dve.wait_ge(pe_i0, s + 1 - H_A)
            nc.vector.scalar_tensor_tensor(S[:, 0, h, :], S[:, 1, h, :], elast[:, h, 2 * t + 1:2 * t + 2],
                                           ps[:, 3, 0:DV], ALU.mult, ALU.add).then_inc(s_upd, 1)

        def mean_square(p):
            dve.wait_ge(o_sq, 2 * p + 2)
            if p >= 4:
                dve.wait_ge(o_rs, p - 3)
            nc.vector.tensor_scalar(ms[:, p % 4, :], ss[:, p % 4, :], 1.0 / DV, EPS, ALU.mult,
                                    ALU.add).then_inc(o_ms, 1)

        def normed(p):
            t, hp = p // 2, p % 2
            dve.wait_ge(o_rs, p + 1)
            if p >= 2 * PT:
                dve.wait_ge(peS_kv, 2 * STREAMS)
            bank = 4 + 2 * (t % 2) + hp if t < PT else 6 + hp
            for k in range(2):
                h = 2 * hp + k
                last = nc.vector.scalar_tensor_tensor(vO[:, t, h * DV:(h + 1) * DV],
                                                      ps[:, bank, k * DV:(k + 1) * DV],
                                                      rs4[:, p % 4, k:k + 1], gna_g[:], ALU.mult, ALU.mult)
            last.then_inc(o_evac, 1)

        dve.wait_ge(qk_done, 3 * H_A * NG)
        dve.wait_ge(w_used, G_O)
        dve.wait_ge(gna_in, 16)
        for h in range(H_A):
            nc.vector.tensor_tensor(ktS[:, h, :].rearrange("p (b s) -> p b s", b=STREAMS),
                                    qkT[:, 1, h, PT * P:TOK].rearrange("p (b s) -> p b s", b=STREAMS),
                                    elast[:, h, 16:24].unsqueeze(2).broadcast_to([P, STREAMS, SEQ_S]),
                                    ALU.mult).then_inc(ktS_done, 1)
        steps = PT * H_A
        mask(0)
        for s in range(steps):
            if s + 1 < steps:
                mask(s + 1)
            update(s)
            if s >= 2:
                if s % 2 == 0:
                    mean_square(s // 2 - 1)
                else:
                    normed(s // 2 - 1)
        mean_square(steps // 2 - 1)
        normed(steps // 2 - 1)
        dve.wait_ge(peS_at, 1)
        nc.vector.tensor_tensor(attS[:], ps[:, 1, :].rearrange("p (h n) -> p h n", h=H_A),
                                cst[:, C_MS:C_MS + P].unsqueeze(1).broadcast_to([P, H_A, P]),
                                ALU.mult).then_inc(attS_done, 1)
        for p in (2 * PT, 2 * PT + 1):
            mean_square(p)
        dve.wait_ge(peS_oT, 1)
        for b in range(STREAMS):
            for hp in range(2):
                i = 2 * b + hp
                dve.wait_ge(peS_kv, i + 1)
                for k in range(2):
                    h = 2 * hp + k
                    last = nc.vector.scalar_tensor_tensor(Ss[:, b, h, :], Ss[:, b, h, :],
                                                          elast[:, h, 16 + b:17 + b],
                                                          ps[:, i % 4, k * DV:(k + 1) * DV], ALU.mult, ALU.add)
                last.then_inc(Ss_done, 1)
        for p in (2 * PT, 2 * PT + 1):
            normed(p)
        def gate(t):
            dve.wait_ge(r_back[t % 2], 16 * (t // 2 + 1))
            if t == 0:
                dve.wait_ge(o_evac, 2 * TILES)
            nc.vector.tensor_tensor(vO[:, t, :], vO[:, t, :], rin[:, t % 2, :], ALU.mult).then_inc(gated, 1)
        gate(0)
        for t in range(TILES):
            if t + 1 < TILES:
                gate(t + 1)
            for half in range(2):
                hi += 1
                transposed_lo(TU_O1 + 2 * t + half, XTR[1], t, half, hi)

        hi_n = [hi]

        def lo_of(u, xt, t, half):
            hi_n[0] += 1
            transposed_lo(u, xt, t, half, hi_n[0])

        def residual(u, t, nh, scale):
            dve.wait_ge(g_full, u + 1)
            x = X[:, t, nh * 512:(nh + 1) * 512]
            if scale is None:
                nc.vector.tensor_tensor(x, x, ps[:, u % 6, :], ALU.add).then_inc(g_free, 1)
            else:
                nc.vector.scalar_tensor_tensor(x, x, scale, ps[:, u % 6, :], ALU.mult, ALU.add).then_inc(g_free, 1)

        def norm(n, grp, use_end):
            tiles = range(grp * GROUP, (grp + 1) * GROUP)
            dve.wait_ge(g_free, use_end)
            for t in tiles:
                i = n * TILES + t
                for k in range(2):
                    nc.vector.bn_stats(bst[:, i % 3, 6 * k:6 * k + 6], X[:, t, k * 512:(k + 1) * 512]).then_inc(ln_st, 1)
                dve.wait_ge(ln_st, 3 * i + 2)
                nc.vector.bn_aggr(mv[:, i % 3, :], bst[:, i % 3, :]).then_inc(ln_st, 1)
                dve.wait_ge(ln_st, 3 * i + 3)
                nc.vector.tensor_scalar(mv[:, i % 3, 1:2], mv[:, i % 3, 1:2], EPS, None, ALU.add).then_inc(ln_var, 1)
            for t in tiles:
                i = n * TILES + t
                dve.wait_ge(ln_rstd, i + 1)
                nc.vector.scalar_tensor_tensor(nmr[:, i % 3:i % 3 + 1], mv[:, i % 3, 0:1], -1.0,
                                               rstd[:, i % 3:i % 3 + 1], ALU.mult, ALU.mult).then_inc(ln_nmr, 1)
            for t in tiles:
                i = n * TILES + t
                dve.wait_ge(ln_gain, i + 1)
                nc.vector.tensor_tensor(X[:, t, :], X[:, t, :], lng[:, 1, :], ALU.add).then_inc(ln_done, 1)

        def hidden(lay, k, u, m, ng):
            if k >= 2:
                dve.wait_ge(up_done, 96 * lay + k - 1)
            dve.wait_ge(t_full, u + 1)
            nc.vector.tensor_scalar(hsq[:, k % 2, :], ps[:, 6 + u % 2, 0:GW], 0.0, None, ALU.max).then_inc(up_r, 1)
            dve.wait_ge(up_r, 96 * lay + k + 1)
            dve.sem_inc(t_free, 1)

        def hidden_lo(lay, k, m, ng):
            dve.wait_ge(up_h, 96 * lay + k + 1)
            dst = slice(ng * GW, (ng + 1) * GW)
            nc.vector.tensor_tensor(hT[:, 1, m, dst], hsq[:, k % 2, :], hT[:, 0, m, dst].bitcast(F32),
                                    ALU.subtract).then_inc(up_done, 1)

        def product_norm(lay, use, xt):
            n = 2 * lay
            for t in range(TILES):
                residual(use + t, t, 0, ALPHA)
            use += TILES
            for t in range(GROUP):
                residual(use + t, t, 1, ALPHA)
            norm(n, 0, use + GROUP)
            for t in range(GROUP, 2 * GROUP):
                residual(use + t, t, 1, ALPHA)
            seq = after_norm(lay)
            for u, _, t, half in seq[:2 * GROUP]:
                lo_of(u, xt, t, half)
            norm(n, 1, use + 2 * GROUP)
            for t in range(2 * GROUP, TILES):
                residual(use + t, t, 1, ALPHA)
            k, last = 0, None
            for u, kind, p, q in seq[2 * GROUP:]:
                if kind == "tr":
                    if last:
                        hidden_lo(*last)
                        last = None
                    lo_of(u, xt, p, q)
                    if (p, q) == (2 * GROUP - 1, 1):
                        norm(n, 2, use + TILES)
                else:
                    hidden(lay, k, u, p, q)
                    if last:
                        hidden_lo(*last)
                    last = (lay, k, p, q)
                    k += 1
            hidden_lo(*last)

        def mlp(lay):
            n = 2 * lay + 1
            for c in range(NFC):
                if c:
                    for m in range(4):
                        for ng in range(NG):
                            k = 12 * c + 3 * m + ng
                            hidden(lay, k, TU_UP[lay] + k, m, ng)
                            if k % 12:
                                hidden_lo(lay, k - 1, *divmod(k % 12 - 1, 3))
                    hidden_lo(lay, 12 * c + 11, 3, 2)
                for nh in range(2):
                    for grp in range(NG):
                        for t in range(grp * GROUP, (grp + 1) * GROUP):
                            residual(GU_MLP[lay] + 2 * TILES * c + nh * TILES + t, t, nh, None if c else ALPHA)
                        if c == NFC - 1 and nh == 1 and grp == 0:
                            norm(n, 0, GU_MLP[lay] + 2 * TILES * c + TILES + GROUP)

        dve.wait_ge(x_res_in, 16 * TILES)
        product_norm(0, GU_O, XTR[2])
        mlp(0)
        for grp in range(NG):
            if grp:
                norm(1, grp, GU_KVQ)
            for t in range(grp * GROUP, (grp + 1) * GROUP):
                for half in range(2):
                    lo_of(TU_L[1] + 2 * t + half, XTR[3], t, half)

        nr = [0]
        for u in range(6):
            for t in range(TILES):
                n = u * TILES + t
                use = GU_KVQ + n
                dve.wait_ge(g_full, use + 1)
                if n >= 6:
                    dve.wait_ge(kv_out[n % 6], 16 * (n // 6))
                if u in (2, 3):
                    nc.vector.tensor_copy(kvs[:, n % 6, :], ps[:, use % 6, :]).then_inc(kv_done, 1)
                    dve.wait_ge(kv_done, n + 1)
                    dve.sem_inc(g_free, 1)
                    continue
                nc.vector.tensor_copy(kvs[:, n % 6, :], ps[:, use % 6, :]).then_inc(g_free, 1)
                dve.wait_ge(g_free, use + 1)
                v = kvs[:, n % 6, :].rearrange("p (g d) -> p g d", d=HD)
                x1, x2 = v[:, :, 0:ROT], v[:, :, ROT:2 * ROT]
                cos = cst[:, C_COS + t * ROT:C_COS + (t + 1) * ROT].unsqueeze(1).broadcast_to([P, 8, ROT])
                sin = cst[:, C_SIN + t * ROT:C_SIN + (t + 1) * ROT].unsqueeze(1).broadcast_to([P, 8, ROT])
                r = [rtmp[:, n % 2, i] for i in range(4)]
                for i, (x, tab) in enumerate(((x1, cos), (x2, sin), (x2, cos), (x1, sin))):
                    nc.vector.tensor_tensor(r[i], x, tab, ALU.mult).then_inc(rope, 1)
                nr[0] += 4
                dve.wait_ge(rope, nr[0])
                nc.vector.tensor_tensor(x1, r[0], r[1], ALU.subtract).then_inc(rope, 1)
                nr[0] += 1
                nc.vector.tensor_tensor(x2, r[2], r[3], ALU.add).then_inc(kv_done, 1)
                dve.wait_ge(rope, nr[0])
                dve.wait_ge(kv_done, n + 1)

        dve.wait_ge(lam_in, 16)
        dve.wait_ge(gnb_in, 16)
        for i in range(2):
            nc.vector.tensor_tensor(lamp[:, i, :], lamt[:, 2 * i, :], lamt[:, 2 * i + 1, :], ALU.mult).then_inc(chain_v, 1)
        dve.wait_ge(chain_v, 2)
        for i in range(2):
            nc.vector.reduce_sum(lam2[:, i:i + 1], lamp[:, i, :], AX.X).then_inc(lam_p, 1)
        nc.vector.tensor_scalar(gnb[:], gnb[:], 1.0 - LAMBDA_INIT, None, ALU.mult).then_inc(chain_v, 1)
        dve.wait_ge(lam_e, 1)
        nc.vector.tensor_tensor(nlam, lam2[:, 1:2], lam2[:, 0:1], ALU.subtract).then_inc(chain_v, 1)
        dve.wait_ge(chain_v, 4)
        nc.vector.tensor_scalar(nlam, nlam, LAMBDA_INIT, None, ALU.subtract).then_inc(chain_v, 1)
        dve.wait_ge(chain_v, 5)
        nc.vector.scalar_tensor_tensor(sgl, cst[:, C_SG + 1:C_SG + 2], nlam, cst[:, C_SG:C_SG + 1],
                                       ALU.mult, ALU.add).then_inc(nl_done, 1)

        def prepare(h, j):
            i = 8 * h + j
            dve.wait_ge(p_hi, i + 1)
            c, part = j % 2, j % 4 // 2
            cols = slice(part * 512, (part + 1) * 512)
            if j < 4:
                nc.vector.tensor_tensor(KD[:, h % 2, 1, c, cols], ps[:, 4, :], KD[:, h % 2, 0, c, cols].bitcast(F32),
                                        ALU.subtract).then_inc(p_free, 1)
            else:
                q = QS[HD:P, h % 2, c, cols]
                nc.vector.tensor_tensor(q, ps[HD:P, 4, :], q.bitcast(F32), ALU.subtract).then_inc(p_free, 1)

        def maxima(s):
            w = (s % PT + 1) * P
            if s >= 2:
                dve.wait_ge(nmx_done, s - 1)
            for c in range(2):
                dve.wait_ge(s_full, 2 * s + c + 1)
                nc.vector.reduce_max(mx[:, s % 2, c:c + 1], ps[:, 2 * c:2 * c + 2, :].rearrange("p a n -> p (a n)")[:, 0:w],
                                     AX.X).then_inc(mx_done, 1)
            dve.wait_ge(mx_done, 2 * s + 2)
            if s >= 2:
                dve.wait_ge(ex_done, 2 * s - 2)
            nc.vector.tensor_scalar(nmx[:, s % 2, :], mx[:, s % 2, :], -float(HD) ** -0.5, None,
                                    ALU.mult).then_inc(nmx_done, 1)

        def combine(s):
            w = (s % PT + 1) * P
            dve.wait_ge(g_done, s + 1)
            dve.wait_ge(ex_done, 2 * s + 2)
            nc.vector.scalar_tensor_tensor(PR[:, s % 2, 0, 0:w], PR[:, s % 2, 1, 0:w], gf[:, s % 4:s % 4 + 1],
                                           PR[:, s % 2, 0, 0:w], ALU.mult, ALU.add).then_inc(cb_done, 1)

        def weights_lo(s):
            for b in range(a_banks(s)):
                use = a_count[s] + b
                dve.wait_ge(a_hi, use + 1)
                n = min(4, s % PT + 1 - 4 * b)
                nc.vector.tensor_tensor(AT[:, s % 2, 1, 4 * b:4 * b + n, :],
                                        ps[:, 5 + use % 2, 0:n * P].rearrange("p (k n) -> p k n", n=P),
                                        AT[:, s % 2, 0, 4 * b:4 * b + n, :].bitcast(F32),
                                        ALU.subtract).then_inc(a_free, 1)

        def out_norm(s):
            dve.wait_ge(f_done, s + 1)
            dve.wait_ge(o_free, s + 1)
            if s >= 2:
                dve.wait_ge(o_out[s % 2], 16 * (s // 2))
            nc.vector.scalar_tensor_tensor(osb[:, s % 2, :], oraw[:, s % 2, :], of[:, s % 4:s % 4 + 1], gnb[:],
                                           ALU.mult, ALU.mult).then_inc(ob_done, 1)

        for j in range(8):
            prepare(0, j)
        maxima(0)
        for s in range(H_B * PT):
            if s // PT + 1 < H_B:
                prepare(s // PT + 1, s % PT)
            if s + 1 < H_B * PT:
                maxima(s + 1)
            combine(s)
            weights_lo(s)
            if s >= 2:
                out_norm(s - 2)
        out_norm(H_B * PT - 2)
        out_norm(H_B * PT - 1)
        for i in range(2):
            dve.wait_ge(o_out[i], 16 * H_B * PT // 2)
        dve.sem_inc(att_done, 1)

        for i in range(2):
            for z in range(2):
                dve.wait_ge(S_tr, 2 * i + z + 1)
                dst = (KTn, QTs)[i]
                nc.vector.tensor_copy(dst[:, 4 * z:4 * z + 4, :],
                                      ps[:, 2 * i + z, :].rearrange("p (k n) -> p k n", n=P)).then_inc(S_cp, 1)

        def cache_keys(w):
            for hh in (1, 3):
                dve.wait_ge(k_tr, 4 * w + hh + 1)
                if w >= 2:
                    dve.wait_ge(s2_full, w - 1)
                nc.vector.tensor_copy(KTb[:, w % 2, hh, :], ps[:, 5, :]).then_inc(k_ev1, 1)

        def maxima2(w):
            bank = 2 * (w % 2)
            dve.wait_ge(s2_full, w + 1)
            nc.vector.reduce_max(mx[:, w % 2, 0:1], ps[:, bank, :], AX.X).then_inc(chain_v, 1)
            nc.vector.reduce_max(mx[:, w % 2, 1:2], ps[:, bank + 1, 0:16], AX.X).then_inc(chain_v, 1)
            dve.wait_ge(chain_v, 5 + 3 * w + 2)
            nc.vector.tensor_tensor(mx[:, w % 2, 0:1], mx[:, w % 2, 0:1], mx[:, w % 2, 1:2], ALU.max).then_inc(chain_v, 1)
            dve.wait_ge(chain_v, 5 + 3 * w + 3)
            nc.vector.tensor_scalar(nmx[:, w % 2, 0:1], mx[:, w % 2, 0:1], -float(HD) ** -0.5, None,
                                    ALU.mult).then_inc(s2_mx, 1)

        def combination(w):
            dve.wait_ge(s2_co, w + 1)
            if w >= 2:
                dve.wait_ge(s2_at, w - 1)
            nc.vector.tensor_scalar(CM[:, w % 2, :], cst[:, C_SEL:C_SEL + 64], coef[:, w % 2:w % 2 + 1], None,
                                    ALU.mult).then_inc(s2_cm, 1)

        def outputs2(w):
            b, z = w // 2, w % 2
            dve.wait_ge(s2_pv, w + 1)
            nc.vector.tensor_copy(oTs[:, 4 * z:4 * z + 4, 16 * b:16 * b + 16],
                                  ps[:, 7, 0:64].rearrange("p (h i) -> p h i", h=4)).then_inc(s2_ot, 1)

        cache_keys(0)
        for w in range(2 * STREAMS):
            if w + 1 < 2 * STREAMS:
                cache_keys(w + 1)
            maxima2(w)
            combination(w)
            outputs2(w)
        dve.wait_ge(s2_finsq, H_B)
        nc.vector.tensor_scalar(msS, ssS, 1.0 / VD, EPS, ALU.mult, ALU.add).then_inc(s2_fms, 1)
        dve.wait_ge(s2_frs, 1)
        for h in range(H_B):
            last = nc.vector.scalar_tensor_tensor(oS[:, h * P:(h + 1) * P], ps[:, h // 4, (h % 4) * P:(h % 4 + 1) * P],
                                                  rsS[:, h:h + 1], gnb[:], ALU.mult, ALU.mult)
        last.then_inc(s2_fo, 1)
        for t in range(TILES):
            for half in range(2):
                lo_of(TU_O2 + 2 * t + half, XTR[0], t, half)
        product_norm(1, GU_O2, XTR[4])
        mlp(1)
        for grp in (1, 2):
            norm(3, grp, GU_MLP[1] + 2 * TILES * NFC)

    ctx.close()


_INS = ['x_prompt', 'x_sample', 'state_gla', 'cache_k', 'cache_v', 'w_in_a', 'w_gate_up_a', 'b_gate_a',
        'g_norm_a', 'w_o_a', 'w_kv', 'w_q_b', 'lam_b', 'g_norm_b', 'w_o_b', 'w_up', 'w_down', 'ln_g', 'ln_b']
_OUTS = [(1, 1024, 1024), (8, 16, 1024), (1, 1, 4, 128, 256), (1, 1024, 8, 2, 64), (1, 1024, 8, 128),
         (1, 8, 4, 128, 256), (8, 16, 8, 2, 64), (8, 16, 8, 128)]


def kernel(**inputs):
    import concourse.bacc as _bacc
    from concourse.bass_utils import run_bass_kernel_spmd as _run

    nc = _bacc.Bacc("TRN2", target_bir_lowering=False, num_devices=1)
    c, m = constants()
    arrays, args = {}, []
    inputs = dict(inputs, b_gate_a=np.asarray(inputs["b_gate_a"]).reshape(H_A, DK).T)
    for name, a in [(n, np.ascontiguousarray(inputs[n])) for n in _INS] + [("consts", c), ("maskrow", m)]:
        arrays[f"in_{name}"] = a
        args.append(nc.dram_tensor(f"in_{name}", a.shape, mybir.dt.from_np(a.dtype), kind="ExternalInput").ap())
    for i, shape in enumerate(_OUTS):
        args.append(nc.dram_tensor(f"out_{i}", shape, F32, kind="ExternalOutput").ap())
    encoder_step(nc, *args)
    r = _run(nc, [arrays], core_ids=[0])
    return tuple(r.results[0][f"out_{i}"] for i in range(len(_OUTS)))
```

```python
from contextlib import ExitStack

import numpy as np
import concourse.bass as bass
from concourse import mybir

F32 = mybir.dt.float32
F32R = mybir.dt.float32r
ALU = mybir.AluOpType
ACT = mybir.ActivationFunctionType
AX = mybir.AxisListType

P = 128
D = 1024
KT = D // P
TILES = 9
PT = TILES - 1
TOK = TILES * P
GROUP = 3
NG = TILES // GROUP
GW = GROUP * P
H_A, DK, DV = 4, 128, 256
CH = 64
H_B, HD, VD = 8, 64, 128
STREAMS, SEQ_S = 8, 16
PAST = 512
FF = 4 * D
FC = 512
NFC = FF // FC
ROT = HD // 4 // 2
ALPHA = float(4 ** 0.25)
LAMBDA_INIT = 0.8 - 0.6 * float(np.exp(-0.3))
EPS = 1e-5
PASSES = ((0, 0), (0, 1), (1, 0))
NEG = -1.0e30

C_ID = 0
C_MP = C_ID + P
C_MS = C_MP + P
C_SEL = C_MS + P
C_ROW = C_SEL + P
C_COS = C_ROW + STREAMS
C_SIN = C_COS + TILES * ROT
C_ONE = C_SIN + TILES * ROT
C_NH = C_ONE + CH
C_SG = C_NH + 10
C_END = C_SG + 2


def constants():
    c = np.zeros((P, C_END), np.float32)
    r = np.arange(P)
    c[:, C_ID:C_ID + P] = np.eye(P)
    j, i = r[:, None], r[None, :]
    c[:, C_MP:C_MP + P] = (j // CH == i // CH) & (j <= i)
    c[:, C_MS:C_MS + P] = (j // SEQ_S == i // SEQ_S) & (j <= i)
    c[:, C_SEL:C_SEL + P] = (j // 32 == i // 32) & (j % 16 == i % 32)
    c[:, C_ROW:C_ROW + STREAMS] = r[:, None] // SEQ_S == np.arange(STREAMS)[None, :]
    inv = 1.0 / (500000.0 ** (np.arange(0, 2 * ROT, 2, dtype=np.float32) / (2 * ROT)))
    for t in range(TILES):
        pos = (t * P + r) if t < PT else PAST + r % SEQ_S
        ang = pos.astype(np.float32)[:, None] * inv.astype(np.float32)[None, :]
        c[:, C_COS + t * ROT:C_COS + (t + 1) * ROT] = np.cos(ang)
        c[:, C_SIN + t * ROT:C_SIN + (t + 1) * ROT] = np.sin(ang)
    c[:, C_ONE:C_ONE + CH] = 1.0
    c[:, C_NH:C_NH + 8] = -0.5
    c[:, C_NH + 8:C_NH + 10] = -1.0
    c[:, C_SG] = (r // 16 % 2 == 0)
    c[:, C_SG + 1] = (r // 16 % 2 == 1)
    m = np.zeros((1, 2 * P), np.float32)
    m[0, :CH] = 1.0
    m[0, P + CH:] = NEG
    return c, m


def encoder_step(nc, x_prompt, x_sample, state_gla, cache_k, cache_v, w_in, w_gate, b_gate, g_norm_a,
                 w_o_a, w_kv, w_q, lam, g_norm_b, w_o_b, w_up, w_down, ln_g, ln_b, consts, maskrow,
                 y_prompt, y_sample, gla_prompt, k_prompt, v_prompt, gla_sample, k_sample, v_sample):
    ctx = ExitStack()

    base = 16512

    def at(name, offset, shape, dt=F32):
        return nc.alloc_sbuf_tensor_at(name, shape, dt, offset=offset)

    O_W = base
    O_RAW = O_W + 4 * 2 * 1024 * 4
    O_XT = O_RAW + 4 * 1024 * 4
    O_Q = O_XT + 2 * KT * TOK * 4
    O_V = O_Q + TILES * D * 4
    O_TMP = O_V + TILES * D * 4
    O_C = O_TMP + 11264
    wsplit = at("wsplit", O_W, [P, 4, 2, 1024], F32R)
    raw = at("raw", O_RAW, [P, 4, 1024])
    XTR = [at(f"xt{i}", O_XT, [P, 2, KT, TOK], F32R) for i in range(5)]
    cst = at("cst", O_C, [P, C_END])
    mrow = at("mrow", O_C + 2976, [1, 2 * P])
    stats = at("stats", O_C + 2976 + 1024, [P, 192])
    xin = at("xin", O_V, [P, TILES, D])
    X = at("x_res", O_Q, [P, TILES, D])
    qkT = at("qkT", O_Q, [P, 2, H_A, TOK])
    vO = at("vO", O_V, [P, TILES, D])
    glT = [vO[0:16, 2 * GROUP + g, 512:512 + GW] for g in range(NG)]
    hT = at("hT", O_V, [P, 2, 4, TOK], F32R)
    gm = at("gm", O_TMP, [P, GW])
    gna = at("gna", O_TMP + 1536, [P, GW])
    gb = at("gb", O_TMP + 2 * 1536, [P, GW])
    geb = at("geb", O_TMP + 3 * 1536, [P, GW])
    genb = at("genb", O_TMP + 4 * 1536, [P, GW])
    wglr = at("wglr", O_TMP + 5 * 1536, [P, KT, 16])
    wgls = at("wgls", O_TMP + 5 * 1536 + 512, [P, 2, KT, 16], F32R)
    wgu = at("wgu", O_TMP + 5 * 1536, [16, H_A * DK])
    sie = at("sie", O_TMP, [P, 2, 512])
    sio = at("sio", O_TMP + 4096, [P, 2, 512])
    rin = at("rin", O_TMP, [P, 2, D])
    lng = at("lng", O_TMP, [P, 2, D])
    hsq = at("hsq", O_TMP + 8192, [P, 2, GW])
    gna_g = at("gna_g", O_TMP + 10240, [P, DV])
    kvs = at("kvs", O_V, [P, 6, 512])
    rtmp = at("rtmp", O_V + 12288, [P, 2, 4, 8, ROT])
    kqd = at("kqd", O_TMP, [P, 2, 4, 2, 2, HD])
    KD = at("KD", O_XT, [P, 2, 2, 2, PT * P], F32R)
    QS = at("QS", O_XT + 32768, [P, 2, 2, PT * P], F32R)
    vhead = at("vhead", O_XT + 49152, [P, 3, PT, P])
    PR = at("PR", O_V, [P, 4, 2, PT * P])
    AT = at("AT", O_XT + 61440, [P, 2, PT, P])
    osb = at("osb", O_TMP + 10240, [P, 2, P])
    osq = at("osq", O_V + 33792, [P, P])
    oraw = at("oraw", O_V + 34304, [P, 2, P])
    gnb = at("gnb", O_TMP + 8192, [P, VD])
    lamt = at("lamt", O_TMP + 8704, [P, 4, HD])
    lamp = at("lamp", O_TMP + 9728, [P, 2, HD])
    Kc = at("Kc", O_XT, [P, 2, 4, D])
    Vc = at("Vc", O_XT + 32768, [P, 2, 4, D])
    vS = at("vS", O_XT + 65536, [P, D])
    KTn = at("KTn", O_XT + 69632, [P, H_B, P])
    Qbd = at("Qbd", O_V, [P, 2, H_B, P])
    KTb = at("KTb", O_V + 8192, [P, 2, 4, 512])
    kqS = at("kqS", O_RAW + 8192, [P, 2, D])
    PS = at("PS", O_V + 24576, [P, 2, 640])
    ATs = at("ATs", O_V + 29696, [P, 2, 5, P])
    oW = at("oW", O_RAW, [P, 2 * STREAMS, P])
    QTs = at("QTs", O_TMP, [P, H_B, P])
    oS = at("oS", O_TMP + 4096, [P, D])
    CM = at("CM", O_TMP + 9216, [P, 2, P])
    sqS = at("sqS", O_TMP + 10240, [P, P])
    oin = at("oin", O_V, [P, PT, D])
    nlam = stats[:, 176:177]
    sgl = stats[:, 177:178]
    lam2 = stats[:, 178:180]
    mx = stats[:, 0:4].rearrange("p (a b) -> p a b", a=2)
    nmx = stats[:, 4:8].rearrange("p (a b) -> p a b", a=2)
    ls = stats[:, 8:16].rearrange("p (a b) -> p a b", a=4)
    rl = stats[:, 16:24].rearrange("p (a b) -> p a b", a=4)
    gf = stats[:, 24:28]
    oss = stats[:, 28:32]
    rq = stats[:, 32:36]
    oms = stats[:, 36:40]
    ors = stats[:, 40:44]
    of = stats[:, 44:48]
    ssS = stats[:, 80:96]
    rsS = stats[:, 96:112]
    coef = stats[:, 72:74]
    bg = stats[:, 0:4]
    nbg = stats[:, 4:8]
    elast = stats[:, 8:8 + H_A * 24].rearrange("p (h c) -> p h c", h=H_A)
    ss = stats[:, 104:112].rearrange("p (a b) -> p a b", a=4)
    ms = stats[:, 112:120].rearrange("p (a b) -> p a b", a=4)
    rs4 = stats[:, 120:128].rearrange("p (a b) -> p a b", a=4)
    bst = stats[:, 128:164].rearrange("p (t s) -> p t s", t=3)
    mv = stats[:, 164:170].rearrange("p (t s) -> p t s", t=3)
    rstd = stats[:, 170:173]
    nmr = stats[:, 173:176]
    ktT = at("ktT", O_XT, [P, 2, P])
    kts = at("kts", O_XT + 1024, [P, 2, P])
    attm = at("attm", O_XT + 2048, [P, 2, P])
    S = at("S", O_XT + 3072, [P, 2, H_A, DV])
    sq = at("sq", O_XT + 3072 + 8192, [P, 2, DV])
    ktS = at("ktS", O_XT + 13312, [P, H_A, P])
    attS = at("attS", O_XT + 15360, [P, H_A, P])
    oT = at("oT", O_XT + 17408, [P, 8, P])
    ktb = at("ktb", O_XT + 21504, [P, STREAMS, H_A * P])
    Ss = at("Ss", O_XT + 37888, [P, STREAMS, H_A, DV])

    ident = cst[:, C_ID:C_ID + P]
    neg1 = cst[:, C_NH + 8:C_NH + 10]

    gate_scr = nc.dram_tensor("gate_scr", (TILES, P, D), F32, kind="Internal").ap()
    q_scr = nc.dram_tensor("q_scr", (TILES, P, D), F32, kind="Internal").ap()
    o_scr = nc.dram_tensor("o_scr", (TILES, P, D), F32, kind="Internal").ap()
    kv_dst = [[k_prompt[0].rearrange("(t p) h c d -> t p (h c d)", p=P)[t] for t in range(PT)]
              + [k_sample.rearrange("b s h c d -> (b s) (h c d)")],
              [v_prompt[0].rearrange("(t p) h v -> t p (h v)", p=P)[t] for t in range(PT)]
              + [v_sample.rearrange("b s h v -> (b s) (h v)")],
              [q_scr[t] for t in range(TILES)]]
    y_dst = [y_prompt[0, t * P:(t + 1) * P, :] for t in range(PT)] + [y_sample.rearrange("b s d -> (b s) d")]
    x_scr = [x_prompt[0, t * P:(t + 1) * P, :] for t in range(PT)] + [
        x_sample.rearrange("b s d -> (b s) d")]

    ps = ctx.enter_context(nc.psum_tensor("ps", [P, 8, 512], F32))

    def sem(name):
        return ctx.enter_context(nc.semaphore(name))

    c_in = sem("c_in")
    bg_in = sem("bg_in")
    mr_in = sem("mr_in")
    wgu_in = sem("wgu_in")
    tile_in = [sem(f"tile_in{t}") for t in range(TILES)]
    raw_in = [sem(f"raw_in{s}") for s in range(4)]
    hi_done = sem("hi_done")
    lo_done = sem("lo_done")
    w_used = sem("w_used")
    t_full = sem("t_full")
    t_hi = sem("t_hi")
    t_free = sem("t_free")
    g_full = sem("g_full")
    g_free = sem("g_free")
    gl_raw = sem("gl_raw")
    gl_hi = sem("gl_hi")
    gl_lo = sem("gl_lo")
    m_done = sem("m_done")
    lg_done = sem("lg_done")
    b_done = sem("b_done")
    eb_done = sem("eb_done")
    qk_done = sem("qk_done")
    la_done = sem("la_done")
    e_read = sem("e_read")
    re_done = sem("re_done")
    rr_done = sem("rr_done")
    rp_done = sem("rp_done")
    ro_done = sem("ro_done")
    r_out = [sem("r_out0"), sem("r_out1")]
    r_back = [sem("r_back0"), sem("r_back1")]
    kt_pre = sem("kt_pre")
    pe_kt = sem("pe_kt")
    pe_at = sem("pe_at")
    kt_tok = sem("kt_tok")
    pe_kv = sem("pe_kv")
    at_m = sem("at_m")
    s_upd = sem("s_upd")
    pe_i0 = sem("pe_i0")
    pe_o = sem("pe_o")
    o_sq = sem("o_sq")
    o_ms = sem("o_ms")
    o_rs = sem("o_rs")
    o_evac = sem("o_evac")
    ss_in = sem("ss_in")
    ktS_done = sem("ktS_done")
    peS_kt = sem("peS_kt")
    ktb_done = sem("ktb_done")
    peS_at = sem("peS_at")
    attS_done = sem("attS_done")
    peS_oT = sem("peS_oT")
    oT_done = sem("oT_done")
    peS_kv = sem("peS_kv")
    Ss_done = sem("Ss_done")
    st_out = sem("st_out")
    gated = sem("gated")
    gna_in = sem("gna_in")
    sts = sem("sts")
    y_out = sem("y_out")
    x_res_in = sem("x_res_in")
    lng_in = sem("lng_in")
    ln_var = sem("ln_var")
    ln_rstd = sem("ln_rstd")
    ln_nmr = sem("ln_nmr")
    ln_norm = sem("ln_norm")
    ln_gain = sem("ln_gain")
    ln_done = sem("ln_done")
    ln_st = sem("ln_st")
    up_r = sem("up_r")
    up_h = sem("up_h")
    up_sq = sem("up_sq")
    rope = sem("rope")
    kv_done = sem("kv_done")
    h_in0 = sem("h_in0")
    h_in1 = sem("h_in1")
    h_v = [sem(f"h_v{i}") for i in range(3)]
    p_full = sem("p_full")
    p_hi = sem("p_hi")
    p_free = sem("p_free")
    s_full = sem("s_full")
    mx_done = sem("mx_done")
    nmx_done = sem("nmx_done")
    ex_done = sem("ex_done")
    g_done = sem("g_done")
    cb_done = sem("cb_done")
    a_full = [sem("a_full0"), sem("a_full1")]
    a_free = [sem("a_free0"), sem("a_free1")]
    o_full = sem("o_full")
    osq_done = sem("osq_done")
    f_done = sem("f_done")
    ob_done = sem("ob_done")
    lam_in = sem("lam_in")
    lam_p = sem("lam_p")
    lam_e = sem("lam_e")
    nl_done = sem("nl_done")
    gnb_in = sem("gnb_in")
    o_out0 = sem("o_out0")
    o_out1 = sem("o_out1")
    S_in = sem("S_in")
    vS_in = sem("vS_in")
    S_tr = sem("S_tr")
    S_cp = sem("S_cp")
    S_qb = sem("S_qb")
    S_z = sem("S_z")
    kc_in = [sem("kc_in0"), sem("kc_in1")]
    vc_in = [sem("vc_in0"), sem("vc_in1")]
    k_tr = sem("k_tr")
    k_ev0 = sem("k_ev0")
    k_ev1 = sem("k_ev1")
    s2_full = sem("s2_full")
    s2_mx = sem("s2_mx")
    s2_ex = sem("s2_ex")
    s2_co = sem("s2_co")
    s2_cm = sem("s2_cm")
    s2_at = sem("s2_at")
    s2_atc = sem("s2_atc")
    s2_pv = sem("s2_pv")
    s2_ot = sem("s2_ot")
    s2_sq = sem("s2_sq")
    s2_rs = sem("s2_rs")
    s2_fin = sem("s2_fin")
    s2_out = sem("s2_out")
    ps_z = sem("ps_z")
    att_done = sem("att_done")
    att_small = sem("att_small")
    o_free = sem("o_free")
    up_done = sem("up_done")
    chain_v = sem("chain_v")
    kv_out = [sem(f"kv_out{i}") for i in range(6)]
    h_kq = [h_in0, h_in1]
    o_out = [o_out0, o_out1]

    TU_X0 = 0
    TU_GL = TU_X0 + 2 * TILES
    TU_Q = TU_GL + NG
    TU_LOG = TU_Q + 8 * NG
    TU_O1 = TU_LOG + H_A * NG
    TU_L = [0] * 3
    TU_L[0] = TU_O1 + 2 * TILES
    TU_UP = [0, 0]
    TU_UP[0] = TU_L[0] + 2 * TILES
    TU_L[1] = TU_UP[0] + NFC * 4 * NG
    TU_O2 = TU_L[1] + 2 * TILES
    TU_L[2] = TU_O2 + 2 * TILES
    TU_UP[1] = TU_L[2] + 2 * TILES
    GU_V = 0
    GU_R = GU_V + 2 * TILES
    GU_O = GU_R + 2 * TILES
    GU_MLP = [GU_O + 2 * TILES, 0]
    GU_KVQ = GU_MLP[0] + NFC * 2 * TILES
    GU_O2 = GU_KVQ + 6 * TILES
    GU_MLP[1] = GU_O2 + 2 * TILES
    UPS = NFC * 4 * NG
    G_QK, G_V, G_R, G_O = 0, 8, 16, 24
    G_MLP = [32, 0]
    G_KVQ = G_MLP[0] + 8 * NFC
    G_O2 = G_KVQ + 24
    G_MLP[1] = G_O2 + 8
    G_TOTAL = G_MLP[1] + 8 * NFC

    def a_banks(s):
        h, i = s // PT, s % PT
        if i < 4:
            return [(i % 2, range(i + 1), 6 * h + i // 2)]
        return [(0, range(4), 6 * h + i - 2), (1, range(4, i + 1), 6 * h + i - 2)]

    STEPS = H_B * PT

    def p_bank(i):
        return 4 + i % 4 if i < 8 else 4

    def after_norm(lay):
        def tr(grp):
            return [("tr", t, half) for t in range(grp * GROUP, (grp + 1) * GROUP) for half in range(2)]

        def up(ng, *ms):
            return [("up", m, ng) for m in ms]
        seq = (tr(0) + up(0, 0, 1, 2) + tr(1) + up(0, 3) + up(1, 0, 1, 2) + tr(2) + up(1, 3) + up(2, 0, 1, 2, 3))
        return [(TU_L[2 * lay] + i, *e) for i, e in enumerate(seq)]

    def quarter_use():
        free = [(t_full, TU_Q + 3 * m + 3) for m in range(8)]
        used = [0]

        def count():
            used[0] += 1
            return (w_used, used[0])

        def of_product(use):
            free.extend([count(), count(), count(), (g_full, use + TILES)])

        for use in (GU_V, GU_R, GU_O):
            of_product(use)
            of_product(use + TILES)
        for lay in range(2):
            first = {e[2]: e[0] + 1 for e in after_norm(lay) if e[1] == "up" and e[3] == NG - 1}
            for c in range(NFC):
                for m in range(4):
                    free.append((t_full, first[m] if c == 0 else TU_UP[lay] + 12 * c + 3 * m + NG))
                for nh in range(2):
                    done = TILES * (nh + 1) if c < NFC - 1 else 5 * GROUP + GROUP * nh
                    free.extend([count(), (g_full, GU_MLP[lay] + 2 * TILES * c + done)])
            if lay == 0:
                for u in range(8):
                    of_product(GU_KVQ + TILES * u)
        return free

    QUARTER_FREE = quarter_use()

    def chunk_quarter_free(lay, c, q):
        semaphore, first = QUARTER_FREE[G_MLP[lay] + 8 + q]
        step = QUARTER_FREE[G_MLP[lay] + 16 + q][1] - first
        return semaphore, c * step + (first - step)

    FIRST_UP = [e[2:] for e in after_norm(0) if e[1] == "up"]
    DOWN_ORDER = [[(nh, grp) for nh in range(2) for grp in range(NG)],
                  [(nh, grp) for grp in range(NG) for nh in range(2)]]
    LOG_AT = {2 * i: (i // NG, i % NG) for i in range(H_A * NG)}

    block = ctx.enter_context(nc.Block())

    @block.sync
    def _(sp):
        def load(g, src, n):
            if g >= 4:
                sp.wait_ge(lo_done, g - 3)
            sp.dma_start(raw[:, g % 4, :].rearrange("p (k n) -> p k n", n=n),
                         src.rearrange("(k p) n -> p k n", p=P)).then_inc(raw_in[g % 4], 16)

        def load_p(g, w, u):
            for j in range(4):
                load(g + j, w[j * 256:(j + 1) * 256, u * 512:(u + 1) * 512], 512)

        for t in range(3):
            sp.dma_start(xin[:, t, :], x_scr[t]).then_inc(tile_in[t], 16)
            if t == 0:
                sp.dma_start(cst[:], consts).then_inc(c_in, 16)
        for m in range(4):
            load(m, w_in[0, :, m * P:(m + 1) * P], P)
            if m < 3:
                for t in (3 + 2 * m, 4 + 2 * m):
                    sp.dma_start(xin[:, t, :], x_scr[t]).then_inc(tile_in[t], 16)
        sp.dma_start(wglr[:], w_in[0, :, 3072:3088].rearrange("(k p) n -> p k n", p=P)).then_inc(gl_raw, 16)
        sp.dma_start(bg, b_gate).then_inc(bg_in, 16)
        sp.dma_start(gna_g[:], g_norm_a[0:1, :].broadcast_to([P, DV])).then_inc(gna_in, 16)
        sp.dma_start(mrow[:], maskrow).then_inc(mr_in, 16)
        for m in range(4, 8):
            load(m, w_in[0, :, m * P:(m + 1) * P], P)
        sp.wait_ge(t_free, TU_Q)
        sp.dma_start(wgu[:], w_gate[0]).then_inc(wgu_in, 16)
        for u in range(2):
            load_p(G_V + 4 * u, w_in[0, :, 1024:2048], u)
        n = 0
        for u in range(2):
            load_p(G_R + 4 * u, w_in[0, :, 2048:3072], u)
        for u in range(2):
            if u == 1:
                load_p(G_O, w_o_a[0], 0)
            for t in range(TILES):
                sp.wait_ge(ro_done, n + 1)
                sp.dma_start(gate_scr[t, :, u * 512:(u + 1) * 512], sio[:, n % 2, :]).then_inc(r_out[n % 2], 16)
                n += 1
        sp.wait_ge(g_full, GU_O)
        for b in range(STREAMS):
            sp.dma_start(Ss[:, b], state_gla[0, b].rearrange("h k v -> k h v")).then_inc(ss_in, 16)
        sp.wait_ge(s_upd, 2 * PT * H_A)
        sp.dma_start(gla_prompt[0, 0].rearrange("h k v -> k h v"), S[:, 0]).then_inc(st_out, 16)
        for b in range(STREAMS):
            sp.wait_ge(Ss_done, 2 * (b + 1))
            sp.dma_start(gla_sample[0, b].rearrange("h k v -> k h v"), Ss[:, b]).then_inc(st_out, 16)
        for n2 in range(2):
            sp.wait_ge(r_out[n2], 16 * TILES)
        for t in range(TILES):
            if t >= 2:
                sp.wait_ge(gated, t - 1)
            else:
                sp.wait_ge(ro_done, 2 * TILES)
            sp.dma_start(rin[:, t % 2, :], gate_scr[t]).then_inc(r_back[t % 2], 16)
        sp.wait_ge(st_out, 16 * (1 + STREAMS))
        sp.wait_ge(g_free, GU_O)
        def norm_params(n):
            if n:
                sp.wait_ge(ln_done, TILES * n)
            for i, w in enumerate((ln_g, ln_b)):
                sp.dma_start(lng[:, i, :], w[n // 2, n % 2:n % 2 + 1, :].broadcast_to([P, D])).then_inc(lng_in, 16)

        def mlp_loads(lay, c):
            if isinstance(c, int):
                col, row = w_up[lay, :, c * FC:(c + 1) * FC], w_down[lay, c * FC:(c + 1) * FC, :]
            else:
                col, row = w_up[lay, :, bass.ds(c * FC, FC)], w_down[lay, bass.ds(c * FC, FC), :]
            for j in range(8):
                if j < 4:
                    src, n = col[:, j * P:(j + 1) * P], P
                else:
                    nh, kp = divmod(j - 4, 2)
                    src, n = row[kp * 256:(kp + 1) * 256, nh * 512:(nh + 1) * 512], 512
                sp.wait_ge(lo_done, 8 * c + (G_MLP[lay] + j - 3))
                sp.dma_start(raw[:, j % 4, :].rearrange("p (k n) -> p k n", n=n),
                             src.rearrange("(k p) n -> p k n", p=P)).then_inc(raw_in[j % 4], 16)

        sp.wait_ge(Ss_done, 2 * STREAMS)
        for t in range(TILES):
            sp.dma_start(X[:, t, :], x_scr[t]).then_inc(x_res_in, 16)
        sp.wait_ge(gated, TILES)
        norm_params(0)
        load_p(G_O + 4, w_o_a[0], 1)
        mlp_loads(0, 0)
        norm_params(1)
        with sp.Fori(1, NFC - 1) as c:
            mlp_loads(0, c)
        mlp_loads(0, NFC - 1)
        def pair_in(i):
            h, mat, part = i // 4, i % 4 // 2, i % 2
            src = k_prompt[0].rearrange("(t p) h c d -> p t h c d", p=P)[:, :, h] if mat == 0 else \
                q_scr[0:PT].rearrange("t p (h c d) -> p t h c d", h=H_B, c=2)[:, :, h]
            if i >= 2:
                sp.wait_ge(p_full, 2 * i - 2)
            for dup in range(2):
                for t in range(4):
                    sp.dma_start(kqd[:, i % 2, t, :, dup, :], src[:, 4 * part + t]).then_inc(h_kq[i % 2], 16)

        n = 0
        for u in range(6):
            w, col = (w_kv, u * 512) if u < 4 else (w_q[0], (u - 4) * 512)
            load_p(G_KVQ + 4 * u, w[:, col:col + 512], 0)
            if u:
                for t in range(TILES):
                    sp.wait_ge(kv_done, n + 1)
                    sp.dma_start(kv_dst[(u - 1) // 2][t][:, (u - 1) % 2 * 512:(u - 1) % 2 * 512 + 512],
                                 kvs[:, n % 6, :]).then_inc(kv_out[n % 6], 16)
                    n += 1
        load_p(G_O2, w_o_b[0], 0)
        sp.wait_ge(ln_done, 2 * TILES)
        for i in range(6):
            sp.wait_ge(kv_out[i], 16 * 2 * TILES // 6)
        pair_in(0)
        pair_in(1)
        sp.dma_start(lamt[:], lam[0:1].broadcast_to([P, 4, HD])).then_inc(lam_in, 16)
        sp.dma_start(gnb[:], g_norm_b[0:1, :].broadcast_to([P, VD])).then_inc(gnb_in, 16)
        for t in range(TILES):
            sp.wait_ge(kv_done, n + 1)
            sp.dma_start(kv_dst[2][t][:, 512:1024], kvs[:, n % 6, :]).then_inc(kv_out[n % 6], 16)
            n += 1
        for i in range(6):
            sp.wait_ge(kv_out[i], 16 * TILES)

        def values_in(h):
            if h >= 3:
                sp.wait_ge(o_full, PT * (h - 2))
            sp.dma_start(vhead[:, h % 3], v_prompt[0].rearrange("(t p) h v -> p t h v", p=P)[:, :, h]).then_inc(h_v[h % 3], 16)

        def out_o(s):
            sp.wait_ge(ob_done, s + 1)
            h, i = s // PT, s % PT
            sp.dma_start(o_scr[i, :, h * P:(h + 1) * P], osb[:, s % 2, :]).then_inc(o_out[s % 2], 16)

        pair_in(2)
        pair_in(3)
        sp.wait_ge(g_full, GU_O2)
        values_in(0)
        pair_in(4)
        values_in(1)
        pair_in(5)
        pair_in(6)
        values_in(2)
        def keys_in(b):
            if b >= 2:
                sp.wait_ge(k_tr, 8 * (b - 1))
            sp.dma_start(Kc[:, b % 2], cache_k[b].rearrange("(t p) h c d -> p t (h c d)", p=P)).then_inc(kc_in[b % 2], 16)

        def cached_values_in(b):
            if b >= 2:
                sp.wait_ge(s2_pv, 2 * (b - 1))
            sp.dma_start(Vc[:, b % 2], cache_v[b].rearrange("(t p) h v -> p t (h v)", p=P)).then_inc(vc_in[b % 2], 16)

        for s in range(STEPS):
            if s % 2 == 0 and 7 + s // 2 < 4 * H_B:
                pair_in(7 + s // 2)
            if s % PT == PT - 1 and s // PT + 3 < H_B:
                values_in(s // PT + 3)
            if s == PT:
                sp.wait_ge(lo_done, G_O2 + 4)
                for i, src in enumerate((kv_dst[0][PT], q_scr[PT])):
                    sp.dma_start(kqS[:, i, :], src).then_inc(S_in, 16)
            if s == STEPS - PT:
                sp.wait_ge(p_full, 8 * H_B)
                sp.wait_ge(s_full, 2 * (STEPS - PT))
                keys_in(0)
            out_o(s)

        sp.wait_ge(o_full, STEPS)
        keys_in(1)
        sp.dma_start(vS[:], kv_dst[1][PT]).then_inc(vS_in, 16)
        cached_values_in(0)

        def sample_out(b):
            sp.wait_ge(s2_fin, 2 * (b + 1))
            dst = o_scr[PT, b * SEQ_S:(b + 1) * SEQ_S, :].rearrange("q (z h v) -> q z h v", z=2, h=4)
            for hh in range(4):
                sp.dma_start(dst[:, :, hh], oW[32 * hh:32 * hh + SEQ_S, 2 * b:2 * b + 2, :]).then_inc(s2_out, 16)

        for b in range(1, STREAMS):
            if b + 1 < STREAMS:
                keys_in(b + 1)
            cached_values_in(b)
            if b >= 3:
                sample_out(b - 3)
        for b in range(STREAMS - 3, STREAMS - 1):
            sample_out(b)
        for i in range(2):
            sp.wait_ge(o_out[i], 16 * H_B * PT // 2)
        sp.wait_ge(s2_full, 2 * STREAMS)
        for t in range(PT):
            if t == 6:
                sp.wait_ge(s2_pv, 2 * STREAMS)
            sp.dma_start(oin[:, t, :], o_scr[t]).then_inc(tile_in[t], 16)
        sample_out(STREAMS - 1)
        sp.wait_ge(s2_out, 64 * STREAMS)
        sp.dma_start(oS[:], o_scr[PT]).then_inc(tile_in[PT], 16)
        load_p(G_O2 + 4, w_o_b[0], 1)
        sp.wait_ge(t_free, TU_O2 + 2 * TILES)
        norm_params(2)
        mlp_loads(1, 0)
        norm_params(3)
        with sp.Fori(1, NFC - 1) as c:
            mlp_loads(1, c)
        mlp_loads(1, NFC - 1)
        for t in range(TILES):
            sp.wait_ge(ln_done, 3 * TILES + t + 1)
            sp.dma_start(y_dst[t], X[:, t, :]).then_inc(y_out, 16)
        sp.wait_ge(y_out, 16 * TILES)

    @block.gpsimd
    def _(pool):
        def split_lo(g, slot=None):
            slot = g % 4 if slot is None else slot
            pool.wait_ge(hi_done, g + 1)
            nc.gpsimd.tensor_tensor(wsplit[:, slot, 1, :], raw[:, slot, :],
                                    wsplit[:, slot, 0, :].bitcast(F32), ALU.subtract).then_inc(lo_done, 1)

        def power(p):
            pool.wait_ge(o_ms, p + 1)
            nc.gpsimd.tensor_tensor(rs4[:, p % 4, :], ms[:, p % 4, :], cst[:, C_NH:C_NH + 2],
                                    ALU.pow).then_inc(o_rs, 1)

        pool.wait_ge(c_in, 16)
        for g in range(4):
            split_lo(g)
        pool.wait_ge(gl_hi, 1)
        nc.gpsimd.tensor_tensor(wgls[:, 1], wglr[:], wgls[:, 0].bitcast(F32), ALU.subtract).then_inc(gl_lo, 1)
        for g in range(4, G_O + 4):
            split_lo(g)
        for p in range(2 * PT + 2):
            power(p)

        def rstds(n, grp):
            for i in range(n * TILES + grp * GROUP, n * TILES + (grp + 1) * GROUP):
                pool.wait_ge(ln_var, i + 1)
                nc.gpsimd.tensor_tensor(rstd[:, i % 3:i % 3 + 1], mv[:, i % 3, 1:2], cst[:, C_NH:C_NH + 1],
                                        ALU.pow).then_inc(ln_rstd, 1)

        def gain(n, t):
            pool.wait_ge(ln_norm, n * TILES + t + 1)
            if t == 0:
                pool.wait_ge(lng_in, 32 * (n + 1))
            nc.gpsimd.tensor_tensor(X[:, t, :], X[:, t, :], lng[:, 0, :], ALU.mult).then_inc(ln_gain, 1)

        def norm(n, grp):
            rstds(n, grp)
            for t in range(grp * GROUP, (grp + 1) * GROUP):
                gain(n, t)

        def product_norm(n, g):
            norm(n, 0)
            rstds(n, 1)
            for j in range(4):
                split_lo(g + 4 + j)
                if j < GROUP:
                    gain(n, GROUP + j)
            norm(n, 2)

        def mlp(lay):
            g = G_MLP[lay]
            for j in range(4, 8):
                split_lo(g + j)
            with pool.Fori(1, NFC - 1) as c:
                for j in range(8):
                    split_lo(8 * c + (g + j), slot=j % 4)
            for j in range(8 * (NFC - 1), 8 * NFC):
                split_lo(g + j)
            norm(2 * lay + 1, 0)
            rstds(2 * lay + 1, 1)
            for j in range(4):
                if j < GROUP:
                    gain(2 * lay + 1, GROUP + j)
                if lay == 0:
                    split_lo(g + 8 * NFC + j)
            norm(2 * lay + 1, 2)

        for j in range(4):
            split_lo(G_O + 4 + j)
        product_norm(0, G_O + 4)
        mlp(0)
        for g in range(G_KVQ + 4, G_O2):
            split_lo(g)

        pp = [0]

        def small(fn, *a, done=None):
            ins = fn(*a)
            if done is None:
                pp[0] += 1
                ins.then_inc(att_small, 1)
                pool.wait_ge(att_small, pp[0])
            else:
                ins.then_inc(done, 1)
        tt, ts = nc.gpsimd.tensor_tensor, nc.gpsimd.tensor_scalar

        def balance(s):
            r = s % 4
            pool.wait_ge(ex_done, 2 * s + 2)
            small(tt, rl[:, r, 1:2], ls[:, r, 1:2], neg1[:, 0:1], ALU.pow)
            small(tt, gf[:, r:r + 1], ls[:, r, 0:1], rl[:, r, 1:2], ALU.mult)
            small(tt, gf[:, r:r + 1], gf[:, r:r + 1], nlam, ALU.mult, done=g_done)
            small(tt, rq[:, r:r + 1], ls[:, r, 0:1], ls[:, r, 0:1], ALU.mult)
            small(ts, rq[:, r:r + 1], rq[:, r:r + 1], EPS, None, ALU.mult)

        def factor(s):
            r = s % 4
            pool.wait_ge(osq_done, s + 1)
            small(tt, oms[:, r:r + 1], oss[:, r:r + 1], rq[:, r:r + 1], ALU.add)
            small(tt, of[:, r:r + 1], oms[:, r:r + 1], cst[:, C_NH:C_NH + 1], ALU.pow, done=f_done)

        pool.wait_ge(nl_done, 1)
        for s in range(STEPS + 2):
            if s < STEPS:
                balance(s)
            if s >= 2:
                factor(s - 2)
            if 2 <= s < 6:
                split_lo(G_O2 + s - 2)

        pool.wait_ge(att_done, 1)
        nc.gpsimd.memset(Qbd[:], 0.0).then_inc(S_z, 1)
        nc.gpsimd.memset(PS[:, :, 512:640], 0.0).then_inc(ps_z, 1)
        pool.wait_ge(S_z, 1)
        pool.wait_ge(ps_z, 1)
        pool.wait_ge(S_cp, 4)

        def queries(b):
            if b >= 2:
                pool.wait_ge(s2_full, 2 * (b - 1))
            for c in range(2):
                for hh in range(4):
                    col = 32 * hh + 16 * c
                    nc.gpsimd.tensor_copy(Qbd[c * HD:(c + 1) * HD, b % 2, hh::4, col:col + 16],
                                          QTs[c * HD:(c + 1) * HD, hh::4, b * 16:b * 16 + 16]).then_inc(S_qb, 1)
                pool.wait_ge(S_qb, 8 * b + 4 * (c + 1))

        def coefficient(w):
            pool.wait_ge(s2_ex, 2 * w + 2)
            r = w % 2
            small(tt, ls[:, r, 0:1], ls[:, r, 0:1], ls[:, r, 1:2], ALU.add)
            small(tt, coef[:, r:r + 1], ls[:, r, 0:1], neg1[:, 0:1], ALU.pow)
            small(tt, coef[:, r:r + 1], coef[:, r:r + 1], sgl, ALU.mult, done=s2_co)

        def clear_new(w):
            pool.wait_ge(s2_at, w - 1)
            nc.gpsimd.memset(PS[:, w % 2, 512:640], 0.0).then_inc(ps_z, 1)
            pool.wait_ge(ps_z, w)

        def sample_rstd(w):
            pool.wait_ge(s2_sq, w + 1)
            small(ts, ssS[:, w:w + 1], ssS[:, w:w + 1], EPS, None, ALU.add)
            small(tt, rsS[:, w:w + 1], ssS[:, w:w + 1], cst[:, C_NH:C_NH + 1], ALU.pow, done=s2_rs)

        queries(0)
        queries(1)
        coefficient(0)
        for w in range(2 * STREAMS + 2):
            if 1 <= w < 2 * STREAMS - 1:
                clear_new(w + 1)
            if w < 2 * STREAMS - 1:
                coefficient(w + 1)
            if w % 2 and (w + 3) // 2 < STREAMS:
                queries((w + 3) // 2)
            if w >= 2:
                sample_rstd(w - 2)
        for j in range(4):
            split_lo(G_O2 + 4 + j)
        product_norm(2, G_O2 + 4)
        mlp(1)

    @block.scalar
    def _(act):
        def split_hi_of(slot, loads, free):
            act.wait_ge(raw_in[slot], 16 * loads)
            if free:
                act.wait_ge(*free)
            nc.scalar.activation(wsplit[:, slot, 0, :], raw[:, slot, :], ACT.Copy).then_inc(hi_done, 1)

        def split_hi(g):
            split_hi_of(g % 4, g // 4 + 1, QUARTER_FREE[g - 4] if g >= 4 else None)

        def transposed_hi(u, xt, t, half):
            act.wait_ge(t_full, u + 1)
            nc.scalar.activation(xt[:, 0, 4 * half:4 * half + 4, t * P:(t + 1) * P],
                                 ps[:, 6 + u % 2, :].rearrange("p (k n) -> p k n", n=P),
                                 ACT.Copy).then_inc(t_hi, 1)

        for t in range(TILES):
            for half in range(2):
                transposed_hi(TU_X0 + 2 * t + half, XTR[0], t, half)
            if t and t % 2 == 0:
                split_hi(t // 2 - 1)
        act.wait_ge(gl_raw, 16)
        nc.scalar.activation(wgls[:, 0], wglr[:], ACT.Copy).then_inc(gl_hi, 1)
        act.wait_ge(c_in, 16)
        act.wait_ge(bg_in, 16)
        nc.scalar.mul(nbg, bg, -1.0).then_inc(la_done, 1)
        for g in range(4, 12):
            split_hi(g)
        for step in range(24):
            if step in LOG_AT:
                i = step // 2
                act.wait_ge(m_done, 2 * i + 2)
                if i == 0:
                    act.wait_ge(la_done, 1)
                h = LOG_AT[step][0]
                nc.scalar.activation(gna[:], gna[:], ACT.Exp, bias=nbg[:, h:h + 1]).then_inc(e_read, 1)
                act.wait_ge(e_read, i + 1)
                nc.scalar.activation(gna[:], gna[:], ACT.Ln, bias=1.0).then_inc(lg_done, 1)
                act.wait_ge(b_done, i + 1)
                if i:
                    act.wait_ge(qk_done, 3 * i)
                nc.scalar.activation(geb[:], gb[:], ACT.Exp, scale=1.0 / 16).then_inc(eb_done, 1)
                nc.scalar.activation(genb[:], gb[:], ACT.Exp, scale=-1.0 / 16).then_inc(eb_done, 1)
            if step % 12 >= 8:
                split_hi(12 + 4 * (step // 12) + step % 12 - 8)
        def exp_r(n):
            use = GU_R + n
            act.wait_ge(g_full, use + 1)
            if n >= 2:
                act.wait_ge(ro_done, n - 1)
            nc.scalar.activation(sie[:, n % 2, :], ps[:, use % 6, :], ACT.Exp, scale=-1.0).then_inc(re_done, 1)

        for u in range(2):
            for n in range(2 * GROUP):
                exp_r(u * TILES + n)
            for j in range(3):
                split_hi(G_R + 4 * u + 4 + j)
            for n in range(2 * GROUP, TILES):
                if n == TILES - 1:
                    split_hi(G_R + 4 * u + 7)
                exp_r(u * TILES + n)

        def decayed(s):
            t, h = s // H_A, s % H_A
            if s >= 2:
                act.wait_ge(pe_kt, s - 1)
            for c in range(2):
                last = nc.scalar.mul(ktT[:, s % 2, c * CH:(c + 1) * CH],
                                     qkT[:, 1, h, t * P + c * CH:t * P + (c + 1) * CH],
                                     elast[:, h, 2 * t + c:2 * t + c + 1])
            last.then_inc(kt_pre, 1)

        def to_tokens(s):
            act.wait_ge(pe_kt, s + 1)
            if s >= 2:
                act.wait_ge(pe_kv, 2 * (s - 1))
            nc.scalar.activation(kts[:, s % 2, :], ps[:, 0, 0:P], ACT.Copy).then_inc(kt_tok, 1)

        def squares(p):
            t, hp = p // 2, p % 2
            act.wait_ge(pe_o, 4 * t + 2 * hp + 2)
            if p >= 4:
                act.wait_ge(o_ms, p - 3)
            for k in range(2):
                if p or k:
                    act.wait_ge(o_sq, 2 * p + k)
                nc.scalar.activation(sq[:, k, :], ps[:, 4 + 2 * (t % 2) + hp, k * DV:(k + 1) * DV],
                                     ACT.Square, accum_out=ss[:, p % 4, k:k + 1]).then_inc(o_sq, 1)

        act.wait_ge(qk_done, 3 * H_A * NG)
        act.wait_ge(g_full, GU_O)
        steps = PT * H_A
        decayed(0)
        decayed(1)
        to_tokens(0)
        for s in range(steps):
            if s + 2 < steps:
                decayed(s + 2)
            if s + 1 < steps:
                to_tokens(s + 1)
            if s % 2 == 1:
                squares(s // 2)
        act.wait_ge(peS_kt, 4)
        for b in range(STREAMS):
            last = nc.scalar.mul(ktb[:, b, :], ps[:, 0, :], cst[:, C_ROW + b:C_ROW + b + 1])
        last.then_inc(ktb_done, 1)
        act.wait_ge(peS_oT, 1)
        for i in range(2):
            last = nc.scalar.activation(oT[:, 4 * i:4 * i + 4, :],
                                        ps[:, 4 + i, :].rearrange("p (k n) -> p k n", n=P), ACT.Copy)
        last.then_inc(oT_done, 1)
        for p in (2 * PT, 2 * PT + 1):
            act.wait_ge(pe_o, 4 * PT + 2 * (p - 2 * PT) + 2)
            act.wait_ge(o_ms, p - 3)
            for k in range(2):
                act.wait_ge(o_sq, 2 * p + k)
                nc.scalar.activation(sq[:, k, :], ps[:, 6 + p - 2 * PT, k * DV:(k + 1) * DV],
                                     ACT.Square, accum_out=ss[:, p % 4, k:k + 1]).then_inc(o_sq, 1)
        act.wait_ge(Ss_done, 2 * STREAMS)
        act.wait_ge(st_out, 16 * (1 + STREAMS))
        for t in range(TILES):
            for half in range(2):
                transposed_hi(TU_O1 + 2 * t + half, XTR[1], t, half)

        def norm(n, grp, between=None, after=None):
            for t in range(grp * GROUP, (grp + 1) * GROUP):
                i = n * TILES + t
                if between:
                    between(t - grp * GROUP)
                act.wait_ge(ln_nmr, i + 1)
                nc.scalar.activation(X[:, t, :], X[:, t, :], ACT.Identity, bias=nmr[:, i % 3:i % 3 + 1],
                                     scale=rstd[:, i % 3:i % 3 + 1]).then_inc(ln_norm, 1)
                if after:
                    after(t - grp * GROUP)

        def hidden(n, m, ng, slot):
            act.wait_ge(up_r, n + 1)
            nc.scalar.activation(hsq[:, slot, :], hsq[:, slot, :], ACT.Square).then_inc(up_sq, 1)
            act.wait_ge(up_sq, n + 1)
            nc.scalar.activation(hT[:, 0, m, ng * GW:(ng + 1) * GW], hsq[:, slot, :], ACT.Copy).then_inc(up_h, 1)

        def residual_norm(lay, g):
            n = 2 * lay
            norm(n, 0)
            k = 0
            for i, (u, kind, p, q) in enumerate(after_norm(lay)):
                if i == 2 * GROUP:
                    norm(n, 1, between=lambda j: split_hi(g + 4 + j))
                    split_hi(g + 4 + GROUP)
                if kind == "tr":
                    transposed_hi(u, XTR[2 if lay == 0 else 4], p, q)
                    if (p, q) == (2 * GROUP - 1, 1):
                        norm(n, 2)
                else:
                    hidden(UPS * lay + k, p, q, k % 2)
                    k += 1
                    if q == NG - 1:
                        split_hi(G_MLP[lay] + 4 + p)

        def normed_transposes(grp):
            for t in range(grp * GROUP, (grp + 1) * GROUP):
                for half in range(2):
                    transposed_hi(TU_L[1] + 2 * t + half, XTR[3], t, half)

        def mlp(lay):
            g = G_MLP[lay]
            for j in range(8, 12):
                split_hi(g + j)

            def ups(c, free):
                for m in range(4):
                    for ng in range(NG):
                        hidden(12 * c + (UPS * lay + 3 * m + ng), m, ng, (3 * m + ng) % 2)
                    split_hi_of(m, 2 * c + (g // 4 + 2), free(m))
            with act.Fori(1, NFC - 1) as c:
                ups(c, lambda q: chunk_quarter_free(lay, c, q))
                for j in range(4):
                    split_hi_of(j, 2 * c + (g // 4 + 3), chunk_quarter_free(lay, c, 4 + j))
            ups(NFC - 1, lambda q: QUARTER_FREE[g + 8 * (NFC - 1) + q])
            norm(2 * lay + 1, 0)
            if lay == 0:
                norm(1, 1, after=lambda j: split_hi(g + 8 * NFC + j) if j < 2 else None)
                normed_transposes(0)
                for j in (2, 3):
                    split_hi(g + 8 * NFC + j)
            else:
                norm(3, 1)
                norm(3, 2)

        for j in range(4):
            split_hi(G_O + 4 + j)
        residual_norm(0, G_O + 4)
        mlp(0)
        for grp in range(NG):
            if grp == 2:
                norm(1, grp)
            if grp:
                normed_transposes(grp)
        for g in range(G_KVQ + 4, G_O2):
            split_hi(g)

        act.wait_ge(lam_p, 2)
        nc.scalar.activation(lam2, lam2, ACT.Exp).then_inc(lam_e, 1)

        def prepare(i):
            h, j = i // 8, i % 8
            act.wait_ge(p_full, i + 1)
            c, part = j % 2, j % 4 // 2
            if j < 4:
                dst = KD[:, h % 2, 0, c, part * 512:(part + 1) * 512]
            else:
                dst = QS[:, h % 2, c, part * 512:(part + 1) * 512]
            nc.scalar.activation(dst, ps[:, p_bank(i), :], ACT.Copy).then_inc(p_hi, 1)

        def exponentials(s, c):
            w = (s % PT + 1) * P
            act.wait_ge(nmx_done, 2 * s + c + 1)
            if s >= 4 and c == 0:
                bank, _, use = a_banks(s - 4)[-1]
                act.wait_ge(a_full[bank], use + 1)
                act.wait_ge(f_done, s - 3)
            nc.scalar.activation(PR[:, s % 4, c, 0:w], ps[:, 2 * c:2 * c + 2, :].rearrange("p a n -> p (a n)")[:, 0:w],
                                 ACT.Exp, bias=nmx[:, s % 2, c:c + 1], scale=HD ** -0.5,
                                 accum_out=ls[:, s % 4, c:c + 1]).then_inc(ex_done, 1)

        def weights_out(s):
            for bank, tiles, use in a_banks(s):
                if bank == 0:
                    act.wait_ge(a_full[0], use + 1)
                    if s >= 2:
                        act.wait_ge(o_full, s - 1)
                    n = len(tiles)
                    nc.scalar.activation(AT[:, s % 2, tiles[0]:tiles[0] + n, :],
                                         ps[:, 5, 0:n * P].rearrange("p (k n) -> p k n", n=P),
                                         ACT.Copy).then_inc(a_free[0], 1)

        def out_square(s):
            act.wait_ge(o_full, s + 1)
            if s:
                act.wait_ge(osq_done, s)
            if s >= 4:
                act.wait_ge(f_done, s - 3)
            nc.scalar.activation(osq[:], ps[:, 7, 0:P], ACT.Square, scale=VD ** -0.5,
                                 accum_out=oss[:, s % 4:s % 4 + 1]).then_inc(osq_done, 1)
            if s >= 2:
                act.wait_ge(ob_done, s - 1)
            nc.scalar.activation(oraw[:, s % 2, :], ps[:, 7, 0:P], ACT.Copy).then_inc(o_free, 1)

        for i in range(8):
            prepare(i)
        for s in range(-1, STEPS + 2):
            if s + 1 < STEPS:
                exponentials(s + 1, 0)
            if s + 9 < 8 * H_B:
                prepare(s + 9)
            if 0 <= s - 1 < STEPS:
                weights_out(s - 1)
            if s + 1 < STEPS:
                exponentials(s + 1, 1)
            if 0 <= s - 2:
                out_square(s - 2)
            if 0 <= s < 4:
                split_hi(G_O2 + s)

        def exps2(w):
            act.wait_ge(s2_mx, w + 1)
            if w < 2:
                act.wait_ge(ps_z, 1)
            else:
                act.wait_ge(s2_at, w - 1)
                act.wait_ge(ps_z, w)
                act.wait_ge(s2_co, w - 1)
            b = w // 2
            nc.scalar.activation(PS[:, w % 2, 0:512], ps[:, w % 2, :], ACT.Exp, bias=nmx[:, w % 2, 0:1],
                                 scale=HD ** -0.5, accum_out=ls[:, w % 2, 0:1]).then_inc(s2_ex, 1)
            nc.scalar.activation(PS[:, w % 2, 512 + 16 * b:528 + 16 * b], ps[:, 2, 0:16], ACT.Exp,
                                 bias=nmx[:, w % 2, 0:1], scale=HD ** -0.5,
                                 accum_out=ls[:, w % 2, 1:2]).then_inc(s2_ex, 1)

        def weights2(w):
            act.wait_ge(s2_at, w + 1)
            if w >= 2:
                act.wait_ge(s2_pv, w - 1)
            nc.scalar.activation(ATs[:, w % 2, 0:4, :], ps[:, 6, :].rearrange("p (k n) -> p k n", k=4), ACT.Copy)
            nc.scalar.activation(ATs[:, w % 2, 4, :], ps[:, 3, 0:P], ACT.Copy).then_inc(s2_atc, 1)

        def sample_square(w):
            act.wait_ge(s2_ot, w + 1)
            if w == 0:
                for i in range(2):
                    act.wait_ge(o_out[i], 16 * STEPS // 2)
            if w:
                act.wait_ge(s2_sq, w)
            nc.scalar.activation(sqS[:], oW[:, w, :], ACT.Square, scale=VD ** -0.5,
                                 accum_out=ssS[:, w:w + 1]).then_inc(s2_sq, 1)

        def cache_keys(w):
            for hh in (0, 2):
                act.wait_ge(k_tr, 4 * w + hh + 1)
                if w >= 2:
                    act.wait_ge(s2_full, w - 1)
                nc.scalar.activation(KTb[:, w % 2, hh, :], ps[:, 4, :], ACT.Copy).then_inc(k_ev0, 1)

        act.wait_ge(S_cp, 4)
        cache_keys(0)
        cache_keys(1)
        exps2(0)
        for w in range(2 * STREAMS):
            if w + 2 < 2 * STREAMS:
                cache_keys(w + 2)
            if w + 1 < 2 * STREAMS:
                exps2(w + 1)
            weights2(w)
            if w >= 2:
                sample_square(w - 2)
        for w in (2 * STREAMS - 2, 2 * STREAMS - 1):
            sample_square(w)
        for t in range(TILES):
            for half in range(2):
                transposed_hi(TU_O2 + 2 * t + half, XTR[0], t, half)
        for j in range(4):
            split_hi(G_O2 + 4 + j)
        residual_norm(1, G_O2 + 4)
        mlp(1)

    @block.tensor
    def _(pe):
        tf = [0]

        def t_bank(u, bank=None):
            if bank is not None:
                pe.wait_ge(t_free, u - 1)
                return bank
            if u >= 2:
                pe.wait_ge(t_free, u - 1)
            return 6 + u % 2

        def transposes(u, src, t, half):
            b = t_bank(u)
            for k in range(4):
                last = nc.tensor.transpose(ps[:, b, k * P:(k + 1) * P],
                                           src[:, t, (4 * half + k) * P:(4 * half + k + 1) * P], ident)
            last.then_inc(t_full, 1)

        def quarter_cols(g, u, xt, ng, M=P, w=None, bank=None):
            b = t_bank(u, bank)
            for k in range(KT):
                for i, (a, c) in enumerate(PASSES):
                    st = wsplit[:, g % 4, a, k * P:(k + 1) * P] if w is None else w[:, a, k, :]
                    last = nc.tensor.matmul(ps[0:M, b, 0:GW], st, xt[:, c, k, ng * GW:(ng + 1) * GW],
                                            start=(k == 0 and i == 0), stop=(k == KT - 1 and i == 2))
            last.then_inc(t_full, 1)

        def product(g, use, xt, before=None):
            for grp in range(NG):
                for j in range(4):
                    if before:
                        before(4 * grp + j)
                    pe.wait_ge(lo_done, g + j + 1)
                    for t in range(GROUP):
                        u = use + grp * GROUP + t
                        if j == 0 and u >= 6:
                            pe.wait_ge(g_free, u - 5)
                        tok = (grp * GROUP + t) * P
                        for k in range(2):
                            for i, (a, c) in enumerate(PASSES):
                                last = nc.tensor.matmul(
                                    ps[:, u % 6, :], xt[:, a, 2 * j + k, tok:tok + P],
                                    wsplit[:, (g + j) % 4, c, k * 512:(k + 1) * 512],
                                    start=(j == 0 and k == 0 and i == 0), stop=(j == 3 and k == 1 and i == 2))
                        if j == 3:
                            last.then_inc(g_full, 1)
                    if grp == NG - 1 and j < 3:
                        last.then_inc(w_used, 1)

        pe.wait_ge(c_in, 16)
        for t in range(TILES):
            pe.wait_ge(tile_in[t], 16)
            for half in range(2):
                transposes(TU_X0 + 2 * t + half, xin, t, half)
        pe.wait_ge(t_free, TU_GL)
        pe.wait_ge(gl_lo, 1)
        for ng in range(NG):
            quarter_cols(0, TU_GL + ng, XTR[0], ng, M=16, w=wgls)
        for m in range(8):
            pe.wait_ge(lo_done, m + 1)
            for ng in range(NG):
                quarter_cols(m, TU_Q + 3 * m + ng, XTR[0], ng)

        def logits(v_step):
            def f(step):
                step += 12 * v_step
                if step not in LOG_AT:
                    return
                h, ng = LOG_AT[step]
                u = TU_LOG + step // 2
                b = t_bank(u)
                if step == 0:
                    pe.wait_ge(wgu_in, 16)
                nc.tensor.matmul(ps[:, b, 0:GW], wgu[:, h * DK:(h + 1) * DK], glT[ng],
                                 start=True, stop=True).then_inc(t_full, 1)
            return f
        for u in range(2):
            product(G_V + 4 * u, GU_V + TILES * u, XTR[0], before=logits(u))
        for u in range(2):
            product(G_R + 4 * u, GU_R + TILES * u, XTR[0])

        pe.wait_ge(g_free, GU_O)
        pe.wait_ge(t_free, TU_O1)
        pe.wait_ge(qk_done, 3 * H_A * NG)

        def scores(s):
            t, h = s // H_A, s % H_A
            pe.wait_ge(kt_pre, s + 1)
            if s:
                pe.wait_ge(kt_tok, s)
                pe.wait_ge(at_m, s)
            nc.tensor.transpose(ps[:, 0, 0:P], ktT[:, s % 2, :], ident).then_inc(pe_kt, 1)
            nc.tensor.matmul(ps[:, 1, 0:P], qkT[:, 1, h, t * P:(t + 1) * P], qkT[:, 0, h, t * P:(t + 1) * P],
                             start=True, stop=True).then_inc(pe_at, 1)

        def outputs(s):
            t, h = s // H_A, s % H_A
            pe.wait_ge(kt_tok, s + 1)
            for c in range(2):
                if s:
                    pe.wait_ge(s_upd, 2 * (s - 1) + c + 1)
                nc.tensor.matmul(ps[:, 2 + c, 0:DV], kts[c * CH:(c + 1) * CH, s % 2, :],
                                 vO[c * CH:(c + 1) * CH, t, h * DV:(h + 1) * DV],
                                 start=True, stop=True).then_inc(pe_kv, 1)
            pe.wait_ge(at_m, s + 1)
            if t >= 2 and h % 2 == 0:
                pe.wait_ge(o_evac, 2 * (t - 2) + h // 2 + 1)
            o = ps[:, 4 + 2 * (t % 2) + h // 2, (h % 2) * DV:(h % 2 + 1) * DV]
            nc.tensor.matmul(o, attm[:, s % 2, :], vO[:, t, h * DV:(h + 1) * DV], start=True, stop=True)
            q = qkT[:, 0, h, t * P:(t + 1) * P]
            if t:
                pe.wait_ge(s_upd, 2 * (s - 4) + 2)
                nc.tensor.matmul(o[0:CH], q[:, 0:CH], S[:, 0, h, :], start=False, stop=True,
                                 skip_group_check=True).then_inc(pe_i0, 1)
            pe.wait_ge(s_upd, 2 * s + 1)
            nc.tensor.matmul(o[CH:P], q[:, CH:P], S[:, 1, h, :], start=False, stop=True,
                             skip_group_check=True).then_inc(pe_o, 1)

        steps = PT * H_A
        scores(0)
        for s in range(steps):
            if s + 1 < steps:
                scores(s + 1)
            outputs(s)

        pe.wait_ge(ktS_done, 4)
        pe.wait_ge(kt_tok, steps)
        pe.wait_ge(at_m, steps)
        tok = slice(PT * P, TOK)
        for h in range(H_A):
            nc.tensor.transpose(ps[:, 0, h * P:(h + 1) * P], ktS[:, h, :], ident).then_inc(peS_kt, 1)
            last = nc.tensor.matmul(ps[:, 1, h * P:(h + 1) * P], qkT[:, 1, h, tok], qkT[:, 0, h, tok],
                                    start=True, stop=True)
        last.then_inc(peS_at, 1)
        pe.wait_ge(ss_in, 16 * STREAMS)
        pe.wait_ge(o_evac, 2 * PT - 2)
        for i in range(8):
            h, vh = i // 2, i % 2
            for b in range(STREAMS):
                last = nc.tensor.matmul(ps[:, 4 + i // 4, (i % 4) * P + b * 16:(i % 4) * P + b * 16 + 16],
                                        Ss[:, b, h, vh * P:(vh + 1) * P],
                                        qkT[:, 0, h, PT * P + b * 16:PT * P + b * 16 + 16],
                                        start=True, stop=True)
        last.then_inc(peS_oT, 1)
        pe.wait_ge(attS_done, 1)
        pe.wait_ge(oT_done, 1)
        pe.wait_ge(o_evac, 2 * PT)
        for h in range(H_A):
            o = ps[:, 6 + h // 2, (h % 2) * DV:(h % 2 + 1) * DV]
            nc.tensor.matmul(o, attS[:, h, :], vO[:, PT, h * DV:(h + 1) * DV], start=True, stop=True)
            for vh in range(2):
                last = nc.tensor.matmul(o[:, vh * P:(vh + 1) * P], oT[:, 2 * h + vh, :], ident,
                                        start=False, stop=True, skip_group_check=True)
            last.then_inc(pe_o, 1)
        pe.wait_ge(ktb_done, 1)
        for b in range(STREAMS):
            for hp in range(2):
                i = 2 * b + hp
                if i >= 4:
                    pe.wait_ge(Ss_done, i - 3)
                for k in range(2):
                    h = 2 * hp + k
                    last = nc.tensor.matmul(ps[:, i % 4, k * DV:(k + 1) * DV], ktb[:, b, h * P:(h + 1) * P],
                                            vO[:, PT, h * DV:(h + 1) * DV], start=True, stop=True)
                last.then_inc(peS_kv, 1)
        for t in range(TILES):
            pe.wait_ge(gated, t + 1)
            for half in range(2):
                transposes(TU_O1 + 2 * t + half, vO, t, half)

        def down(g, use, hidden, order, before=None):
            v = 0
            for nh, grp in order:
                if before:
                    before(nh, grp)
                for kp in range(2):
                    q = 2 * nh + kp
                    pe.wait_ge(lo_done, g + q + 1)
                    if nh == 0:
                        pe.wait_ge(up_done, hidden[kp][grp])
                    for t in range(GROUP):
                        if kp == 0:
                            pe.wait_ge(g_free, use + v + t - 5)
                        tok = (grp * GROUP + t) * P
                        for k in range(2):
                            for i, (a, b) in enumerate(PASSES):
                                last = nc.tensor.matmul(
                                    ps[:, (v + t) % 6, :], hT[:, a, 2 * kp + k, tok:tok + P],
                                    wsplit[:, q, b, k * 512:(k + 1) * 512],
                                    start=(kp == 0 and k == 0 and i == 0),
                                    stop=(kp == 1 and k == 1 and i == 2))
                        if kp == 1:
                            last.then_inc(g_full, 1)
                        elif t == GROUP - 1 and grp == NG - 1:
                            last.then_inc(w_used, 1)
                v += GROUP

        def up(u, m, ng, xt, g, bank=None):
            if ng == 0:
                pe.wait_ge(lo_done, g + m + 1)
            quarter_cols(m, u, xt, ng, bank=bank)

        def product_norm(lay, g, use, xt_in, xt_out):
            seq = after_norm(lay)

            def first_group(step):
                if 8 <= step < 11:
                    for u, _, t, half in seq[2 * (step - 8):2 * (step - 8) + 2]:
                        if half == 0:
                            pe.wait_ge(ln_done, 2 * lay * TILES + t + 1)
                        transposes(u, X, t, half)
            product(g, use, xt_in)
            product(g + 4, use + TILES, xt_in, before=first_group)
            for u, kind, p, q in seq[2 * GROUP:]:
                if kind == "tr":
                    if q == 0:
                        pe.wait_ge(ln_done, 2 * lay * TILES + p + 1)
                    transposes(u, X, p, q)
                else:
                    if p == 0:
                        pe.wait_ge(t_free, max(e[0] for e in seq if e[1] == "tr" and e[2] // GROUP == q) + 1)
                    up(u, p, q, xt_out, G_MLP[lay])

        def normed_transposes(grp):
            for t in range(grp * GROUP, (grp + 1) * GROUP):
                pe.wait_ge(ln_done, TILES + t + 1)
                for half in range(2):
                    transposes(TU_L[1] + 2 * t + half, X, t, half)

        def mlp(lay, xt):
            g = G_MLP[lay]
            first = [[UPS * lay + FIRST_UP.index((2 * kp + 1, grp)) + 1 for grp in range(NG)] for kp in range(2)]
            down(g + 4, GU_MLP[lay], first, DOWN_ORDER[0])

            def first_group(nh, grp):
                if lay == 0 and (nh, grp) == (1, NG - 1):
                    normed_transposes(0)

            def chunk(c, order, before=None):
                for m in range(4):
                    for ng in range(NG):
                        k = 3 * m + ng
                        up(12 * c + (TU_UP[lay] + k), m, ng, xt, 8 * c + g, bank=6 + (TU_UP[lay] + k) % 2)
                hidden = [[12 * c + (UPS * lay + n + grp) for grp in range(NG)] for n in (4, 10)]
                down(8 * c + (g + 4), 2 * TILES * c + GU_MLP[lay], hidden, order, before)
            with pe.Fori(1, NFC - 1) as c:
                chunk(c, DOWN_ORDER[0])
            chunk(NFC - 1, DOWN_ORDER[1], first_group)

        pe.wait_ge(t_free, TU_O1 + 2 * TILES)
        product_norm(0, G_O, GU_O, XTR[1], XTR[2])
        mlp(0, XTR[2])
        def next_group(step):
            if step % 4 == 0:
                grp = step // 4
                if grp:
                    normed_transposes(grp)
                pe.wait_ge(t_free, TU_L[1] + 2 * GROUP * (grp + 1))
        for u in range(6):
            product(G_KVQ + 4 * u, GU_KVQ + TILES * u, XTR[3], before=next_group if u == 0 else None)

        pe.wait_ge(g_free, GU_O2)
        pe.wait_ge(t_free, TU_O2)

        def prepare(i):
            h, j = i // 8, i % 8
            pair = 4 * h + j // 2
            if j % 2 == 0:
                pe.wait_ge(h_kq[pair % 2], 128 * (pair // 2 + 1))
            if i >= 4:
                pe.wait_ge(p_free, i if i >= 8 else i - 3)
            for k in range(4):
                last = nc.tensor.transpose(ps[:, p_bank(i), k * P:(k + 1) * P],
                                           kqd[:, pair % 2, k, j % 2].rearrange("p a d -> p (a d)"), ident)
            last.then_inc(p_full, 1)

        def scores(s, c):
            h, i = s // PT, s % PT
            w = (i + 1) * P
            if i in (0, 4):
                pe.wait_ge(p_free, 8 * h + (6 if i == 0 else 8))
            if s:
                pe.wait_ge(ex_done, 2 * (s - 1) + c + 1)
            for b in range((w + 511) // 512):
                n = min(512, w - 512 * b)
                o = ps[:, 2 * c + b, 0:n]
                q = QS[:, h % 2, c, i * P:(i + 1) * P]
                nc.tensor.matmul(o, q, KD[:, h % 2, 0, c, 512 * b:512 * b + n], start=True, stop=False)
                nc.tensor.matmul(o, q, KD[:, h % 2, 1, c, 512 * b:512 * b + n], start=False, stop=True)
            nc.tensor.matmul(ps[:, 2 * c + b, n - P:n], mrow[:, 0:P], mrow[:, P:2 * P],
                             start=False, stop=True, skip_group_check=True).then_inc(s_full, 1)

        def weights(s):
            pe.wait_ge(cb_done, s + 1)
            for bank, tiles, use in a_banks(s):
                if use:
                    pe.wait_ge(a_free[bank], use)
                for k, kt in enumerate(tiles):
                    last = nc.tensor.transpose(ps[:, 5 + bank, k * P:(k + 1) * P],
                                               PR[:, s % 4, 0, kt * P:(kt + 1) * P], ident)
                last.then_inc(a_full[bank], 1)

        def values(s):
            h, i = s // PT, s % PT
            for bank, _, use in a_banks(s):
                pe.wait_ge(a_free[bank], use + 1)
            if i == 0:
                pe.wait_ge(h_v[h % 3], 16 * (h // 3 + 1))
            if s:
                pe.wait_ge(o_free, s)
            for kt in range(i + 1):
                last = nc.tensor.matmul(ps[:, 7, 0:P], AT[:, s % 2, kt, :], vhead[:, h % 3, kt, :],
                                        start=(kt == 0), stop=(kt == i))
            last.then_inc(o_full, 1)

        pe.wait_ge(mr_in, 16)
        for i in range(8):
            prepare(i)
        for s in range(-1, STEPS + 2):
            if s + 1 < STEPS:
                scores(s + 1, 0)
            if s + 9 < 8 * H_B:
                prepare(s + 9)
            if 0 <= s - 1 < STEPS:
                weights(s - 1)
            if s + 1 < STEPS:
                scores(s + 1, 1)
            if 0 <= s - 2:
                values(s - 2)

        pe.wait_ge(S_in, 32)
        pe.wait_ge(att_done, 1)
        for i in range(2):
            for z in range(2):
                for k in range(4):
                    last = nc.tensor.transpose(ps[:, 2 * i + z, k * P:(k + 1) * P],
                                               kqS[:, i, (4 * z + k) * P:(4 * z + k + 1) * P], ident)
                last.then_inc(S_tr, 1)
        pe.wait_ge(S_cp, 4)

        def cache_keys(w, hh):
            b, z = w // 2, w % 2
            if z == 0 and hh == 0:
                pe.wait_ge(kc_in[b % 2], 16 * (b // 2 + 1))
            ev = (k_ev0, k_ev1)[hh % 2]
            n = 2 * w + hh // 2
            if n:
                pe.wait_ge(ev, n)
            for kt in range(4):
                last = nc.tensor.transpose(ps[:, 4 + hh % 2, kt * P:(kt + 1) * P],
                                           Kc[:, b % 2, kt, (4 * z + hh) * P:(4 * z + hh + 1) * P], ident)
            last.then_inc(k_tr, 1)

        def scores2(w, hh):
            b, z = w // 2, w % 2
            if hh == 0:
                pe.wait_ge(S_qb, 8 * (b + 1))
                pe.wait_ge(k_ev0, 2 * w + 2)
                pe.wait_ge(k_ev1, 2 * w + 2)
                if w >= 2:
                    pe.wait_ge(s2_ex, 2 * w - 2)
            nc.tensor.matmul(ps[:, w % 2, :], Qbd[:, b % 2, 4 * z + hh, :], KTb[:, w % 2, hh, :],
                             start=(hh == 0), stop=(hh == 3))
            if hh == 3:
                if w:
                    pe.wait_ge(s2_ex, 2 * w)
                for hn in range(4):
                    last = nc.tensor.matmul(ps[:, 2, 0:16], Qbd[:, b % 2, 4 * z + hn, :],
                                            KTn[:, 4 * z + hn, 16 * b:16 * b + 16],
                                            start=(hn == 0), stop=(hn == 3))
                last.then_inc(s2_full, 1)

        def weights2(w):
            pe.wait_ge(s2_ex, 2 * w + 2)
            pe.wait_ge(s2_cm, w + 1)
            if w:
                pe.wait_ge(s2_atc, w)
            for kt in range(5):
                o = ps[:, 6, kt * P:(kt + 1) * P] if kt < 4 else ps[:, 3, 0:P]
                last = nc.tensor.matmul(o, PS[:, w % 2, kt * P:(kt + 1) * P],
                                        CM[:, w % 2, :], start=True, stop=True)
            last.then_inc(s2_at, 1)

        def values2(w):
            b, z = w // 2, w % 2
            pe.wait_ge(s2_atc, w + 1)
            if w == 0:
                pe.wait_ge(vS_in, 16)
            if z == 0:
                pe.wait_ge(vc_in[b % 2], 16 * (b // 2 + 1))
            if w:
                pe.wait_ge(s2_ot, w)
            for kt in range(5):
                v = (Vc[:, b % 2, kt, :] if kt < 4 else vS)[:, z * 512:(z + 1) * 512]
                last = nc.tensor.matmul(ps[:, 7, :], ATs[:, w % 2, kt, :], v, start=(kt == 0), stop=(kt == 4))
            last.then_inc(s2_pv, 1)

        for hh in range(4):
            cache_keys(0, hh)
        for w in range(-1, 2 * STREAMS):
            for hh in range(4):
                if w + 2 < 2 * STREAMS:
                    cache_keys(w + 2, hh)
                if w + 1 < 2 * STREAMS:
                    scores2(w + 1, hh)
            if w < 0:
                continue
            weights2(w)
            if w:
                values2(w - 1)
        values2(2 * STREAMS - 1)
        for t in range(TILES):
            for half in range(2):
                u = TU_O2 + 2 * t + half
                if half == 0:
                    pe.wait_ge(tile_in[t], 32)
                if t < PT:
                    transposes(u, oin, t, half)
                else:
                    transposes(u, oS[:].unsqueeze(1), 0, half)
        pe.wait_ge(t_free, TU_O2 + 2 * TILES)
        product_norm(1, G_O2, GU_O2, XTR[0], XTR[4])
        mlp(1, XTR[4])

    @block.vector
    def _(dve):
        def transposed_lo(u, xt, t, half, n_hi):
            dve.wait_ge(t_hi, n_hi)
            dst = slice(t * P, (t + 1) * P)
            nc.vector.tensor_tensor(xt[:, 1, 4 * half:4 * half + 4, dst],
                                    ps[:, 6 + u % 2, :].rearrange("p (k n) -> p k n", n=P),
                                    xt[:, 0, 4 * half:4 * half + 4, dst].bitcast(F32),
                                    ALU.subtract).then_inc(t_free, 1)

        hi = 0
        for t in range(TILES):
            for half in range(2):
                hi += 1
                transposed_lo(TU_X0 + 2 * t + half, XTR[0], t, half, hi)
        for ng in range(NG):
            u = TU_GL + ng
            dve.wait_ge(t_full, u + 1)
            if ng == 0:
                dve.wait_ge(t_free, TU_GL)
            nc.vector.tensor_copy(glT[ng], ps[0:16, 6 + u % 2, 0:GW]).then_inc(t_free, 1)
        for m in range(8):
            for ng in range(NG):
                u = TU_Q + 3 * m + ng
                dve.wait_ge(t_full, u + 1)
                dst = qkT[:, m // 4, m % 4, ng * GW:(ng + 1) * GW]
                if m < 4:
                    nc.vector.tensor_scalar(dst, ps[:, 6 + u % 2, 0:GW], float(DK) ** -0.5, None,
                                            ALU.mult).then_inc(t_free, 1)
                else:
                    nc.vector.tensor_copy(dst, ps[:, 6 + u % 2, 0:GW]).then_inc(t_free, 1)
        chain = 0
        for step in range(24):
            if step in LOG_AT:
                h, ng = LOG_AT[step]
                i = step // 2
                u = TU_LOG + i
                dve.wait_ge(t_full, u + 1)
                if i:
                    dve.wait_ge(b_done, i)
                nc.vector.tensor_scalar(gm[:], ps[:, 6 + u % 2, 0:GW], bg[:, h:h + 1], 0.0, ALU.add,
                                        ALU.min).then_inc(m_done, 1)
                dve.wait_ge(m_done, 2 * i + 1)
                nc.vector.scalar_tensor_tensor(gna[:], gm[:], 2.0, ps[:, 6 + u % 2, 0:GW], ALU.mult,
                                               ALU.subtract).then_inc(m_done, 1)
                dve.wait_ge(m_done, 2 * i + 2)
                dve.sem_inc(t_free, 1)
                dve.wait_ge(lg_done, i + 1)
                nc.vector.tensor_tensor(gm[:], gm[:], gna[:], ALU.subtract).then_inc(sts, 1)
                dve.wait_ge(sts, i + 1)
                if i:
                    dve.wait_ge(eb_done, 2 * i)
                pos, nscan = ng * GW, 0
                while pos < (ng + 1) * GW:
                    w = CH if pos < PT * P else SEQ_S
                    o = pos - ng * GW
                    last = nc.vector.tensor_tensor_scan(gb[:, o:o + w], cst[:, C_ONE:C_ONE + w], gm[:, o:o + w],
                                                        0.0, ALU.mult, ALU.add)
                    pos += w
                last.then_inc(b_done, 1)
                dve.wait_ge(eb_done, 2 * i + 2)
                q = qkT[:, 0, h, ng * GW:(ng + 1) * GW]
                k = qkT[:, 1, h, ng * GW:(ng + 1) * GW]
                nc.vector.tensor_tensor(q, q, geb[:], ALU.mult).then_inc(qk_done, 1)
                nc.vector.tensor_tensor(k, k, genb[:], ALU.mult).then_inc(qk_done, 1)
                if ng < 2:
                    nc.vector.tensor_copy(elast[:, h, 6 * ng:6 * ng + 6], geb[:, CH - 1::CH]).then_inc(qk_done, 1)
                else:
                    nc.vector.tensor_copy(elast[:, h, 12:16], geb[:, CH - 1:4 * CH:CH])
                    nc.vector.tensor_copy(elast[:, h, 16:24], geb[:, 4 * CH + SEQ_S - 1::SEQ_S]).then_inc(qk_done, 1)
            if step % 4 == 3:
                for t in range(GROUP):
                    use = GU_V + (step // 4) * GROUP + t
                    dve.wait_ge(g_full, use + 1)
                    if step == 11 or step == 23:
                        dve.wait_ge(t_full, 0 + TU_LOG + min(H_A * NG, 12))  if 0 else None
                    tile = use % TILES
                    nc.vector.tensor_copy(vO[:, tile, (use // TILES) * 512:(use // TILES + 1) * 512],
                                          ps[:, use % 6, :]).then_inc(g_free, 1)
        def denominator(n):
            dve.wait_ge(re_done, n + 1)
            nc.vector.tensor_scalar(sie[:, n % 2, :], sie[:, n % 2, :], 1.0, None, ALU.add).then_inc(rr_done, 1)

        denominator(0)
        for n in range(2 * TILES):
            use = GU_R + n
            dve.wait_ge(rr_done, n + 1)
            nc.vector.reciprocal(sie[:, n % 2, :], sie[:, n % 2, :]).then_inc(rp_done, 1)
            if n + 1 < 2 * TILES:
                denominator(n + 1)
            dve.wait_ge(rp_done, n + 1)
            if n >= 2:
                dve.wait_ge(r_out[n % 2], 16 * (n // 2))
            nc.vector.tensor_tensor(sio[:, n % 2, :], ps[:, use % 6, :], sie[:, n % 2, :],
                                    ALU.mult).then_inc(ro_done, 1)
            dve.wait_ge(ro_done, n + 1)
            dve.sem_inc(g_free, 1)

        def mask(s):
            dve.wait_ge(pe_at, s + 1)
            if s >= 2:
                dve.wait_ge(pe_o, s - 1)
            nc.vector.tensor_tensor(attm[:, s % 2, :], ps[:, 1, 0:P], cst[:, C_MP:C_MP + P],
                                    ALU.mult).then_inc(at_m, 1)

        def update(s):
            t, h = s // H_A, s % H_A
            dve.wait_ge(pe_kv, 2 * s + 1)
            if t:
                dve.wait_ge(pe_o, s - 3)
                nc.vector.scalar_tensor_tensor(S[:, 1, h, :], S[:, 0, h, :], elast[:, h, 2 * t:2 * t + 1],
                                               ps[:, 2, 0:DV], ALU.mult, ALU.add).then_inc(s_upd, 1)
            else:
                nc.vector.tensor_copy(S[:, 1, h, :], ps[:, 2, 0:DV]).then_inc(s_upd, 1)
            dve.wait_ge(pe_kv, 2 * s + 2)
            dve.wait_ge(s_upd, 2 * s + 1)
            if t:
                dve.wait_ge(pe_i0, s + 1 - H_A)
            nc.vector.scalar_tensor_tensor(S[:, 0, h, :], S[:, 1, h, :], elast[:, h, 2 * t + 1:2 * t + 2],
                                           ps[:, 3, 0:DV], ALU.mult, ALU.add).then_inc(s_upd, 1)

        def mean_square(p):
            dve.wait_ge(o_sq, 2 * p + 2)
            if p >= 4:
                dve.wait_ge(o_rs, p - 3)
            nc.vector.tensor_scalar(ms[:, p % 4, :], ss[:, p % 4, :], 1.0 / DV, EPS, ALU.mult,
                                    ALU.add).then_inc(o_ms, 1)

        def normed(p):
            t, hp = p // 2, p % 2
            dve.wait_ge(o_rs, p + 1)
            if p >= 2 * PT:
                dve.wait_ge(peS_kv, 2 * STREAMS)
            bank = 4 + 2 * (t % 2) + hp if t < PT else 6 + hp
            for k in range(2):
                h = 2 * hp + k
                last = nc.vector.scalar_tensor_tensor(vO[:, t, h * DV:(h + 1) * DV],
                                                      ps[:, bank, k * DV:(k + 1) * DV],
                                                      rs4[:, p % 4, k:k + 1], gna_g[:], ALU.mult, ALU.mult)
            last.then_inc(o_evac, 1)

        dve.wait_ge(qk_done, 3 * H_A * NG)
        dve.wait_ge(g_full, GU_O)
        dve.wait_ge(gna_in, 16)
        for h in range(H_A):
            nc.vector.tensor_tensor(ktS[:, h, :].rearrange("p (b s) -> p b s", b=STREAMS),
                                    qkT[:, 1, h, PT * P:TOK].rearrange("p (b s) -> p b s", b=STREAMS),
                                    elast[:, h, 16:24].unsqueeze(2).broadcast_to([P, STREAMS, SEQ_S]),
                                    ALU.mult).then_inc(ktS_done, 1)
        steps = PT * H_A
        mask(0)
        for s in range(steps):
            if s + 1 < steps:
                mask(s + 1)
            update(s)
            if s >= 2:
                if s % 2 == 0:
                    mean_square(s // 2 - 1)
                else:
                    normed(s // 2 - 1)
        mean_square(steps // 2 - 1)
        normed(steps // 2 - 1)
        dve.wait_ge(peS_at, 1)
        nc.vector.tensor_tensor(attS[:], ps[:, 1, :].rearrange("p (h n) -> p h n", h=H_A),
                                cst[:, C_MS:C_MS + P].unsqueeze(1).broadcast_to([P, H_A, P]),
                                ALU.mult).then_inc(attS_done, 1)
        for p in (2 * PT, 2 * PT + 1):
            mean_square(p)
        dve.wait_ge(peS_oT, 1)
        for b in range(STREAMS):
            for hp in range(2):
                i = 2 * b + hp
                dve.wait_ge(peS_kv, i + 1)
                for k in range(2):
                    h = 2 * hp + k
                    last = nc.vector.scalar_tensor_tensor(Ss[:, b, h, :], Ss[:, b, h, :],
                                                          elast[:, h, 16 + b:17 + b],
                                                          ps[:, i % 4, k * DV:(k + 1) * DV], ALU.mult, ALU.add)
                last.then_inc(Ss_done, 1)
        for p in (2 * PT, 2 * PT + 1):
            normed(p)
        def gate(t):
            dve.wait_ge(r_back[t % 2], 16 * (t // 2 + 1))
            if t == 0:
                dve.wait_ge(o_evac, 2 * TILES)
            nc.vector.tensor_tensor(vO[:, t, :], vO[:, t, :], rin[:, t % 2, :], ALU.mult).then_inc(gated, 1)
        gate(0)
        for t in range(TILES):
            if t + 1 < TILES:
                gate(t + 1)
            for half in range(2):
                hi += 1
                transposed_lo(TU_O1 + 2 * t + half, XTR[1], t, half, hi)

        hi_n = [hi]

        def lo_of(u, xt, t, half):
            hi_n[0] += 1
            transposed_lo(u, xt, t, half, hi_n[0])

        def residual(u, t, nh, scale, bank=None):
            bank = u % 6 if bank is None else bank
            dve.wait_ge(g_full, u + 1)
            x = X[:, t, nh * 512:(nh + 1) * 512]
            if scale is None:
                nc.vector.tensor_tensor(x, x, ps[:, bank, :], ALU.add).then_inc(g_free, 1)
            else:
                nc.vector.scalar_tensor_tensor(x, x, scale, ps[:, bank, :], ALU.mult, ALU.add).then_inc(g_free, 1)

        def tile_stats(i, t, uses):
            dve.wait_ge(g_free, uses)
            for k in range(2):
                nc.vector.bn_stats(bst[:, i % 3, 6 * k:6 * k + 6], X[:, t, k * 512:(k + 1) * 512]).then_inc(ln_st, 1)
            dve.wait_ge(ln_st, 3 * i + 2)
            nc.vector.bn_aggr(mv[:, i % 3, :], bst[:, i % 3, :]).then_inc(ln_st, 1)
            dve.wait_ge(ln_st, 3 * i + 3)
            nc.vector.tensor_scalar(mv[:, i % 3, 1:2], mv[:, i % 3, 1:2], EPS, None, ALU.add).then_inc(ln_var, 1)

        def shift(i):
            dve.wait_ge(ln_rstd, i + 1)
            nc.vector.scalar_tensor_tensor(nmr[:, i % 3:i % 3 + 1], mv[:, i % 3, 0:1], -1.0,
                                           rstd[:, i % 3:i % 3 + 1], ALU.mult, ALU.mult).then_inc(ln_nmr, 1)

        def bias(n, t):
            dve.wait_ge(ln_gain, n * TILES + t + 1)
            nc.vector.tensor_tensor(X[:, t, :], X[:, t, :], lng[:, 1, :], ALU.add).then_inc(ln_done, 1)

        def biases(n, grp):
            for t in range(grp * GROUP, (grp + 1) * GROUP):
                bias(n, t)

        def hidden(n, u, slot, bank, first=False):
            if not first:
                dve.wait_ge(up_done, n - 1)
            dve.wait_ge(t_full, u + 1)
            nc.vector.tensor_scalar(hsq[:, slot, :], ps[:, bank, 0:GW], 0.0, None, ALU.max).then_inc(up_r, 1)
            dve.wait_ge(up_r, n + 1)
            dve.sem_inc(t_free, 1)

        def hidden_lo(n, m, ng, slot):
            dve.wait_ge(up_h, n + 1)
            dst = slice(ng * GW, (ng + 1) * GW)
            nc.vector.tensor_tensor(hT[:, 1, m, dst], hsq[:, slot, :], hT[:, 0, m, dst].bitcast(F32),
                                    ALU.subtract).then_inc(up_done, 1)

        def product_norm(lay, use, xt):
            n = 2 * lay
            for t in range(TILES):
                residual(use + t, t, 0, ALPHA)
            use += TILES
            seq = after_norm(lay)

            def last_products(grp):
                for t in range(grp * GROUP, (grp + 1) * GROUP):
                    residual(use + t, t, 1, ALPHA)
                    tile_stats(n * TILES + t, t, use + t + 1)

            def shifts(grp):
                for t in range(grp * GROUP, (grp + 1) * GROUP):
                    shift(n * TILES + t)
            last_products(0)
            shifts(0)
            biases(n, 0)
            last_products(1)
            shifts(1)
            for u, _, t, half in seq[:2 * GROUP]:
                lo_of(u, xt, t, half)
            last_products(2)
            bias(n, GROUP)
            k, last = 0, None
            for u, kind, p, q in seq[2 * GROUP:]:
                if kind == "tr":
                    if last:
                        hidden_lo(*last)
                        last = None
                    lo_of(u, xt, p, q)
                else:
                    n_up = UPS * lay + k
                    hidden(n_up, u, k % 2, 6 + u % 2, first=n_up < 2)
                    if last:
                        hidden_lo(*last)
                    last = (n_up, p, q, k % 2)
                    if k < 2:
                        bias(n, GROUP + 1 + k)
                    if k == 1:
                        shifts(2)
                    if 3 <= k < 6:
                        bias(n, 2 * GROUP + k - 3)
                    k += 1
            hidden_lo(*last)

        def normed_transposes(grp):
            for t in range(grp * GROUP, (grp + 1) * GROUP):
                for half in range(2):
                    lo_of(TU_L[1] + 2 * t + half, XTR[3], t, half)

        def mlp(lay):
            n = 2 * lay + 1

            def ups(c):
                for k in range(12):
                    n_up = 12 * c + (UPS * lay + k)
                    hidden(n_up, 12 * c + (TU_UP[lay] + k), k % 2, 6 + (TU_UP[lay] + k) % 2)
                    if k:
                        hidden_lo(12 * c + (UPS * lay + k - 1), *divmod(k - 1, NG), (k - 1) % 2)
                hidden_lo(12 * c + (UPS * lay + 11), 3, 2, 1)

            def downs(c, scale=None):
                for v, (nh, t) in enumerate((nh, t) for nh in range(2) for t in range(TILES)):
                    residual(2 * TILES * c + (GU_MLP[lay] + v), t, nh, scale, bank=v % 6)

            def last_downs():
                use = GU_MLP[lay] + 2 * TILES * (NFC - 1)
                for nh, grp in DOWN_ORDER[1]:
                    for t in range(grp * GROUP, (grp + 1) * GROUP):
                        residual(use, t, nh, None)
                        use += 1
                        if nh == 1:
                            tile_stats(n * TILES + t, t, use)
                            if t % GROUP:
                                shift(n * TILES + t - 1)
                    if nh == 1:
                        shift(n * TILES + t)
                    elif grp:
                        if lay == 0 and grp == NG - 1:
                            normed_transposes(0)
                        biases(n, grp - 1)
            downs(0, ALPHA)
            with dve.Fori(1, NFC - 1) as c:
                ups(c)
                downs(c)
            ups(NFC - 1)
            last_downs()

        dve.wait_ge(x_res_in, 16 * TILES)
        product_norm(0, GU_O, XTR[2])
        mlp(0)
        for grp in range(NG):
            if grp == 2:
                biases(1, grp)
            if grp:
                normed_transposes(grp)

        nr = [0]
        for u in range(6):
            for t in range(TILES):
                n = u * TILES + t
                use = GU_KVQ + n
                dve.wait_ge(g_full, use + 1)
                if n >= 6:
                    dve.wait_ge(kv_out[n % 6], 16 * (n // 6))
                if u in (2, 3):
                    nc.vector.tensor_copy(kvs[:, n % 6, :], ps[:, use % 6, :]).then_inc(kv_done, 1)
                    dve.wait_ge(kv_done, n + 1)
                    dve.sem_inc(g_free, 1)
                    continue
                nc.vector.tensor_copy(kvs[:, n % 6, :], ps[:, use % 6, :]).then_inc(g_free, 1)
                dve.wait_ge(g_free, use + 1)
                v = kvs[:, n % 6, :].rearrange("p (g d) -> p g d", d=HD)
                x1, x2 = v[:, :, 0:ROT], v[:, :, ROT:2 * ROT]
                cos = cst[:, C_COS + t * ROT:C_COS + (t + 1) * ROT].unsqueeze(1).broadcast_to([P, 8, ROT])
                sin = cst[:, C_SIN + t * ROT:C_SIN + (t + 1) * ROT].unsqueeze(1).broadcast_to([P, 8, ROT])
                r = [rtmp[:, n % 2, i] for i in range(4)]
                for i, (x, tab) in enumerate(((x1, cos), (x2, sin), (x2, cos), (x1, sin))):
                    nc.vector.tensor_tensor(r[i], x, tab, ALU.mult).then_inc(rope, 1)
                nr[0] += 4
                dve.wait_ge(rope, nr[0])
                nc.vector.tensor_tensor(x1, r[0], r[1], ALU.subtract).then_inc(rope, 1)
                nr[0] += 1
                nc.vector.tensor_tensor(x2, r[2], r[3], ALU.add).then_inc(kv_done, 1)
                dve.wait_ge(rope, nr[0])
                dve.wait_ge(kv_done, n + 1)

        dve.wait_ge(lam_in, 16)
        dve.wait_ge(gnb_in, 16)
        for i in range(2):
            nc.vector.tensor_tensor(lamp[:, i, :], lamt[:, 2 * i, :], lamt[:, 2 * i + 1, :], ALU.mult).then_inc(chain_v, 1)
        dve.wait_ge(chain_v, 2)
        for i in range(2):
            nc.vector.reduce_sum(lam2[:, i:i + 1], lamp[:, i, :], AX.X).then_inc(lam_p, 1)
        nc.vector.tensor_scalar(gnb[:], gnb[:], 1.0 - LAMBDA_INIT, None, ALU.mult).then_inc(chain_v, 1)
        dve.wait_ge(lam_e, 1)
        nc.vector.tensor_tensor(nlam, lam2[:, 1:2], lam2[:, 0:1], ALU.subtract).then_inc(chain_v, 1)
        dve.wait_ge(chain_v, 4)
        nc.vector.tensor_scalar(nlam, nlam, LAMBDA_INIT, None, ALU.subtract).then_inc(chain_v, 1)
        dve.wait_ge(chain_v, 5)
        nc.vector.scalar_tensor_tensor(sgl, cst[:, C_SG + 1:C_SG + 2], nlam, cst[:, C_SG:C_SG + 1],
                                       ALU.mult, ALU.add).then_inc(nl_done, 1)

        def prepare(i):
            h, j = i // 8, i % 8
            dve.wait_ge(p_hi, i + 1)
            c, part = j % 2, j % 4 // 2
            cols = slice(part * 512, (part + 1) * 512)
            if j < 4:
                nc.vector.tensor_tensor(KD[:, h % 2, 1, c, cols], ps[:, p_bank(i), :], KD[:, h % 2, 0, c, cols].bitcast(F32),
                                        ALU.subtract).then_inc(p_free, 1)
            else:
                q = QS[HD:P, h % 2, c, cols]
                nc.vector.tensor_tensor(q, ps[HD:P, p_bank(i), :], q.bitcast(F32), ALU.subtract).then_inc(p_free, 1)

        def maxima(s, c):
            w = (s % PT + 1) * P
            if s >= 2:
                dve.wait_ge(nmx_done, 2 * s - 3 + c)
            dve.wait_ge(s_full, 2 * s + c + 1)
            nc.vector.reduce_max(mx[:, s % 2, c:c + 1], ps[:, 2 * c:2 * c + 2, :].rearrange("p a n -> p (a n)")[:, 0:w],
                                 AX.X).then_inc(mx_done, 1)
            dve.wait_ge(mx_done, 2 * s + c + 1)
            nc.vector.tensor_scalar(nmx[:, s % 2, c:c + 1], mx[:, s % 2, c:c + 1], -float(HD) ** -0.5, None,
                                    ALU.mult).then_inc(nmx_done, 1)

        def combine(s):
            w = (s % PT + 1) * P
            dve.wait_ge(g_done, s + 1)
            dve.wait_ge(ex_done, 2 * s + 2)
            nc.vector.scalar_tensor_tensor(PR[:, s % 4, 0, 0:w], PR[:, s % 4, 1, 0:w], gf[:, s % 4:s % 4 + 1],
                                           PR[:, s % 4, 0, 0:w], ALU.mult, ALU.add).then_inc(cb_done, 1)

        def weights_out(s):
            for bank, tiles, use in a_banks(s):
                if bank == 1:
                    dve.wait_ge(a_full[1], use + 1)
                    if s >= 2:
                        dve.wait_ge(o_full, s - 1)
                    n = len(tiles)
                    nc.vector.tensor_copy(AT[:, s % 2, tiles[0]:tiles[0] + n, :],
                                          ps[:, 6, 0:n * P].rearrange("p (k n) -> p k n", n=P)).then_inc(a_free[1], 1)

        def out_norm(s):
            dve.wait_ge(f_done, s + 1)
            dve.wait_ge(o_free, s + 1)
            if s >= 2:
                dve.wait_ge(o_out[s % 2], 16 * (s // 2))
            nc.vector.scalar_tensor_tensor(osb[:, s % 2, :], oraw[:, s % 2, :], of[:, s % 4:s % 4 + 1], gnb[:],
                                           ALU.mult, ALU.mult).then_inc(ob_done, 1)

        for i in range(8):
            prepare(i)
        for s in range(-1, STEPS + 3):
            if s + 1 < STEPS:
                maxima(s + 1, 0)
            if 0 <= s - 1 < STEPS:
                weights_out(s - 1)
            if s + 1 < STEPS:
                maxima(s + 1, 1)
            if 0 <= s < STEPS:
                combine(s)
            if s + 9 < 8 * H_B:
                prepare(s + 9)
            if 0 <= s - 3:
                out_norm(s - 3)
        dve.wait_ge(ob_done, STEPS)
        dve.sem_inc(att_done, 1)

        for i in range(2):
            for z in range(2):
                dve.wait_ge(S_tr, 2 * i + z + 1)
                dst = (KTn, QTs)[i]
                nc.vector.tensor_copy(dst[:, 4 * z:4 * z + 4, :],
                                      ps[:, 2 * i + z, :].rearrange("p (k n) -> p k n", n=P)).then_inc(S_cp, 1)

        def cache_keys(w, hh):
            dve.wait_ge(k_tr, 4 * w + hh + 1)
            if w >= 2:
                dve.wait_ge(s2_full, w - 1)
            nc.vector.tensor_copy(KTb[:, w % 2, hh, :], ps[:, 5, :]).then_inc(k_ev1, 1)

        def maxima2(w):
            dve.wait_ge(s2_full, w + 1)
            nc.vector.reduce_max(mx[:, w % 2, 0:1], ps[:, w % 2, :], AX.X).then_inc(chain_v, 1)
            nc.vector.reduce_max(mx[:, w % 2, 1:2], ps[:, 2, 0:16], AX.X).then_inc(chain_v, 1)
            dve.wait_ge(chain_v, 5 + 3 * w + 2)
            nc.vector.tensor_tensor(mx[:, w % 2, 0:1], mx[:, w % 2, 0:1], mx[:, w % 2, 1:2], ALU.max).then_inc(chain_v, 1)
            dve.wait_ge(chain_v, 5 + 3 * w + 3)
            nc.vector.tensor_scalar(nmx[:, w % 2, 0:1], mx[:, w % 2, 0:1], -float(HD) ** -0.5, None,
                                    ALU.mult).then_inc(s2_mx, 1)

        def combination(w):
            dve.wait_ge(s2_co, w + 1)
            if w >= 2:
                dve.wait_ge(s2_at, w - 1)
            nc.vector.tensor_scalar(CM[:, w % 2, :], cst[:, C_SEL:C_SEL + P], coef[:, w % 2:w % 2 + 1], None,
                                    ALU.mult).then_inc(s2_cm, 1)

        def outputs2(w):
            dve.wait_ge(s2_pv, w + 1)
            for hh in range(4):
                last = nc.vector.tensor_copy(oW[32 * hh:32 * hh + 32, w, :],
                                             ps[32 * hh:32 * hh + 32, 7, hh * P:(hh + 1) * P])
            last.then_inc(s2_ot, 1)

        def sample_norm(w):
            dve.wait_ge(s2_rs, w + 1)
            nc.vector.scalar_tensor_tensor(oW[:, w, :], oW[:, w, :], rsS[:, w:w + 1], gnb[:],
                                           ALU.mult, ALU.mult).then_inc(s2_fin, 1)

        for hh in (1, 3):
            cache_keys(0, hh)
        for hh in (1, 3):
            cache_keys(1, hh)
        maxima2(0)
        for w in range(2 * STREAMS):
            if w + 2 < 2 * STREAMS:
                cache_keys(w + 2, 1)
            combination(w)
            if w + 2 < 2 * STREAMS:
                cache_keys(w + 2, 3)
            if w + 1 < 2 * STREAMS:
                maxima2(w + 1)
            if w:
                outputs2(w - 1)
            if w >= 3:
                sample_norm(w - 3)
        outputs2(2 * STREAMS - 1)
        for w in range(2 * STREAMS - 3, 2 * STREAMS):
            sample_norm(w)
        for t in range(TILES):
            for half in range(2):
                lo_of(TU_O2 + 2 * t + half, XTR[0], t, half)
        product_norm(1, GU_O2, XTR[4])
        mlp(1)
        biases(3, NG - 1)

    ctx.close()


_INS = ['x_prompt', 'x_sample', 'state_gla', 'cache_k', 'cache_v', 'w_in_a', 'w_gate_up_a', 'b_gate_a',
        'g_norm_a', 'w_o_a', 'w_kv', 'w_q_b', 'lam_b', 'g_norm_b', 'w_o_b', 'w_up', 'w_down', 'ln_g', 'ln_b']
_OUTS = [(1, 1024, 1024), (8, 16, 1024), (1, 1, 4, 128, 256), (1, 1024, 8, 2, 64), (1, 1024, 8, 128),
         (1, 8, 4, 128, 256), (8, 16, 8, 2, 64), (8, 16, 8, 128)]


def kernel(**inputs):
    import concourse.bacc as _bacc
    from concourse.bass_utils import run_bass_kernel_spmd as _run

    nc = _bacc.Bacc("TRN2", target_bir_lowering=False, num_devices=1)
    c, m = constants()
    arrays, args = {}, []
    inputs = dict(inputs, b_gate_a=np.asarray(inputs["b_gate_a"]).reshape(H_A, DK).T)
    for name, a in [(n, np.ascontiguousarray(inputs[n])) for n in _INS] + [("consts", c), ("maskrow", m)]:
        arrays[f"in_{name}"] = a
        args.append(nc.dram_tensor(f"in_{name}", a.shape, mybir.dt.from_np(a.dtype), kind="ExternalInput").ap())
    for i, shape in enumerate(_OUTS):
        args.append(nc.dram_tensor(f"out_{i}", shape, F32, kind="ExternalOutput").ap())
    encoder_step(nc, *args)
    r = _run(nc, [arrays], core_ids=[0])
    return tuple(r.results[0][f"out_{i}"] for i in range(len(_OUTS)))
```

```python
from contextlib import ExitStack

import numpy as np
import concourse.bass as bass
from concourse import mybir

F32 = mybir.dt.float32
F32R = mybir.dt.float32r
ALU = mybir.AluOpType
ACT = mybir.ActivationFunctionType
AX = mybir.AxisListType

P = 128
D = 1024
KT = D // P
TILES = 9
PT = TILES - 1
TOK = TILES * P
GROUP = 3
NG = TILES // GROUP
GW = GROUP * P
H_A, DK, DV = 4, 128, 256
CH = 64
H_B, HD, VD = 8, 64, 128
STREAMS, SEQ_S = 8, 16
PAST = 512
FF = 4 * D
FC = 512
NFC = FF // FC
ROT = HD // 4 // 2
ALPHA = float(4 ** 0.25)
LAMBDA_INIT = 0.8 - 0.6 * float(np.exp(-0.3))
EPS = 1e-5
PASSES = ((0, 0), (0, 1), (1, 0))
NEG = -1.0e30

C_ID = 0
C_MP = C_ID + P
C_MS = C_MP + P
C_SEL = C_MS + P
C_ROW = C_SEL + P
C_COS = C_ROW + STREAMS
C_SIN = C_COS + TILES * ROT
C_ONE = C_SIN + TILES * ROT
C_NH = C_ONE + CH
C_SG = C_NH + 10
C_END = C_SG + 2


def constants():
    c = np.zeros((P, C_END), np.float32)
    r = np.arange(P)
    c[:, C_ID:C_ID + P] = np.eye(P)
    j, i = r[:, None], r[None, :]
    c[:, C_MP:C_MP + P] = (j // CH == i // CH) & (j <= i)
    c[:, C_MS:C_MS + P] = (j // SEQ_S == i // SEQ_S) & (j <= i)
    c[:, C_SEL:C_SEL + P] = (j // 32 == i // 32) & (j % 16 == i % 32)
    c[:, C_ROW:C_ROW + STREAMS] = r[:, None] // SEQ_S == np.arange(STREAMS)[None, :]
    inv = 1.0 / (500000.0 ** (np.arange(0, 2 * ROT, 2, dtype=np.float32) / (2 * ROT)))
    for t in range(TILES):
        pos = (t * P + r) if t < PT else PAST + r % SEQ_S
        ang = pos.astype(np.float32)[:, None] * inv.astype(np.float32)[None, :]
        c[:, C_COS + t * ROT:C_COS + (t + 1) * ROT] = np.cos(ang)
        c[:, C_SIN + t * ROT:C_SIN + (t + 1) * ROT] = np.sin(ang)
    c[:, C_ONE:C_ONE + CH] = 1.0
    c[:, C_NH:C_NH + 8] = -0.5
    c[:, C_NH + 8:C_NH + 10] = -1.0
    c[:, C_SG] = (r // 16 % 2 == 0)
    c[:, C_SG + 1] = (r // 16 % 2 == 1)
    m = np.zeros((1, 2 * P), np.float32)
    m[0, :CH] = 1.0
    m[0, P + CH:] = NEG
    return c, m


def encoder_step(nc, x_prompt, x_sample, state_gla, cache_k, cache_v, w_in, w_gate, b_gate, g_norm_a,
                 w_o_a, w_kv, w_q, lam, g_norm_b, w_o_b, w_up, w_down, ln_g, ln_b, consts, maskrow,
                 y_prompt, y_sample, gla_prompt, k_prompt, v_prompt, gla_sample, k_sample, v_sample):
    ctx = ExitStack()

    base = 16512

    def at(name, offset, shape, dt=F32):
        return nc.alloc_sbuf_tensor_at(name, shape, dt, offset=offset)

    O_W = base
    O_RAW = O_W + 4 * 2 * 1024 * 4
    O_XT = O_RAW + 4 * 1024 * 4
    O_Q = O_XT + 2 * KT * TOK * 4
    O_V = O_Q + TILES * D * 4
    O_TMP = O_V + TILES * D * 4
    O_C = O_TMP + 11264
    wsplit = at("wsplit", O_W, [P, 4, 2, 1024], F32R)
    raw = at("raw", O_RAW, [P, 4, 1024])
    XTR = [at(f"xt{i}", O_XT, [P, 2, KT, TOK], F32R) for i in range(5)]
    cst = at("cst", O_C, [P, C_END])
    mrow = at("mrow", O_C + 2976, [1, 2 * P])
    stats = at("stats", O_C + 2976 + 1024, [P, 192])
    xin = at("xin", O_V, [P, TILES, D])
    X = at("x_res", O_Q, [P, TILES, D])
    qkT = at("qkT", O_Q, [P, 2, H_A, TOK])
    vO = at("vO", O_V, [P, TILES, D])
    glT = [vO[0:16, 2 * GROUP + g, 512:512 + GW] for g in range(NG)]
    hT = at("hT", O_V, [P, 2, 4, TOK], F32R)
    gm = at("gm", O_TMP, [P, GW])
    gna = at("gna", O_TMP + 1536, [P, GW])
    gb = at("gb", O_TMP + 2 * 1536, [P, GW])
    geb = at("geb", O_TMP + 3 * 1536, [P, GW])
    genb = at("genb", O_TMP + 4 * 1536, [P, GW])
    wglr = at("wglr", O_TMP + 5 * 1536, [P, KT, 16])
    wgls = at("wgls", O_TMP + 5 * 1536 + 512, [P, 2, KT, 16], F32R)
    wgu = at("wgu", O_TMP + 5 * 1536, [16, H_A * DK])
    sie = at("sie", O_TMP, [P, 2, 512])
    sio = at("sio", O_TMP + 4096, [P, 2, 512])
    rin = at("rin", O_TMP, [P, 2, D])
    lng = at("lng", O_TMP, [P, 2, D])
    hsq = at("hsq", O_TMP + 8192, [P, 2, GW])
    gna_g = at("gna_g", O_TMP + 10240, [P, DV])
    kvs = at("kvs", O_V, [P, 6, 512])
    rtmp = at("rtmp", O_V + 12288, [P, 2, 4, 8, ROT])
    kqd = at("kqd", O_TMP, [P, 2, 4, 2, 2, HD])
    KD = at("KD", O_XT, [P, 2, 2, 2, PT * P], F32R)
    QS = at("QS", O_XT + 32768, [P, 2, 2, PT * P], F32R)
    vhead = at("vhead", O_XT + 49152, [P, 3, PT, P])
    PR = at("PR", O_V, [P, 4, 2, PT * P])
    AT = at("AT", O_XT + 61440, [P, 2, PT, P])
    osb = at("osb", O_TMP + 10240, [P, 2, P])
    osq = at("osq", O_V + 33792, [P, P])
    oraw = at("oraw", O_V + 34304, [P, 2, P])
    gnb = at("gnb", O_TMP + 8192, [P, VD])
    lamt = at("lamt", O_TMP + 8704, [P, 4, HD])
    lamp = at("lamp", O_TMP + 9728, [P, 2, HD])
    Kc = at("Kc", O_XT, [P, 2, 4, D])
    Vc = at("Vc", O_XT + 32768, [P, 2, 4, D])
    vS = at("vS", O_XT + 65536, [P, D])
    KTn = at("KTn", O_XT + 69632, [P, H_B, P])
    Qbd = at("Qbd", O_V, [P, 2, H_B, P])
    KTb = at("KTb", O_V + 8192, [P, 2, 4, 512])
    kqS = at("kqS", O_RAW + 8192, [P, 2, D])
    PS = at("PS", O_V + 24576, [P, 2, 640])
    ATs = at("ATs", O_V + 29696, [P, 2, 5, P])
    oW = at("oW", O_RAW, [P, 2 * STREAMS, P])
    QTs = at("QTs", O_TMP, [P, H_B, P])
    oS = at("oS", O_TMP + 4096, [P, D])
    CM = at("CM", O_TMP + 9216, [P, 2, P])
    sqS = at("sqS", O_TMP + 10240, [P, P])
    oin = at("oin", O_V, [P, PT, D])
    nlam = stats[:, 176:177]
    sgl = stats[:, 177:178]
    lam2 = stats[:, 178:180]
    mx = stats[:, 0:4].rearrange("p (a b) -> p a b", a=2)
    nmx = stats[:, 4:8].rearrange("p (a b) -> p a b", a=2)
    ls = stats[:, 8:16].rearrange("p (a b) -> p a b", a=4)
    rl = stats[:, 16:24].rearrange("p (a b) -> p a b", a=4)
    gf = stats[:, 24:28]
    oss = stats[:, 28:32]
    rq = stats[:, 32:36]
    oms = stats[:, 36:40]
    of = stats[:, 44:48]
    ssS = stats[:, 80:96]
    rsS = stats[:, 96:112]
    coef = stats[:, 72:74]
    bg = stats[:, 0:4]
    nbg = stats[:, 4:8]
    elast = stats[:, 8:8 + H_A * 24].rearrange("p (h c) -> p h c", h=H_A)
    ss = stats[:, 104:112].rearrange("p (a b) -> p a b", a=4)
    ms = stats[:, 112:120].rearrange("p (a b) -> p a b", a=4)
    rs4 = stats[:, 120:128].rearrange("p (a b) -> p a b", a=4)
    bst = stats[:, 128:164].rearrange("p (t s) -> p t s", t=3)
    mv = stats[:, 164:170].rearrange("p (t s) -> p t s", t=3)
    rstd = stats[:, 170:173]
    nmr = stats[:, 173:176]
    ktT = at("ktT", O_XT, [P, 2, P])
    kts = at("kts", O_XT + 1024, [P, 2, P])
    attm = at("attm", O_XT + 2048, [P, 2, P])
    S = at("S", O_XT + 3072, [P, 2, H_A, DV])
    sq = at("sq", O_XT + 3072 + 8192, [P, 2, DV])
    ktS = at("ktS", O_XT + 13312, [P, H_A, P])
    attS = at("attS", O_XT + 15360, [P, H_A, P])
    oT = at("oT", O_XT + 17408, [P, 8, P])
    ktb = at("ktb", O_XT + 21504, [P, STREAMS, H_A * P])
    Ss = at("Ss", O_XT + 37888, [P, STREAMS, H_A, DV])

    ident = cst[:, C_ID:C_ID + P]
    neg1 = cst[:, C_NH + 8:C_NH + 10]

    gate_scr = nc.dram_tensor("gate_scr", (TILES, P, D), F32, kind="Internal").ap()
    q_scr = nc.dram_tensor("q_scr", (TILES, P, D), F32, kind="Internal").ap()
    o_scr = nc.dram_tensor("o_scr", (TILES, P, D), F32, kind="Internal").ap()
    kv_dst = [[k_prompt[0].rearrange("(t p) h c d -> t p (h c d)", p=P)[t] for t in range(PT)]
              + [k_sample.rearrange("b s h c d -> (b s) (h c d)")],
              [v_prompt[0].rearrange("(t p) h v -> t p (h v)", p=P)[t] for t in range(PT)]
              + [v_sample.rearrange("b s h v -> (b s) (h v)")],
              [q_scr[t] for t in range(TILES)]]
    y_dst = [y_prompt[0, t * P:(t + 1) * P, :] for t in range(PT)] + [y_sample.rearrange("b s d -> (b s) d")]
    x_scr = [x_prompt[0, t * P:(t + 1) * P, :] for t in range(PT)] + [
        x_sample.rearrange("b s d -> (b s) d")]

    ps = ctx.enter_context(nc.psum_tensor("ps", [P, 8, 512], F32))

    def sem(name):
        return ctx.enter_context(nc.semaphore(name))

    const_in = sem("const_in")
    bias_in = sem("bias_in")
    mask_in = sem("mask_in")
    wgu_in = sem("wgu_in")
    tile_in = [sem(f"tile_in{t}") for t in range(TILES)]
    raw_in = [sem(f"raw_in{s}") for s in range(4)]
    hi_done = sem("hi_done")
    lo_done = sem("lo_done")
    w_used = sem("w_used")
    t_full = sem("t_full")
    t_hi = sem("t_hi")
    t_free = sem("t_free")
    g_full = sem("g_full")
    g_free = sem("g_free")
    gl_raw = sem("gl_raw")
    gl_hi = sem("gl_hi")
    gl_lo = sem("gl_lo")
    gate_min = sem("gate_min")
    gate_log = sem("gate_log")
    gate_cum = sem("gate_cum")
    gate_decays = sem("gate_decays")
    qk_scaled = sem("qk_scaled")
    nbias_done = sem("nbias_done")
    gate_exp = sem("gate_exp")
    r_exp = sem("r_exp")
    r_den = sem("r_den")
    r_recip = sem("r_recip")
    r_silu = sem("r_silu")
    r_out = [sem("r_out0"), sem("r_out1")]
    r_back = [sem("r_back0"), sem("r_back1")]
    decayed_keys = sem("decayed_keys")
    keys_turned = sem("keys_turned")
    scan_scores = sem("scan_scores")
    keys_by_token = sem("keys_by_token")
    scan_kv = sem("scan_kv")
    scores_masked = sem("scores_masked")
    state_updated = sem("state_updated")
    state_read0 = sem("state_read0")
    scan_out = sem("scan_out")
    squares_done = sem("squares_done")
    mean_sq_done = sem("mean_sq_done")
    rms_done = sem("rms_done")
    scan_normed = sem("scan_normed")
    smp_states_in = sem("smp_states_in")
    smp_decayed = sem("smp_decayed")
    smp_turned = sem("smp_turned")
    smp_blocks = sem("smp_blocks")
    smp_scores = sem("smp_scores")
    smp_masked = sem("smp_masked")
    smp_state_out = sem("smp_state_out")
    smp_out_copied = sem("smp_out_copied")
    smp_kv = sem("smp_kv")
    smp_updated = sem("smp_updated")
    states_out = sem("states_out")
    gated = sem("gated")
    gna_in = sem("gna_in")
    gate_d = sem("gate_d")
    y_out = sem("y_out")
    x_res_in = sem("x_res_in")
    lng_in = sem("lng_in")
    ln_var = sem("ln_var")
    ln_rstd = sem("ln_rstd")
    ln_nmr = sem("ln_nmr")
    ln_norm = sem("ln_norm")
    ln_gain = sem("ln_gain")
    ln_done = sem("ln_done")
    ln_st = sem("ln_st")
    up_r = sem("up_r")
    up_h = sem("up_h")
    up_sq = sem("up_sq")
    rope = sem("rope")
    kv_done = sem("kv_done")
    pair_loaded = [sem("pair_loaded0"), sem("pair_loaded1")]
    values_loaded = [sem(f"values_loaded{i}") for i in range(3)]
    turned_full = sem("turned_full")
    turned_hi = sem("turned_hi")
    turned_free = sem("turned_free")
    s_full = sem("s_full")
    max_done = sem("max_done")
    negmax_done = sem("negmax_done")
    exp_done = sem("exp_done")
    balance_done = sem("balance_done")
    combined = sem("combined")
    a_full = [sem("a_full0"), sem("a_full1")]
    a_free = [sem("a_free0"), sem("a_free1")]
    o_full = sem("o_full")
    out_squared = sem("out_squared")
    factor_done = sem("factor_done")
    out_normed = sem("out_normed")
    lam_in = sem("lam_in")
    lam_p = sem("lam_p")
    lam_e = sem("lam_e")
    lambda_done = sem("lambda_done")
    gnb_in = sem("gnb_in")
    o_out = [sem("o_out0"), sem("o_out1")]
    smp_qk_in = sem("smp_qk_in")
    smp_v_in = sem("smp_v_in")
    smp_qk_turned = sem("smp_qk_turned")
    smp_qk_copied = sem("smp_qk_copied")
    smp_q_blocks = sem("smp_q_blocks")
    smp_q_zero = sem("smp_q_zero")
    kc_in = [sem("kc_in0"), sem("kc_in1")]
    vc_in = [sem("vc_in0"), sem("vc_in1")]
    cache_turned = sem("cache_turned")
    keys_copied0 = sem("keys_copied0")
    keys_copied1 = sem("keys_copied1")
    smp_s_full = sem("smp_s_full")
    smp_max = sem("smp_max")
    smp_exp = sem("smp_exp")
    smp_coef = sem("smp_coef")
    smp_select = sem("smp_select")
    smp_w_turned = sem("smp_w_turned")
    smp_w_copied = sem("smp_w_copied")
    smp_pv = sem("smp_pv")
    smp_out = sem("smp_out")
    smp_sq = sem("smp_sq")
    smp_rms = sem("smp_rms")
    smp_fin = sem("smp_fin")
    smp_stored = sem("smp_stored")
    smp_w_zero = sem("smp_w_zero")
    prompt_done = sem("prompt_done")
    pool_small = sem("pool_small")
    o_free = sem("o_free")
    up_done = sem("up_done")
    dve_steps = sem("dve_steps")
    kv_out = [sem(f"kv_out{i}") for i in range(6)]

    TU_X0 = 0
    TU_GL = TU_X0 + 2 * TILES
    TU_Q = TU_GL + NG
    TU_LOG = TU_Q + 8 * NG
    TU_O1 = TU_LOG + H_A * NG
    TU_L = [0] * 3
    TU_L[0] = TU_O1 + 2 * TILES
    TU_UP = [0, 0]
    TU_UP[0] = TU_L[0] + 2 * TILES
    TU_L[1] = TU_UP[0] + NFC * 4 * NG
    TU_O2 = TU_L[1] + 2 * TILES
    TU_L[2] = TU_O2 + 2 * TILES
    TU_UP[1] = TU_L[2] + 2 * TILES
    GU_V = 0
    GU_R = GU_V + 2 * TILES
    GU_O = GU_R + 2 * TILES
    GU_MLP = [GU_O + 2 * TILES, 0]
    GU_KVQ = GU_MLP[0] + NFC * 2 * TILES
    GU_O2 = GU_KVQ + 6 * TILES
    GU_MLP[1] = GU_O2 + 2 * TILES
    UPS = NFC * 4 * NG
    G_QK, G_V, G_R, G_O = 0, 8, 16, 24
    G_MLP = [32, 0]
    G_KVQ = G_MLP[0] + 8 * NFC
    G_O2 = G_KVQ + 24
    G_MLP[1] = G_O2 + 8

    def a_banks(s):
        h, i = s // PT, s % PT
        if i < 4:
            return [(i % 2, range(i + 1), 6 * h + i // 2)]
        return [(0, range(4), 6 * h + i - 2), (1, range(4, i + 1), 6 * h + i - 2)]

    STEPS = H_B * PT

    def p_bank(i):
        return 4 + i % 4 if i < 8 else 4

    def after_norm(lay):
        def tr(grp):
            return [("tr", t, half) for t in range(grp * GROUP, (grp + 1) * GROUP) for half in range(2)]

        def up(ng, *ms):
            return [("up", m, ng) for m in ms]
        seq = (tr(0) + up(0, 0, 1, 2) + tr(1) + up(0, 3) + up(1, 0, 1, 2) + tr(2) + up(1, 3) + up(2, 0, 1, 2, 3))
        return [(TU_L[2 * lay] + i, *e) for i, e in enumerate(seq)]

    def quarter_use():
        free = [(t_full, TU_Q + 3 * m + 3) for m in range(8)]
        used = [0]

        def count():
            used[0] += 1
            return (w_used, used[0])

        def of_product(use):
            free.extend([count(), count(), count(), (g_full, use + TILES)])

        for use in (GU_V, GU_R, GU_O):
            of_product(use)
            of_product(use + TILES)
        for lay in range(2):
            first = {e[2]: e[0] + 1 for e in after_norm(lay) if e[1] == "up" and e[3] == NG - 1}
            for c in range(NFC):
                for m in range(4):
                    free.append((t_full, first[m] if c == 0 else TU_UP[lay] + 12 * c + 3 * m + NG))
                for nh in range(2):
                    done = TILES * (nh + 1) if c < NFC - 1 else 5 * GROUP + GROUP * nh
                    free.extend([count(), (g_full, GU_MLP[lay] + 2 * TILES * c + done)])
            if lay == 0:
                for u in range(8):
                    of_product(GU_KVQ + TILES * u)
        return free

    QUARTER_FREE = quarter_use()

    def chunk_quarter_free(lay, c, q):
        semaphore, first = QUARTER_FREE[G_MLP[lay] + 8 + q]
        step = QUARTER_FREE[G_MLP[lay] + 16 + q][1] - first
        return semaphore, c * step + (first - step)

    FIRST_UP = [e[2:] for e in after_norm(0) if e[1] == "up"]
    DOWN_ORDER = [[(nh, grp) for nh in range(2) for grp in range(NG)],
                  [(nh, grp) for grp in range(NG) for nh in range(2)]]
    LOG_AT = {2 * i: (i // NG, i % NG) for i in range(H_A * NG)}

    block = ctx.enter_context(nc.Block())

    @block.sync
    def _(sp):
        def load(g, src, n):
            if g >= 4:
                sp.wait_ge(lo_done, g - 3)
            sp.dma_start(raw[:, g % 4, :].rearrange("p (k n) -> p k n", n=n),
                         src.rearrange("(k p) n -> p k n", p=P)).then_inc(raw_in[g % 4], 16)

        def load_p(g, w, u):
            for j in range(4):
                load(g + j, w[j * 256:(j + 1) * 256, u * 512:(u + 1) * 512], 512)

        for t in range(3):
            sp.dma_start(xin[:, t, :], x_scr[t]).then_inc(tile_in[t], 16)
            if t == 0:
                sp.dma_start(cst[:], consts).then_inc(const_in, 16)
        for m in range(4):
            load(m, w_in[0, :, m * P:(m + 1) * P], P)
            if m < 3:
                for t in (3 + 2 * m, 4 + 2 * m):
                    sp.dma_start(xin[:, t, :], x_scr[t]).then_inc(tile_in[t], 16)
        sp.dma_start(wglr[:], w_in[0, :, 3072:3088].rearrange("(k p) n -> p k n", p=P)).then_inc(gl_raw, 16)
        sp.dma_start(bg, b_gate).then_inc(bias_in, 16)
        sp.dma_start(gna_g[:], g_norm_a[0:1, :].broadcast_to([P, DV])).then_inc(gna_in, 16)
        sp.dma_start(mrow[:], maskrow).then_inc(mask_in, 16)
        for m in range(4, 8):
            load(m, w_in[0, :, m * P:(m + 1) * P], P)
        sp.wait_ge(t_free, TU_Q)
        sp.dma_start(wgu[:], w_gate[0]).then_inc(wgu_in, 16)
        for u in range(2):
            load_p(G_V + 4 * u, w_in[0, :, 1024:2048], u)
        n = 0
        for u in range(2):
            load_p(G_R + 4 * u, w_in[0, :, 2048:3072], u)
        for u in range(2):
            if u == 1:
                load_p(G_O, w_o_a[0], 0)
            for t in range(TILES):
                sp.wait_ge(r_silu, n + 1)
                sp.dma_start(gate_scr[t, :, u * 512:(u + 1) * 512], sio[:, n % 2, :]).then_inc(r_out[n % 2], 16)
                n += 1
        sp.wait_ge(g_full, GU_O)
        for b in range(STREAMS):
            sp.dma_start(Ss[:, b], state_gla[0, b].rearrange("h k v -> k h v")).then_inc(smp_states_in, 16)
        def gates_back(t):
            if t >= 2:
                sp.wait_ge(gated, t - 1)
            sp.dma_start(rin[:, t % 2, :], gate_scr[t]).then_inc(r_back[t % 2], 16)

        for n2 in range(2):
            sp.wait_ge(r_out[n2], 16 * TILES)
        sp.wait_ge(r_silu, 2 * TILES)
        for t in range(2):
            gates_back(t)
        sp.wait_ge(state_updated, 2 * PT * H_A)
        sp.dma_start(gla_prompt[0, 0].rearrange("h k v -> k h v"), S[:, 0]).then_inc(states_out, 16)
        for b in range(STREAMS):
            sp.wait_ge(smp_updated, 2 * (b + 1))
            sp.dma_start(gla_sample[0, b].rearrange("h k v -> k h v"), Ss[:, b]).then_inc(states_out, 16)
        for t in range(TILES):
            sp.dma_start(X[:, t, :], x_scr[t]).then_inc(x_res_in, 16)
            if t + 2 < TILES:
                gates_back(t + 2)
        sp.wait_ge(states_out, 16 * (1 + STREAMS))
        sp.wait_ge(g_free, GU_O)
        def norm_params(n):
            if n:
                sp.wait_ge(ln_done, TILES * n)
            for i, w in enumerate((ln_g, ln_b)):
                sp.dma_start(lng[:, i, :], w[n // 2, n % 2:n % 2 + 1, :].broadcast_to([P, D])).then_inc(lng_in, 16)

        def mlp_loads(lay, c):
            if isinstance(c, int):
                col, row = w_up[lay, :, c * FC:(c + 1) * FC], w_down[lay, c * FC:(c + 1) * FC, :]
            else:
                col, row = w_up[lay, :, bass.ds(c * FC, FC)], w_down[lay, bass.ds(c * FC, FC), :]
            for j in range(8):
                if j < 4:
                    src, n = col[:, j * P:(j + 1) * P], P
                else:
                    nh, kp = divmod(j - 4, 2)
                    src, n = row[kp * 256:(kp + 1) * 256, nh * 512:(nh + 1) * 512], 512
                sp.wait_ge(lo_done, 8 * c + (G_MLP[lay] + j - 3))
                sp.dma_start(raw[:, j % 4, :].rearrange("p (k n) -> p k n", n=n),
                             src.rearrange("(k p) n -> p k n", p=P)).then_inc(raw_in[j % 4], 16)

        sp.wait_ge(gated, TILES)
        norm_params(0)
        load_p(G_O + 4, w_o_a[0], 1)
        mlp_loads(0, 0)
        norm_params(1)
        with sp.Fori(1, NFC - 1) as c:
            mlp_loads(0, c)
        mlp_loads(0, NFC - 1)
        def pair_in(i):
            h, mat, part = i // 4, i % 4 // 2, i % 2
            src = k_prompt[0].rearrange("(t p) h c d -> p t h c d", p=P)[:, :, h] if mat == 0 else \
                q_scr[0:PT].rearrange("t p (h c d) -> p t h c d", h=H_B, c=2)[:, :, h]
            if i >= 2:
                sp.wait_ge(turned_full, 2 * i - 2)
            for dup in range(2):
                for t in range(4):
                    sp.dma_start(kqd[:, i % 2, t, :, dup, :], src[:, 4 * part + t]).then_inc(pair_loaded[i % 2], 16)

        n = 0
        for u in range(6):
            w, col = (w_kv, u * 512) if u < 4 else (w_q[0], (u - 4) * 512)
            load_p(G_KVQ + 4 * u, w[:, col:col + 512], 0)
            if u:
                for t in range(TILES):
                    sp.wait_ge(kv_done, n + 1)
                    sp.dma_start(kv_dst[(u - 1) // 2][t][:, (u - 1) % 2 * 512:(u - 1) % 2 * 512 + 512],
                                 kvs[:, n % 6, :]).then_inc(kv_out[n % 6], 16)
                    n += 1
        load_p(G_O2, w_o_b[0], 0)
        sp.wait_ge(ln_done, 2 * TILES)
        for i in range(6):
            sp.wait_ge(kv_out[i], 16 * 2 * TILES // 6)
        pair_in(0)
        pair_in(1)
        sp.dma_start(lamt[:], lam[0:1].broadcast_to([P, 4, HD])).then_inc(lam_in, 16)
        sp.dma_start(gnb[:], g_norm_b[0:1, :].broadcast_to([P, VD])).then_inc(gnb_in, 16)
        for t in range(TILES):
            sp.wait_ge(kv_done, n + 1)
            sp.dma_start(kv_dst[2][t][:, 512:1024], kvs[:, n % 6, :]).then_inc(kv_out[n % 6], 16)
            n += 1
        for i in range(6):
            sp.wait_ge(kv_out[i], 16 * TILES)

        def values_in(h):
            if h >= 3:
                sp.wait_ge(o_full, PT * (h - 2))
            sp.dma_start(vhead[:, h % 3], v_prompt[0].rearrange("(t p) h v -> p t h v", p=P)[:, :, h]).then_inc(values_loaded[h % 3], 16)

        def out_o(s):
            sp.wait_ge(out_normed, s + 1)
            h, i = s // PT, s % PT
            sp.dma_start(o_scr[i, :, h * P:(h + 1) * P], osb[:, s % 2, :]).then_inc(o_out[s % 2], 16)

        pair_in(2)
        pair_in(3)
        sp.wait_ge(g_full, GU_O2)
        values_in(0)
        pair_in(4)
        values_in(1)
        pair_in(5)
        pair_in(6)
        values_in(2)
        def keys_in(b):
            if b >= 2:
                sp.wait_ge(cache_turned, 8 * (b - 1))
            sp.dma_start(Kc[:, b % 2], cache_k[b].rearrange("(t p) h c d -> p t (h c d)", p=P)).then_inc(kc_in[b % 2], 16)

        def cached_values_in(b):
            if b >= 2:
                sp.wait_ge(smp_pv, 2 * (b - 1))
            sp.dma_start(Vc[:, b % 2], cache_v[b].rearrange("(t p) h v -> p t (h v)", p=P)).then_inc(vc_in[b % 2], 16)

        for s in range(STEPS):
            if s % 2 == 0 and 7 + s // 2 < 4 * H_B:
                pair_in(7 + s // 2)
            if s % PT == PT - 1 and s // PT + 3 < H_B:
                values_in(s // PT + 3)
            if s == PT:
                sp.wait_ge(lo_done, G_O2 + 4)
                for i, src in enumerate((kv_dst[0][PT], q_scr[PT])):
                    sp.dma_start(kqS[:, i, :], src).then_inc(smp_qk_in, 16)
            if s == STEPS - PT:
                sp.wait_ge(turned_full, 8 * H_B)
                sp.wait_ge(s_full, 2 * (STEPS - PT))
                keys_in(0)
            out_o(s)

        sp.wait_ge(o_full, STEPS)
        keys_in(1)
        sp.dma_start(vS[:], kv_dst[1][PT]).then_inc(smp_v_in, 16)
        cached_values_in(0)

        def sample_out(b):
            sp.wait_ge(smp_fin, 2 * (b + 1))
            dst = o_scr[PT, b * SEQ_S:(b + 1) * SEQ_S, :].rearrange("q (z h v) -> q z h v", z=2, h=4)
            for hh in range(4):
                sp.dma_start(dst[:, :, hh], oW[32 * hh:32 * hh + SEQ_S, 2 * b:2 * b + 2, :]).then_inc(smp_stored, 16)

        for b in range(1, STREAMS):
            if b + 1 < STREAMS:
                keys_in(b + 1)
            cached_values_in(b)
            if b >= 3:
                sample_out(b - 3)
        for b in range(STREAMS - 3, STREAMS - 1):
            sample_out(b)
        for i in range(2):
            sp.wait_ge(o_out[i], 16 * H_B * PT // 2)
        sp.wait_ge(smp_s_full, 2 * STREAMS)
        for t in range(PT):
            if t == 6:
                sp.wait_ge(smp_pv, 2 * STREAMS)
            sp.dma_start(oin[:, t, :], o_scr[t]).then_inc(tile_in[t], 16)
        sample_out(STREAMS - 1)
        sp.wait_ge(smp_stored, 64 * STREAMS)
        sp.dma_start(oS[:], o_scr[PT]).then_inc(tile_in[PT], 16)
        load_p(G_O2 + 4, w_o_b[0], 1)
        sp.wait_ge(t_free, TU_O2 + 2 * TILES)
        norm_params(2)
        mlp_loads(1, 0)
        norm_params(3)
        with sp.Fori(1, NFC - 1) as c:
            mlp_loads(1, c)
        mlp_loads(1, NFC - 1)
        for t in range(TILES):
            sp.wait_ge(ln_done, 3 * TILES + t + 1)
            sp.dma_start(y_dst[t], X[:, t, :]).then_inc(y_out, 16)
        sp.wait_ge(y_out, 16 * TILES)

    @block.gpsimd
    def _(pool):
        def split_lo(g, slot=None):
            slot = g % 4 if slot is None else slot
            pool.wait_ge(hi_done, g + 1)
            nc.gpsimd.tensor_tensor(wsplit[:, slot, 1, :], raw[:, slot, :],
                                    wsplit[:, slot, 0, :].bitcast(F32), ALU.subtract).then_inc(lo_done, 1)

        def power(p):
            pool.wait_ge(mean_sq_done, p + 1)
            nc.gpsimd.tensor_tensor(rs4[:, p % 4, :], ms[:, p % 4, :], cst[:, C_NH:C_NH + 2],
                                    ALU.pow).then_inc(rms_done, 1)

        pool.wait_ge(const_in, 16)
        for g in range(4):
            split_lo(g)
        pool.wait_ge(gl_hi, 1)
        nc.gpsimd.tensor_tensor(wgls[:, 1], wglr[:], wgls[:, 0].bitcast(F32), ALU.subtract).then_inc(gl_lo, 1)
        for g in range(4, G_O + 4):
            split_lo(g)
        for p in range(2 * PT + 2):
            power(p)

        def rstds(n, grp):
            for i in range(n * TILES + grp * GROUP, n * TILES + (grp + 1) * GROUP):
                pool.wait_ge(ln_var, i + 1)
                nc.gpsimd.tensor_tensor(rstd[:, i % 3:i % 3 + 1], mv[:, i % 3, 1:2], cst[:, C_NH:C_NH + 1],
                                        ALU.pow).then_inc(ln_rstd, 1)

        def gain(n, t):
            pool.wait_ge(ln_norm, n * TILES + t + 1)
            if t == 0:
                pool.wait_ge(lng_in, 32 * (n + 1))
            nc.gpsimd.tensor_tensor(X[:, t, :], X[:, t, :], lng[:, 0, :], ALU.mult).then_inc(ln_gain, 1)

        def norm(n, grp):
            rstds(n, grp)
            for t in range(grp * GROUP, (grp + 1) * GROUP):
                gain(n, t)

        def product_norm(n, g):
            norm(n, 0)
            rstds(n, 1)
            for j in range(4):
                split_lo(g + 4 + j)
                if j < GROUP:
                    gain(n, GROUP + j)
            norm(n, 2)

        def mlp(lay):
            g = G_MLP[lay]
            for j in range(4, 8):
                split_lo(g + j)
            with pool.Fori(1, NFC - 1) as c:
                for j in range(8):
                    split_lo(8 * c + (g + j), slot=j % 4)
            for j in range(8 * (NFC - 1), 8 * NFC):
                split_lo(g + j)
            norm(2 * lay + 1, 0)
            rstds(2 * lay + 1, 1)
            for j in range(4):
                if j < GROUP:
                    gain(2 * lay + 1, GROUP + j)
                if lay == 0:
                    split_lo(g + 8 * NFC + j)
            norm(2 * lay + 1, 2)

        for j in range(4):
            split_lo(G_O + 4 + j)
        product_norm(0, G_O + 4)
        mlp(0)
        for g in range(G_KVQ + 4, G_O2):
            split_lo(g)

        pool_steps = [0]

        def small(fn, *a, done=None):
            ins = fn(*a)
            if done is None:
                pool_steps[0] += 1
                ins.then_inc(pool_small, 1)
                pool.wait_ge(pool_small, pool_steps[0])
            else:
                ins.then_inc(done, 1)
        tt, ts = nc.gpsimd.tensor_tensor, nc.gpsimd.tensor_scalar

        def balance(s):
            r = s % 4
            pool.wait_ge(exp_done, 2 * s + 2)
            small(tt, rl[:, r, 1:2], ls[:, r, 1:2], neg1[:, 0:1], ALU.pow)
            small(tt, gf[:, r:r + 1], ls[:, r, 0:1], rl[:, r, 1:2], ALU.mult)
            small(tt, gf[:, r:r + 1], gf[:, r:r + 1], nlam, ALU.mult, done=balance_done)
            small(tt, rq[:, r:r + 1], ls[:, r, 0:1], ls[:, r, 0:1], ALU.mult)
            small(ts, rq[:, r:r + 1], rq[:, r:r + 1], EPS, None, ALU.mult)

        def factor(s):
            r = s % 4
            pool.wait_ge(out_squared, s + 1)
            small(tt, oms[:, r:r + 1], oss[:, r:r + 1], rq[:, r:r + 1], ALU.add)
            small(tt, of[:, r:r + 1], oms[:, r:r + 1], cst[:, C_NH:C_NH + 1], ALU.pow, done=factor_done)

        pool.wait_ge(lambda_done, 1)
        for s in range(STEPS + 2):
            if s < STEPS:
                balance(s)
            if s >= 2:
                factor(s - 2)
            if 2 <= s < 6:
                split_lo(G_O2 + s - 2)

        pool.wait_ge(prompt_done, 1)
        nc.gpsimd.memset(Qbd[:], 0.0).then_inc(smp_q_zero, 1)
        nc.gpsimd.memset(PS[:, :, 512:640], 0.0).then_inc(smp_w_zero, 1)
        pool.wait_ge(smp_q_zero, 1)
        pool.wait_ge(smp_w_zero, 1)
        pool.wait_ge(smp_qk_copied, 4)

        def queries(b):
            if b >= 2:
                pool.wait_ge(smp_s_full, 2 * (b - 1))
            for c in range(2):
                for hh in range(4):
                    col = 32 * hh + 16 * c
                    nc.gpsimd.tensor_copy(Qbd[c * HD:(c + 1) * HD, b % 2, hh::4, col:col + 16],
                                          QTs[c * HD:(c + 1) * HD, hh::4, b * 16:b * 16 + 16]).then_inc(smp_q_blocks, 1)
                pool.wait_ge(smp_q_blocks, 8 * b + 4 * (c + 1))

        def coefficient(w):
            pool.wait_ge(smp_exp, 2 * w + 2)
            r = w % 2
            small(tt, ls[:, r, 0:1], ls[:, r, 0:1], ls[:, r, 1:2], ALU.add)
            small(tt, coef[:, r:r + 1], ls[:, r, 0:1], neg1[:, 0:1], ALU.pow)
            small(tt, coef[:, r:r + 1], coef[:, r:r + 1], sgl, ALU.mult, done=smp_coef)

        def clear_new(w):
            pool.wait_ge(smp_w_turned, w - 1)
            nc.gpsimd.memset(PS[:, w % 2, 512:640], 0.0).then_inc(smp_w_zero, 1)
            pool.wait_ge(smp_w_zero, w)

        def sample_rstd(w):
            pool.wait_ge(smp_sq, w + 1)
            small(ts, ssS[:, w:w + 1], ssS[:, w:w + 1], EPS, None, ALU.add)
            small(tt, rsS[:, w:w + 1], ssS[:, w:w + 1], cst[:, C_NH:C_NH + 1], ALU.pow, done=smp_rms)

        queries(0)
        queries(1)
        coefficient(0)
        for w in range(2 * STREAMS + 2):
            if 1 <= w < 2 * STREAMS - 1:
                clear_new(w + 1)
            if w < 2 * STREAMS - 1:
                coefficient(w + 1)
            if w % 2 and (w + 3) // 2 < STREAMS:
                queries((w + 3) // 2)
            if w >= 2:
                sample_rstd(w - 2)
        for j in range(4):
            split_lo(G_O2 + 4 + j)
        product_norm(2, G_O2 + 4)
        mlp(1)

    @block.scalar
    def _(act):
        def split_hi_of(slot, loads, free):
            act.wait_ge(raw_in[slot], 16 * loads)
            if free:
                act.wait_ge(*free)
            nc.scalar.activation(wsplit[:, slot, 0, :], raw[:, slot, :], ACT.Copy).then_inc(hi_done, 1)

        def split_hi(g):
            split_hi_of(g % 4, g // 4 + 1, QUARTER_FREE[g - 4] if g >= 4 else None)

        def transposed_hi(u, xt, t, half):
            act.wait_ge(t_full, u + 1)
            nc.scalar.activation(xt[:, 0, 4 * half:4 * half + 4, t * P:(t + 1) * P],
                                 ps[:, 6 + u % 2, :].rearrange("p (k n) -> p k n", n=P),
                                 ACT.Copy).then_inc(t_hi, 1)

        for t in range(TILES):
            for half in range(2):
                transposed_hi(TU_X0 + 2 * t + half, XTR[0], t, half)
            if t and t % 2 == 0:
                split_hi(t // 2 - 1)
        act.wait_ge(gl_raw, 16)
        nc.scalar.activation(wgls[:, 0], wglr[:], ACT.Copy).then_inc(gl_hi, 1)
        act.wait_ge(const_in, 16)
        act.wait_ge(bias_in, 16)
        nc.scalar.mul(nbg, bg, -1.0).then_inc(nbias_done, 1)
        for g in range(4, 12):
            split_hi(g)
        for step in range(24):
            if step in LOG_AT:
                i = step // 2
                act.wait_ge(gate_min, 2 * i + 2)
                if i == 0:
                    act.wait_ge(nbias_done, 1)
                h = LOG_AT[step][0]
                nc.scalar.activation(gna[:], gna[:], ACT.Exp, bias=nbg[:, h:h + 1]).then_inc(gate_exp, 1)
                act.wait_ge(gate_exp, i + 1)
                nc.scalar.activation(gna[:], gna[:], ACT.Ln, bias=1.0).then_inc(gate_log, 1)
                act.wait_ge(gate_cum, i + 1)
                if i:
                    act.wait_ge(qk_scaled, 3 * i)
                nc.scalar.activation(geb[:], gb[:], ACT.Exp, scale=1.0 / 16).then_inc(gate_decays, 1)
                nc.scalar.activation(genb[:], gb[:], ACT.Exp, scale=-1.0 / 16).then_inc(gate_decays, 1)
            if step % 12 >= 8:
                split_hi(12 + 4 * (step // 12) + step % 12 - 8)
        def exp_r(n):
            use = GU_R + n
            act.wait_ge(g_full, use + 1)
            if n >= 2:
                act.wait_ge(r_silu, n - 1)
            nc.scalar.activation(sie[:, n % 2, :], ps[:, use % 6, :], ACT.Exp, scale=-1.0).then_inc(r_exp, 1)

        for u in range(2):
            for n in range(2 * GROUP):
                exp_r(u * TILES + n)
            for j in range(3):
                split_hi(G_R + 4 * u + 4 + j)
            for n in range(2 * GROUP, TILES):
                if n == TILES - 1:
                    split_hi(G_R + 4 * u + 7)
                exp_r(u * TILES + n)

        def decayed(s):
            t, h = s // H_A, s % H_A
            if s >= 2:
                act.wait_ge(keys_turned, s - 1)
            for c in range(2):
                last = nc.scalar.mul(ktT[:, s % 2, c * CH:(c + 1) * CH],
                                     qkT[:, 1, h, t * P + c * CH:t * P + (c + 1) * CH],
                                     elast[:, h, 2 * t + c:2 * t + c + 1])
            last.then_inc(decayed_keys, 1)

        def to_tokens(s):
            act.wait_ge(keys_turned, s + 1)
            if s >= 2:
                act.wait_ge(scan_kv, 2 * (s - 1))
            nc.scalar.activation(kts[:, s % 2, :], ps[:, 0, 0:P], ACT.Copy).then_inc(keys_by_token, 1)

        def squares(p):
            t, hp = p // 2, p % 2
            act.wait_ge(scan_out, 4 * t + 2 * hp + 2)
            if p >= 4:
                act.wait_ge(mean_sq_done, p - 3)
            for k in range(2):
                if p or k:
                    act.wait_ge(squares_done, 2 * p + k)
                nc.scalar.activation(sq[:, k, :], ps[:, 4 + 2 * (t % 2) + hp, k * DV:(k + 1) * DV],
                                     ACT.Square, accum_out=ss[:, p % 4, k:k + 1]).then_inc(squares_done, 1)

        act.wait_ge(qk_scaled, 3 * H_A * NG)
        act.wait_ge(g_full, GU_O)
        steps = PT * H_A
        decayed(0)
        decayed(1)
        to_tokens(0)
        for s in range(steps):
            if s + 2 < steps:
                decayed(s + 2)
            if s + 1 < steps:
                to_tokens(s + 1)
            if s % 2 == 1:
                squares(s // 2)
        act.wait_ge(smp_turned, 4)
        for b in range(STREAMS):
            last = nc.scalar.mul(ktb[:, b, :], ps[:, 0, :], cst[:, C_ROW + b:C_ROW + b + 1])
        last.then_inc(smp_blocks, 1)
        act.wait_ge(smp_state_out, 1)
        for i in range(2):
            last = nc.scalar.activation(oT[:, 4 * i:4 * i + 4, :],
                                        ps[:, 4 + i, :].rearrange("p (k n) -> p k n", n=P), ACT.Copy)
        last.then_inc(smp_out_copied, 1)
        for p in (2 * PT, 2 * PT + 1):
            act.wait_ge(scan_out, 4 * PT + 2 * (p - 2 * PT) + 2)
            act.wait_ge(mean_sq_done, p - 3)
            for k in range(2):
                act.wait_ge(squares_done, 2 * p + k)
                nc.scalar.activation(sq[:, k, :], ps[:, 6 + p - 2 * PT, k * DV:(k + 1) * DV],
                                     ACT.Square, accum_out=ss[:, p % 4, k:k + 1]).then_inc(squares_done, 1)
        act.wait_ge(smp_updated, 2 * STREAMS)
        act.wait_ge(states_out, 16 * (1 + STREAMS))
        for t in range(TILES):
            for half in range(2):
                transposed_hi(TU_O1 + 2 * t + half, XTR[1], t, half)

        def norm(n, grp, between=None, after=None):
            for t in range(grp * GROUP, (grp + 1) * GROUP):
                i = n * TILES + t
                if between:
                    between(t - grp * GROUP)
                act.wait_ge(ln_nmr, i + 1)
                nc.scalar.activation(X[:, t, :], X[:, t, :], ACT.Identity, bias=nmr[:, i % 3:i % 3 + 1],
                                     scale=rstd[:, i % 3:i % 3 + 1]).then_inc(ln_norm, 1)
                if after:
                    after(t - grp * GROUP)

        def hidden(n, m, ng, slot):
            act.wait_ge(up_r, n + 1)
            nc.scalar.activation(hsq[:, slot, :], hsq[:, slot, :], ACT.Square).then_inc(up_sq, 1)
            act.wait_ge(up_sq, n + 1)
            nc.scalar.activation(hT[:, 0, m, ng * GW:(ng + 1) * GW], hsq[:, slot, :], ACT.Copy).then_inc(up_h, 1)

        def residual_norm(lay, g):
            n = 2 * lay
            norm(n, 0)
            k = 0
            for i, (u, kind, p, q) in enumerate(after_norm(lay)):
                if i == 2 * GROUP:
                    norm(n, 1, between=lambda j: split_hi(g + 4 + j))
                    split_hi(g + 4 + GROUP)
                if kind == "tr":
                    transposed_hi(u, XTR[2 if lay == 0 else 4], p, q)
                    if (p, q) == (2 * GROUP - 1, 1):
                        norm(n, 2)
                else:
                    hidden(UPS * lay + k, p, q, k % 2)
                    k += 1
                    if q == NG - 1:
                        split_hi(G_MLP[lay] + 4 + p)

        def normed_transposes(grp):
            for t in range(grp * GROUP, (grp + 1) * GROUP):
                for half in range(2):
                    transposed_hi(TU_L[1] + 2 * t + half, XTR[3], t, half)

        def mlp(lay):
            g = G_MLP[lay]
            for j in range(8, 12):
                split_hi(g + j)

            def ups(c, free):
                for m in range(4):
                    for ng in range(NG):
                        hidden(12 * c + (UPS * lay + 3 * m + ng), m, ng, (3 * m + ng) % 2)
                    split_hi_of(m, 2 * c + (g // 4 + 2), free(m))
            with act.Fori(1, NFC - 1) as c:
                ups(c, lambda q: chunk_quarter_free(lay, c, q))
                for j in range(4):
                    split_hi_of(j, 2 * c + (g // 4 + 3), chunk_quarter_free(lay, c, 4 + j))
            ups(NFC - 1, lambda q: QUARTER_FREE[g + 8 * (NFC - 1) + q])
            norm(2 * lay + 1, 0)
            if lay == 0:
                norm(1, 1, after=lambda j: split_hi(g + 8 * NFC + j) if j < 2 else None)
                normed_transposes(0)
                for j in (2, 3):
                    split_hi(g + 8 * NFC + j)
            else:
                norm(3, 1)
                norm(3, 2)

        for j in range(4):
            split_hi(G_O + 4 + j)
        residual_norm(0, G_O + 4)
        mlp(0)
        for grp in range(NG):
            if grp == 2:
                norm(1, grp)
            if grp:
                normed_transposes(grp)
        for g in range(G_KVQ + 4, G_O2):
            split_hi(g)

        act.wait_ge(lam_p, 2)
        nc.scalar.activation(lam2, lam2, ACT.Exp).then_inc(lam_e, 1)

        def prepare(i):
            h, j = i // 8, i % 8
            act.wait_ge(turned_full, i + 1)
            c, part = j % 2, j % 4 // 2
            if j < 4:
                dst = KD[:, h % 2, 0, c, part * 512:(part + 1) * 512]
            else:
                dst = QS[:, h % 2, c, part * 512:(part + 1) * 512]
            nc.scalar.activation(dst, ps[:, p_bank(i), :], ACT.Copy).then_inc(turned_hi, 1)

        def exponentials(s, c):
            w = (s % PT + 1) * P
            act.wait_ge(negmax_done, 2 * s + c + 1)
            if s >= 4 and c == 0:
                bank, _, use = a_banks(s - 4)[-1]
                act.wait_ge(a_full[bank], use + 1)
                act.wait_ge(factor_done, s - 3)
            nc.scalar.activation(PR[:, s % 4, c, 0:w], ps[:, 2 * c:2 * c + 2, :].rearrange("p a n -> p (a n)")[:, 0:w],
                                 ACT.Exp, bias=nmx[:, s % 2, c:c + 1], scale=HD ** -0.5,
                                 accum_out=ls[:, s % 4, c:c + 1]).then_inc(exp_done, 1)

        def weights_out(s):
            for bank, tiles, use in a_banks(s):
                if bank == 0:
                    act.wait_ge(a_full[0], use + 1)
                    if s >= 2:
                        act.wait_ge(o_full, s - 1)
                    n = len(tiles)
                    nc.scalar.activation(AT[:, s % 2, tiles[0]:tiles[0] + n, :],
                                         ps[:, 5, 0:n * P].rearrange("p (k n) -> p k n", n=P),
                                         ACT.Copy).then_inc(a_free[0], 1)

        def out_square(s):
            act.wait_ge(o_full, s + 1)
            if s:
                act.wait_ge(out_squared, s)
            if s >= 4:
                act.wait_ge(factor_done, s - 3)
            nc.scalar.activation(osq[:], ps[:, 7, 0:P], ACT.Square, scale=VD ** -0.5,
                                 accum_out=oss[:, s % 4:s % 4 + 1]).then_inc(out_squared, 1)
            if s >= 2:
                act.wait_ge(out_normed, s - 1)
            nc.scalar.activation(oraw[:, s % 2, :], ps[:, 7, 0:P], ACT.Copy).then_inc(o_free, 1)

        for i in range(8):
            prepare(i)
        for s in range(-1, STEPS + 2):
            if s + 1 < STEPS:
                exponentials(s + 1, 0)
            if s + 9 < 8 * H_B:
                prepare(s + 9)
            if 0 <= s - 1 < STEPS:
                weights_out(s - 1)
            if s + 1 < STEPS:
                exponentials(s + 1, 1)
            if 0 <= s - 2:
                out_square(s - 2)
            if 0 <= s < 4:
                split_hi(G_O2 + s)

        def exps2(w):
            act.wait_ge(smp_max, w + 1)
            if w < 2:
                act.wait_ge(smp_w_zero, 1)
            else:
                act.wait_ge(smp_w_turned, w - 1)
                act.wait_ge(smp_w_zero, w)
                act.wait_ge(smp_coef, w - 1)
            b = w // 2
            nc.scalar.activation(PS[:, w % 2, 0:512], ps[:, w % 2, :], ACT.Exp, bias=nmx[:, w % 2, 0:1],
                                 scale=HD ** -0.5, accum_out=ls[:, w % 2, 0:1]).then_inc(smp_exp, 1)
            nc.scalar.activation(PS[:, w % 2, 512 + 16 * b:528 + 16 * b], ps[:, 2, 0:16], ACT.Exp,
                                 bias=nmx[:, w % 2, 0:1], scale=HD ** -0.5,
                                 accum_out=ls[:, w % 2, 1:2]).then_inc(smp_exp, 1)

        def weights2(w):
            act.wait_ge(smp_w_turned, w + 1)
            if w >= 2:
                act.wait_ge(smp_pv, w - 1)
            nc.scalar.activation(ATs[:, w % 2, 0:4, :], ps[:, 6, :].rearrange("p (k n) -> p k n", k=4), ACT.Copy)
            nc.scalar.activation(ATs[:, w % 2, 4, :], ps[:, 3, 0:P], ACT.Copy).then_inc(smp_w_copied, 1)

        def sample_square(w):
            act.wait_ge(smp_out, w + 1)
            if w == 0:
                for i in range(2):
                    act.wait_ge(o_out[i], 16 * STEPS // 2)
            if w:
                act.wait_ge(smp_sq, w)
            nc.scalar.activation(sqS[:], oW[:, w, :], ACT.Square, scale=VD ** -0.5,
                                 accum_out=ssS[:, w:w + 1]).then_inc(smp_sq, 1)

        def cache_keys(w):
            for hh in (0, 2):
                act.wait_ge(cache_turned, 4 * w + hh + 1)
                if w >= 2:
                    act.wait_ge(smp_s_full, w - 1)
                nc.scalar.activation(KTb[:, w % 2, hh, :], ps[:, 4, :], ACT.Copy).then_inc(keys_copied0, 1)

        act.wait_ge(smp_qk_copied, 4)
        cache_keys(0)
        cache_keys(1)
        exps2(0)
        for w in range(2 * STREAMS):
            if w + 2 < 2 * STREAMS:
                cache_keys(w + 2)
            if w + 1 < 2 * STREAMS:
                exps2(w + 1)
            weights2(w)
            if w >= 2:
                sample_square(w - 2)
        for w in (2 * STREAMS - 2, 2 * STREAMS - 1):
            sample_square(w)
        for t in range(TILES):
            for half in range(2):
                transposed_hi(TU_O2 + 2 * t + half, XTR[0], t, half)
        for j in range(4):
            split_hi(G_O2 + 4 + j)
        residual_norm(1, G_O2 + 4)
        mlp(1)

    @block.tensor
    def _(pe):
        def t_bank(u, bank=None):
            if bank is not None:
                pe.wait_ge(t_free, u - 1)
                return bank
            if u >= 2:
                pe.wait_ge(t_free, u - 1)
            return 6 + u % 2

        def transposes(u, src, t, half):
            b = t_bank(u)
            for k in range(4):
                last = nc.tensor.transpose(ps[:, b, k * P:(k + 1) * P],
                                           src[:, t, (4 * half + k) * P:(4 * half + k + 1) * P], ident)
            last.then_inc(t_full, 1)

        def quarter_cols(g, u, xt, ng, M=P, w=None, bank=None):
            b = t_bank(u, bank)
            for k in range(KT):
                for i, (a, c) in enumerate(PASSES):
                    st = wsplit[:, g % 4, a, k * P:(k + 1) * P] if w is None else w[:, a, k, :]
                    last = nc.tensor.matmul(ps[0:M, b, 0:GW], st, xt[:, c, k, ng * GW:(ng + 1) * GW],
                                            start=(k == 0 and i == 0), stop=(k == KT - 1 and i == 2))
            last.then_inc(t_full, 1)

        def product(g, use, xt, before=None):
            for grp in range(NG):
                for j in range(4):
                    if before:
                        before(4 * grp + j)
                    pe.wait_ge(lo_done, g + j + 1)
                    for t in range(GROUP):
                        u = use + grp * GROUP + t
                        if j == 0 and u >= 6:
                            pe.wait_ge(g_free, u - 5)
                        tok = (grp * GROUP + t) * P
                        for k in range(2):
                            for i, (a, c) in enumerate(PASSES):
                                last = nc.tensor.matmul(
                                    ps[:, u % 6, :], xt[:, a, 2 * j + k, tok:tok + P],
                                    wsplit[:, (g + j) % 4, c, k * 512:(k + 1) * 512],
                                    start=(j == 0 and k == 0 and i == 0), stop=(j == 3 and k == 1 and i == 2))
                        if j == 3:
                            last.then_inc(g_full, 1)
                    if grp == NG - 1 and j < 3:
                        last.then_inc(w_used, 1)

        pe.wait_ge(const_in, 16)
        for t in range(TILES):
            pe.wait_ge(tile_in[t], 16)
            for half in range(2):
                transposes(TU_X0 + 2 * t + half, xin, t, half)
        pe.wait_ge(t_free, TU_GL)
        pe.wait_ge(gl_lo, 1)
        for ng in range(NG):
            quarter_cols(0, TU_GL + ng, XTR[0], ng, M=16, w=wgls)
        for m in range(8):
            pe.wait_ge(lo_done, m + 1)
            for ng in range(NG):
                quarter_cols(m, TU_Q + 3 * m + ng, XTR[0], ng)

        def logits(v_step):
            def f(step):
                step += 12 * v_step
                if step not in LOG_AT:
                    return
                h, ng = LOG_AT[step]
                u = TU_LOG + step // 2
                b = t_bank(u)
                if step == 0:
                    pe.wait_ge(wgu_in, 16)
                nc.tensor.matmul(ps[:, b, 0:GW], wgu[:, h * DK:(h + 1) * DK], glT[ng],
                                 start=True, stop=True).then_inc(t_full, 1)
            return f
        for u in range(2):
            product(G_V + 4 * u, GU_V + TILES * u, XTR[0], before=logits(u))
        for u in range(2):
            product(G_R + 4 * u, GU_R + TILES * u, XTR[0])

        pe.wait_ge(g_free, GU_O)
        pe.wait_ge(t_free, TU_O1)
        pe.wait_ge(qk_scaled, 3 * H_A * NG)

        def scores(s):
            t, h = s // H_A, s % H_A
            pe.wait_ge(decayed_keys, s + 1)
            if s:
                pe.wait_ge(keys_by_token, s)
                pe.wait_ge(scores_masked, s)
            nc.tensor.transpose(ps[:, 0, 0:P], ktT[:, s % 2, :], ident).then_inc(keys_turned, 1)
            nc.tensor.matmul(ps[:, 1, 0:P], qkT[:, 1, h, t * P:(t + 1) * P], qkT[:, 0, h, t * P:(t + 1) * P],
                             start=True, stop=True).then_inc(scan_scores, 1)

        def outputs(s):
            t, h = s // H_A, s % H_A
            pe.wait_ge(keys_by_token, s + 1)
            for c in range(2):
                if s:
                    pe.wait_ge(state_updated, 2 * (s - 1) + c + 1)
                nc.tensor.matmul(ps[:, 2 + c, 0:DV], kts[c * CH:(c + 1) * CH, s % 2, :],
                                 vO[c * CH:(c + 1) * CH, t, h * DV:(h + 1) * DV],
                                 start=True, stop=True).then_inc(scan_kv, 1)
            pe.wait_ge(scores_masked, s + 1)
            if t >= 2 and h % 2 == 0:
                pe.wait_ge(scan_normed, 2 * (t - 2) + h // 2 + 1)
            o = ps[:, 4 + 2 * (t % 2) + h // 2, (h % 2) * DV:(h % 2 + 1) * DV]
            nc.tensor.matmul(o, attm[:, s % 2, :], vO[:, t, h * DV:(h + 1) * DV], start=True, stop=True)
            q = qkT[:, 0, h, t * P:(t + 1) * P]
            if t:
                pe.wait_ge(state_updated, 2 * (s - 4) + 2)
                nc.tensor.matmul(o[0:CH], q[:, 0:CH], S[:, 0, h, :], start=False, stop=True,
                                 skip_group_check=True).then_inc(state_read0, 1)
            pe.wait_ge(state_updated, 2 * s + 1)
            nc.tensor.matmul(o[CH:P], q[:, CH:P], S[:, 1, h, :], start=False, stop=True,
                             skip_group_check=True).then_inc(scan_out, 1)

        steps = PT * H_A
        scores(0)
        for s in range(steps):
            if s + 1 < steps:
                scores(s + 1)
            outputs(s)

        pe.wait_ge(smp_decayed, 4)
        pe.wait_ge(keys_by_token, steps)
        pe.wait_ge(scores_masked, steps)
        tok = slice(PT * P, TOK)
        for h in range(H_A):
            nc.tensor.transpose(ps[:, 0, h * P:(h + 1) * P], ktS[:, h, :], ident).then_inc(smp_turned, 1)
            last = nc.tensor.matmul(ps[:, 1, h * P:(h + 1) * P], qkT[:, 1, h, tok], qkT[:, 0, h, tok],
                                    start=True, stop=True)
        last.then_inc(smp_scores, 1)
        pe.wait_ge(smp_states_in, 16 * STREAMS)
        pe.wait_ge(scan_normed, 2 * PT - 2)
        for i in range(8):
            h, vh = i // 2, i % 2
            for b in range(STREAMS):
                last = nc.tensor.matmul(ps[:, 4 + i // 4, (i % 4) * P + b * 16:(i % 4) * P + b * 16 + 16],
                                        Ss[:, b, h, vh * P:(vh + 1) * P],
                                        qkT[:, 0, h, PT * P + b * 16:PT * P + b * 16 + 16],
                                        start=True, stop=True)
        last.then_inc(smp_state_out, 1)
        pe.wait_ge(smp_masked, 1)
        pe.wait_ge(smp_out_copied, 1)
        pe.wait_ge(scan_normed, 2 * PT)
        for h in range(H_A):
            o = ps[:, 6 + h // 2, (h % 2) * DV:(h % 2 + 1) * DV]
            nc.tensor.matmul(o, attS[:, h, :], vO[:, PT, h * DV:(h + 1) * DV], start=True, stop=True)
            for vh in range(2):
                last = nc.tensor.matmul(o[:, vh * P:(vh + 1) * P], oT[:, 2 * h + vh, :], ident,
                                        start=False, stop=True, skip_group_check=True)
            last.then_inc(scan_out, 1)
        pe.wait_ge(smp_blocks, 1)
        for b in range(STREAMS):
            for hp in range(2):
                i = 2 * b + hp
                if i >= 4:
                    pe.wait_ge(smp_updated, i - 3)
                for k in range(2):
                    h = 2 * hp + k
                    last = nc.tensor.matmul(ps[:, i % 4, k * DV:(k + 1) * DV], ktb[:, b, h * P:(h + 1) * P],
                                            vO[:, PT, h * DV:(h + 1) * DV], start=True, stop=True)
                last.then_inc(smp_kv, 1)
        def gated_tile(t):
            pe.wait_ge(gated, t + 1)
            for half in range(2):
                transposes(TU_O1 + 2 * t + half, vO, t, half)

        def down(g, use, hidden, order, before=None):
            v = 0
            for nh, grp in order:
                if before:
                    before(nh, grp)
                for kp in range(2):
                    q = 2 * nh + kp
                    pe.wait_ge(lo_done, g + q + 1)
                    if nh == 0:
                        pe.wait_ge(up_done, hidden[kp][grp])
                    for t in range(GROUP):
                        if kp == 0:
                            pe.wait_ge(g_free, use + v + t - 5)
                        tok = (grp * GROUP + t) * P
                        for k in range(2):
                            for i, (a, b) in enumerate(PASSES):
                                last = nc.tensor.matmul(
                                    ps[:, (v + t) % 6, :], hT[:, a, 2 * kp + k, tok:tok + P],
                                    wsplit[:, q, b, k * 512:(k + 1) * 512],
                                    start=(kp == 0 and k == 0 and i == 0),
                                    stop=(kp == 1 and k == 1 and i == 2))
                        if kp == 1:
                            last.then_inc(g_full, 1)
                        elif t == GROUP - 1 and grp == NG - 1:
                            last.then_inc(w_used, 1)
                v += GROUP

        def up(u, m, ng, xt, g, bank=None):
            if ng == 0:
                pe.wait_ge(lo_done, g + m + 1)
            quarter_cols(m, u, xt, ng, bank=bank)

        def product_norm(lay, g, use, xt_in, xt_out, tile, uses):
            seq = after_norm(lay)

            def first_group(step):
                if 8 <= step < 11:
                    for u, _, t, half in seq[2 * (step - 8):2 * (step - 8) + 2]:
                        if half == 0:
                            pe.wait_ge(ln_done, 2 * lay * TILES + t + 1)
                        transposes(u, X, t, half)

            def next_tiles(step):
                if step % 4 == 0:
                    pe.wait_ge(t_free, uses + 2 * GROUP * (step // 4 + 1))
                elif step < 8:
                    tile(step // 4 * GROUP + step % 4 + GROUP - 1)
            for t in range(GROUP):
                tile(t)
            product(g, use, xt_in, before=next_tiles)
            product(g + 4, use + TILES, xt_in, before=first_group)
            for u, kind, p, q in seq[2 * GROUP:]:
                if kind == "tr":
                    if q == 0:
                        pe.wait_ge(ln_done, 2 * lay * TILES + p + 1)
                    transposes(u, X, p, q)
                else:
                    if p == 0:
                        pe.wait_ge(t_free, max(e[0] for e in seq if e[1] == "tr" and e[2] // GROUP == q) + 1)
                    up(u, p, q, xt_out, G_MLP[lay])

        def normed_transposes(grp):
            for t in range(grp * GROUP, (grp + 1) * GROUP):
                pe.wait_ge(ln_done, TILES + t + 1)
                for half in range(2):
                    transposes(TU_L[1] + 2 * t + half, X, t, half)

        def mlp(lay, xt):
            g = G_MLP[lay]
            first = [[UPS * lay + FIRST_UP.index((2 * kp + 1, grp)) + 1 for grp in range(NG)] for kp in range(2)]
            down(g + 4, GU_MLP[lay], first, DOWN_ORDER[0])

            def first_group(nh, grp):
                if lay == 0 and (nh, grp) == (1, NG - 1):
                    normed_transposes(0)

            def chunk(c, order, before=None):
                for m in range(4):
                    for ng in range(NG):
                        k = 3 * m + ng
                        up(12 * c + (TU_UP[lay] + k), m, ng, xt, 8 * c + g, bank=6 + (TU_UP[lay] + k) % 2)
                hidden = [[12 * c + (UPS * lay + n + grp) for grp in range(NG)] for n in (4, 10)]
                down(8 * c + (g + 4), 2 * TILES * c + GU_MLP[lay], hidden, order, before)
            with pe.Fori(1, NFC - 1) as c:
                chunk(c, DOWN_ORDER[0])
            chunk(NFC - 1, DOWN_ORDER[1], first_group)

        product_norm(0, G_O, GU_O, XTR[1], XTR[2], gated_tile, TU_O1)
        mlp(0, XTR[2])
        def next_group(step):
            if step in (3, 7):
                normed_transposes(step // 4 + 1)
            if step % 4 == 0:
                pe.wait_ge(t_free, TU_L[1] + 2 * GROUP * (step // 4 + 1))
        for u in range(6):
            product(G_KVQ + 4 * u, GU_KVQ + TILES * u, XTR[3], before=next_group if u == 0 else None)

        pe.wait_ge(g_free, GU_O2)
        pe.wait_ge(t_free, TU_O2)

        def prepare(i):
            h, j = i // 8, i % 8
            pair = 4 * h + j // 2
            if j % 2 == 0:
                pe.wait_ge(pair_loaded[pair % 2], 128 * (pair // 2 + 1))
            if i >= 4:
                pe.wait_ge(turned_free, i if i >= 8 else i - 3)
            for k in range(4):
                last = nc.tensor.transpose(ps[:, p_bank(i), k * P:(k + 1) * P],
                                           kqd[:, pair % 2, k, j % 2].rearrange("p a d -> p (a d)"), ident)
            last.then_inc(turned_full, 1)

        def scores(s, c):
            h, i = s // PT, s % PT
            w = (i + 1) * P
            if i in (0, 4):
                pe.wait_ge(turned_free, 8 * h + (6 if i == 0 else 8))
            if s:
                pe.wait_ge(exp_done, 2 * (s - 1) + c + 1)
            for b in range((w + 511) // 512):
                n = min(512, w - 512 * b)
                o = ps[:, 2 * c + b, 0:n]
                q = QS[:, h % 2, c, i * P:(i + 1) * P]
                nc.tensor.matmul(o, q, KD[:, h % 2, 0, c, 512 * b:512 * b + n], start=True, stop=False)
                nc.tensor.matmul(o, q, KD[:, h % 2, 1, c, 512 * b:512 * b + n], start=False, stop=True)
            nc.tensor.matmul(ps[:, 2 * c + b, n - P:n], mrow[:, 0:P], mrow[:, P:2 * P],
                             start=False, stop=True, skip_group_check=True).then_inc(s_full, 1)

        def weights(s):
            pe.wait_ge(combined, s + 1)
            for bank, tiles, use in a_banks(s):
                if use:
                    pe.wait_ge(a_free[bank], use)
                for k, kt in enumerate(tiles):
                    last = nc.tensor.transpose(ps[:, 5 + bank, k * P:(k + 1) * P],
                                               PR[:, s % 4, 0, kt * P:(kt + 1) * P], ident)
                last.then_inc(a_full[bank], 1)

        def values(s):
            h, i = s // PT, s % PT
            for bank, _, use in a_banks(s):
                pe.wait_ge(a_free[bank], use + 1)
            if i == 0:
                pe.wait_ge(values_loaded[h % 3], 16 * (h // 3 + 1))
            if s:
                pe.wait_ge(o_free, s)
            for kt in range(i + 1):
                last = nc.tensor.matmul(ps[:, 7, 0:P], AT[:, s % 2, kt, :], vhead[:, h % 3, kt, :],
                                        start=(kt == 0), stop=(kt == i))
            last.then_inc(o_full, 1)

        pe.wait_ge(mask_in, 16)
        for i in range(8):
            prepare(i)
        for s in range(-1, STEPS + 2):
            if s + 1 < STEPS:
                scores(s + 1, 0)
            if s + 9 < 8 * H_B:
                prepare(s + 9)
            if 0 <= s - 1 < STEPS:
                weights(s - 1)
            if s + 1 < STEPS:
                scores(s + 1, 1)
            if 0 <= s - 2:
                values(s - 2)

        pe.wait_ge(smp_qk_in, 32)
        pe.wait_ge(prompt_done, 1)
        for i in range(2):
            for z in range(2):
                for k in range(4):
                    last = nc.tensor.transpose(ps[:, 2 * i + z, k * P:(k + 1) * P],
                                               kqS[:, i, (4 * z + k) * P:(4 * z + k + 1) * P], ident)
                last.then_inc(smp_qk_turned, 1)
        pe.wait_ge(smp_qk_copied, 4)

        def cache_keys(w, hh):
            b, z = w // 2, w % 2
            if z == 0 and hh == 0:
                pe.wait_ge(kc_in[b % 2], 16 * (b // 2 + 1))
            ev = (keys_copied0, keys_copied1)[hh % 2]
            n = 2 * w + hh // 2
            if n:
                pe.wait_ge(ev, n)
            for kt in range(4):
                last = nc.tensor.transpose(ps[:, 4 + hh % 2, kt * P:(kt + 1) * P],
                                           Kc[:, b % 2, kt, (4 * z + hh) * P:(4 * z + hh + 1) * P], ident)
            last.then_inc(cache_turned, 1)

        def scores2(w, hh):
            b, z = w // 2, w % 2
            if hh == 0:
                pe.wait_ge(smp_q_blocks, 8 * (b + 1))
                pe.wait_ge(keys_copied0, 2 * w + 2)
                pe.wait_ge(keys_copied1, 2 * w + 2)
                if w >= 2:
                    pe.wait_ge(smp_exp, 2 * w - 2)
            nc.tensor.matmul(ps[:, w % 2, :], Qbd[:, b % 2, 4 * z + hh, :], KTb[:, w % 2, hh, :],
                             start=(hh == 0), stop=(hh == 3))
            if hh == 3:
                if w:
                    pe.wait_ge(smp_exp, 2 * w)
                for hn in range(4):
                    last = nc.tensor.matmul(ps[:, 2, 0:16], Qbd[:, b % 2, 4 * z + hn, :],
                                            KTn[:, 4 * z + hn, 16 * b:16 * b + 16],
                                            start=(hn == 0), stop=(hn == 3))
                last.then_inc(smp_s_full, 1)

        def weights2(w):
            pe.wait_ge(smp_exp, 2 * w + 2)
            pe.wait_ge(smp_select, w + 1)
            if w:
                pe.wait_ge(smp_w_copied, w)
            for kt in range(5):
                o = ps[:, 6, kt * P:(kt + 1) * P] if kt < 4 else ps[:, 3, 0:P]
                last = nc.tensor.matmul(o, PS[:, w % 2, kt * P:(kt + 1) * P],
                                        CM[:, w % 2, :], start=True, stop=True)
            last.then_inc(smp_w_turned, 1)

        def values2(w):
            b, z = w // 2, w % 2
            pe.wait_ge(smp_w_copied, w + 1)
            if w == 0:
                pe.wait_ge(smp_v_in, 16)
            if z == 0:
                pe.wait_ge(vc_in[b % 2], 16 * (b // 2 + 1))
            if w:
                pe.wait_ge(smp_out, w)
            for kt in range(5):
                v = (Vc[:, b % 2, kt, :] if kt < 4 else vS)[:, z * 512:(z + 1) * 512]
                last = nc.tensor.matmul(ps[:, 7, :], ATs[:, w % 2, kt, :], v, start=(kt == 0), stop=(kt == 4))
            last.then_inc(smp_pv, 1)

        for hh in range(4):
            cache_keys(0, hh)
        for w in range(-1, 2 * STREAMS):
            for hh in range(4):
                if w + 2 < 2 * STREAMS:
                    cache_keys(w + 2, hh)
                if w + 1 < 2 * STREAMS:
                    scores2(w + 1, hh)
            if w < 0:
                continue
            weights2(w)
            if w:
                values2(w - 1)
        values2(2 * STREAMS - 1)
        def attended_tile(t):
            pe.wait_ge(tile_in[t], 32)
            for half in range(2):
                u = TU_O2 + 2 * t + half
                if t < PT:
                    transposes(u, oin, t, half)
                else:
                    transposes(u, oS[:].unsqueeze(1), 0, half)

        product_norm(1, G_O2, GU_O2, XTR[0], XTR[4], attended_tile, TU_O2)
        mlp(1, XTR[4])

    @block.vector
    def _(dve):
        def transposed_lo(u, xt, t, half, n_hi):
            dve.wait_ge(t_hi, n_hi)
            dst = slice(t * P, (t + 1) * P)
            nc.vector.tensor_tensor(xt[:, 1, 4 * half:4 * half + 4, dst],
                                    ps[:, 6 + u % 2, :].rearrange("p (k n) -> p k n", n=P),
                                    xt[:, 0, 4 * half:4 * half + 4, dst].bitcast(F32),
                                    ALU.subtract).then_inc(t_free, 1)

        hi = 0
        for t in range(TILES):
            for half in range(2):
                hi += 1
                transposed_lo(TU_X0 + 2 * t + half, XTR[0], t, half, hi)
        for ng in range(NG):
            u = TU_GL + ng
            dve.wait_ge(t_full, u + 1)
            if ng == 0:
                dve.wait_ge(t_free, TU_GL)
            nc.vector.tensor_copy(glT[ng], ps[0:16, 6 + u % 2, 0:GW]).then_inc(t_free, 1)
        for m in range(8):
            for ng in range(NG):
                u = TU_Q + 3 * m + ng
                dve.wait_ge(t_full, u + 1)
                dst = qkT[:, m // 4, m % 4, ng * GW:(ng + 1) * GW]
                if m < 4:
                    nc.vector.tensor_scalar(dst, ps[:, 6 + u % 2, 0:GW], float(DK) ** -0.5, None,
                                            ALU.mult).then_inc(t_free, 1)
                else:
                    nc.vector.tensor_copy(dst, ps[:, 6 + u % 2, 0:GW]).then_inc(t_free, 1)
        chain = 0
        for step in range(24):
            if step in LOG_AT:
                h, ng = LOG_AT[step]
                i = step // 2
                u = TU_LOG + i
                dve.wait_ge(t_full, u + 1)
                if i:
                    dve.wait_ge(gate_cum, i)
                nc.vector.tensor_scalar(gm[:], ps[:, 6 + u % 2, 0:GW], bg[:, h:h + 1], 0.0, ALU.add,
                                        ALU.min).then_inc(gate_min, 1)
                dve.wait_ge(gate_min, 2 * i + 1)
                nc.vector.scalar_tensor_tensor(gna[:], gm[:], 2.0, ps[:, 6 + u % 2, 0:GW], ALU.mult,
                                               ALU.subtract).then_inc(gate_min, 1)
                dve.wait_ge(gate_min, 2 * i + 2)
                dve.sem_inc(t_free, 1)
                dve.wait_ge(gate_log, i + 1)
                nc.vector.tensor_tensor(gm[:], gm[:], gna[:], ALU.subtract).then_inc(gate_d, 1)
                dve.wait_ge(gate_d, i + 1)
                if i:
                    dve.wait_ge(gate_decays, 2 * i)
                pos, nscan = ng * GW, 0
                while pos < (ng + 1) * GW:
                    w = CH if pos < PT * P else SEQ_S
                    o = pos - ng * GW
                    last = nc.vector.tensor_tensor_scan(gb[:, o:o + w], cst[:, C_ONE:C_ONE + w], gm[:, o:o + w],
                                                        0.0, ALU.mult, ALU.add)
                    pos += w
                last.then_inc(gate_cum, 1)
                dve.wait_ge(gate_decays, 2 * i + 2)
                q = qkT[:, 0, h, ng * GW:(ng + 1) * GW]
                k = qkT[:, 1, h, ng * GW:(ng + 1) * GW]
                nc.vector.tensor_tensor(q, q, geb[:], ALU.mult).then_inc(qk_scaled, 1)
                nc.vector.tensor_tensor(k, k, genb[:], ALU.mult).then_inc(qk_scaled, 1)
                if ng < 2:
                    nc.vector.tensor_copy(elast[:, h, 6 * ng:6 * ng + 6], geb[:, CH - 1::CH]).then_inc(qk_scaled, 1)
                else:
                    nc.vector.tensor_copy(elast[:, h, 12:16], geb[:, CH - 1:4 * CH:CH])
                    nc.vector.tensor_copy(elast[:, h, 16:24], geb[:, 4 * CH + SEQ_S - 1::SEQ_S]).then_inc(qk_scaled, 1)
            if step % 4 == 3:
                for t in range(GROUP):
                    use = GU_V + (step // 4) * GROUP + t
                    dve.wait_ge(g_full, use + 1)
                    tile = use % TILES
                    nc.vector.tensor_copy(vO[:, tile, (use // TILES) * 512:(use // TILES + 1) * 512],
                                          ps[:, use % 6, :]).then_inc(g_free, 1)
        def denominator(n):
            dve.wait_ge(r_exp, n + 1)
            nc.vector.tensor_scalar(sie[:, n % 2, :], sie[:, n % 2, :], 1.0, None, ALU.add).then_inc(r_den, 1)

        denominator(0)
        for n in range(2 * TILES):
            use = GU_R + n
            dve.wait_ge(r_den, n + 1)
            nc.vector.reciprocal(sie[:, n % 2, :], sie[:, n % 2, :]).then_inc(r_recip, 1)
            if n + 1 < 2 * TILES:
                denominator(n + 1)
            dve.wait_ge(r_recip, n + 1)
            if n >= 2:
                dve.wait_ge(r_out[n % 2], 16 * (n // 2))
            nc.vector.tensor_tensor(sio[:, n % 2, :], ps[:, use % 6, :], sie[:, n % 2, :],
                                    ALU.mult).then_inc(r_silu, 1)
            dve.wait_ge(r_silu, n + 1)
            dve.sem_inc(g_free, 1)

        def mask(s):
            dve.wait_ge(scan_scores, s + 1)
            if s >= 2:
                dve.wait_ge(scan_out, s - 1)
            nc.vector.tensor_tensor(attm[:, s % 2, :], ps[:, 1, 0:P], cst[:, C_MP:C_MP + P],
                                    ALU.mult).then_inc(scores_masked, 1)

        def update(s):
            t, h = s // H_A, s % H_A
            dve.wait_ge(scan_kv, 2 * s + 1)
            if t:
                dve.wait_ge(scan_out, s - 3)
                nc.vector.scalar_tensor_tensor(S[:, 1, h, :], S[:, 0, h, :], elast[:, h, 2 * t:2 * t + 1],
                                               ps[:, 2, 0:DV], ALU.mult, ALU.add).then_inc(state_updated, 1)
            else:
                nc.vector.tensor_copy(S[:, 1, h, :], ps[:, 2, 0:DV]).then_inc(state_updated, 1)
            dve.wait_ge(scan_kv, 2 * s + 2)
            dve.wait_ge(state_updated, 2 * s + 1)
            if t:
                dve.wait_ge(state_read0, s + 1 - H_A)
            nc.vector.scalar_tensor_tensor(S[:, 0, h, :], S[:, 1, h, :], elast[:, h, 2 * t + 1:2 * t + 2],
                                           ps[:, 3, 0:DV], ALU.mult, ALU.add).then_inc(state_updated, 1)

        def mean_square(p):
            dve.wait_ge(squares_done, 2 * p + 2)
            if p >= 4:
                dve.wait_ge(rms_done, p - 3)
            nc.vector.tensor_scalar(ms[:, p % 4, :], ss[:, p % 4, :], 1.0 / DV, EPS, ALU.mult,
                                    ALU.add).then_inc(mean_sq_done, 1)

        def normed(p):
            t, hp = p // 2, p % 2
            dve.wait_ge(rms_done, p + 1)
            if p >= 2 * PT:
                dve.wait_ge(smp_kv, 2 * STREAMS)
            bank = 4 + 2 * (t % 2) + hp if t < PT else 6 + hp
            for k in range(2):
                h = 2 * hp + k
                last = nc.vector.scalar_tensor_tensor(vO[:, t, h * DV:(h + 1) * DV],
                                                      ps[:, bank, k * DV:(k + 1) * DV],
                                                      rs4[:, p % 4, k:k + 1], gna_g[:], ALU.mult, ALU.mult)
            last.then_inc(scan_normed, 1)

        dve.wait_ge(qk_scaled, 3 * H_A * NG)
        dve.wait_ge(g_full, GU_O)
        dve.wait_ge(gna_in, 16)
        for h in range(H_A):
            nc.vector.tensor_tensor(ktS[:, h, :].rearrange("p (b s) -> p b s", b=STREAMS),
                                    qkT[:, 1, h, PT * P:TOK].rearrange("p (b s) -> p b s", b=STREAMS),
                                    elast[:, h, 16:24].unsqueeze(2).broadcast_to([P, STREAMS, SEQ_S]),
                                    ALU.mult).then_inc(smp_decayed, 1)
        steps = PT * H_A
        mask(0)
        for s in range(steps):
            if s + 1 < steps:
                mask(s + 1)
            update(s)
            if s >= 2:
                if s % 2 == 0:
                    mean_square(s // 2 - 1)
                else:
                    normed(s // 2 - 1)
        mean_square(steps // 2 - 1)
        normed(steps // 2 - 1)
        dve.wait_ge(smp_scores, 1)
        nc.vector.tensor_tensor(attS[:], ps[:, 1, :].rearrange("p (h n) -> p h n", h=H_A),
                                cst[:, C_MS:C_MS + P].unsqueeze(1).broadcast_to([P, H_A, P]),
                                ALU.mult).then_inc(smp_masked, 1)
        for p in (2 * PT, 2 * PT + 1):
            mean_square(p)
        dve.wait_ge(smp_state_out, 1)
        for b in range(STREAMS):
            for hp in range(2):
                i = 2 * b + hp
                dve.wait_ge(smp_kv, i + 1)
                for k in range(2):
                    h = 2 * hp + k
                    last = nc.vector.scalar_tensor_tensor(Ss[:, b, h, :], Ss[:, b, h, :],
                                                          elast[:, h, 16 + b:17 + b],
                                                          ps[:, i % 4, k * DV:(k + 1) * DV], ALU.mult, ALU.add)
                last.then_inc(smp_updated, 1)
        for p in (2 * PT, 2 * PT + 1):
            normed(p)
        def gate(t):
            dve.wait_ge(r_back[t % 2], 16 * (t // 2 + 1))
            if t == 0:
                dve.wait_ge(scan_normed, 2 * TILES)
            nc.vector.tensor_tensor(vO[:, t, :], vO[:, t, :], rin[:, t % 2, :], ALU.mult).then_inc(gated, 1)
        def gated_group(grp):
            for t in range(grp * GROUP, (grp + 1) * GROUP):
                if t + 1 < TILES:
                    gate(t + 1)
                for half in range(2):
                    lo_of(TU_O1 + 2 * t + half, XTR[1], t, half)

        hi_n = [hi]

        def lo_of(u, xt, t, half):
            hi_n[0] += 1
            transposed_lo(u, xt, t, half, hi_n[0])

        def residual(u, t, nh, scale, bank=None):
            bank = u % 6 if bank is None else bank
            dve.wait_ge(g_full, u + 1)
            x = X[:, t, nh * 512:(nh + 1) * 512]
            if scale is None:
                nc.vector.tensor_tensor(x, x, ps[:, bank, :], ALU.add).then_inc(g_free, 1)
            else:
                nc.vector.scalar_tensor_tensor(x, x, scale, ps[:, bank, :], ALU.mult, ALU.add).then_inc(g_free, 1)

        def tile_stats(i, t, uses):
            dve.wait_ge(g_free, uses)
            for k in range(2):
                nc.vector.bn_stats(bst[:, i % 3, 6 * k:6 * k + 6], X[:, t, k * 512:(k + 1) * 512]).then_inc(ln_st, 1)
            dve.wait_ge(ln_st, 3 * i + 2)
            nc.vector.bn_aggr(mv[:, i % 3, :], bst[:, i % 3, :]).then_inc(ln_st, 1)
            dve.wait_ge(ln_st, 3 * i + 3)
            nc.vector.tensor_scalar(mv[:, i % 3, 1:2], mv[:, i % 3, 1:2], EPS, None, ALU.add).then_inc(ln_var, 1)

        def shift(i):
            dve.wait_ge(ln_rstd, i + 1)
            nc.vector.scalar_tensor_tensor(nmr[:, i % 3:i % 3 + 1], mv[:, i % 3, 0:1], -1.0,
                                           rstd[:, i % 3:i % 3 + 1], ALU.mult, ALU.mult).then_inc(ln_nmr, 1)

        def bias(n, t):
            dve.wait_ge(ln_gain, n * TILES + t + 1)
            nc.vector.tensor_tensor(X[:, t, :], X[:, t, :], lng[:, 1, :], ALU.add).then_inc(ln_done, 1)

        def biases(n, grp):
            for t in range(grp * GROUP, (grp + 1) * GROUP):
                bias(n, t)

        def hidden(n, u, slot, bank, first=False):
            if not first:
                dve.wait_ge(up_done, n - 1)
            dve.wait_ge(t_full, u + 1)
            nc.vector.tensor_scalar(hsq[:, slot, :], ps[:, bank, 0:GW], 0.0, None, ALU.max).then_inc(up_r, 1)
            dve.wait_ge(up_r, n + 1)
            dve.sem_inc(t_free, 1)

        def hidden_lo(n, m, ng, slot):
            dve.wait_ge(up_h, n + 1)
            dst = slice(ng * GW, (ng + 1) * GW)
            nc.vector.tensor_tensor(hT[:, 1, m, dst], hsq[:, slot, :], hT[:, 0, m, dst].bitcast(F32),
                                    ALU.subtract).then_inc(up_done, 1)

        def product_norm(lay, use, xt, low_halves):
            n = 2 * lay
            low_halves(0)
            for grp in range(NG):
                if grp + 1 < NG:
                    low_halves(grp + 1)
                if lay == 0 and grp == 0:
                    dve.wait_ge(x_res_in, 16 * TILES)
                for t in range(grp * GROUP, (grp + 1) * GROUP):
                    residual(use + t, t, 0, ALPHA)
            use += TILES
            seq = after_norm(lay)

            def last_products(grp):
                for t in range(grp * GROUP, (grp + 1) * GROUP):
                    residual(use + t, t, 1, ALPHA)
                    tile_stats(n * TILES + t, t, use + t + 1)

            def shifts(grp):
                for t in range(grp * GROUP, (grp + 1) * GROUP):
                    shift(n * TILES + t)
            last_products(0)
            shifts(0)
            biases(n, 0)
            last_products(1)
            shifts(1)
            for u, _, t, half in seq[:2 * GROUP]:
                lo_of(u, xt, t, half)
            last_products(2)
            bias(n, GROUP)
            k, last = 0, None
            for u, kind, p, q in seq[2 * GROUP:]:
                if kind == "tr":
                    if last:
                        hidden_lo(*last)
                        last = None
                    lo_of(u, xt, p, q)
                else:
                    n_up = UPS * lay + k
                    hidden(n_up, u, k % 2, 6 + u % 2, first=n_up < 2)
                    if last:
                        hidden_lo(*last)
                    last = (n_up, p, q, k % 2)
                    if k < 2:
                        bias(n, GROUP + 1 + k)
                    if k == 1:
                        shifts(2)
                    if 3 <= k < 6:
                        bias(n, 2 * GROUP + k - 3)
                    k += 1
            hidden_lo(*last)

        def normed_transposes(grp):
            for t in range(grp * GROUP, (grp + 1) * GROUP):
                for half in range(2):
                    lo_of(TU_L[1] + 2 * t + half, XTR[3], t, half)

        def mlp(lay):
            n = 2 * lay + 1

            def ups(c):
                for k in range(12):
                    n_up = 12 * c + (UPS * lay + k)
                    hidden(n_up, 12 * c + (TU_UP[lay] + k), k % 2, 6 + (TU_UP[lay] + k) % 2)
                    if k:
                        hidden_lo(12 * c + (UPS * lay + k - 1), *divmod(k - 1, NG), (k - 1) % 2)
                hidden_lo(12 * c + (UPS * lay + 11), 3, 2, 1)

            def downs(c, scale=None):
                for v, (nh, t) in enumerate((nh, t) for nh in range(2) for t in range(TILES)):
                    residual(2 * TILES * c + (GU_MLP[lay] + v), t, nh, scale, bank=v % 6)

            def last_downs():
                use = GU_MLP[lay] + 2 * TILES * (NFC - 1)
                for nh, grp in DOWN_ORDER[1]:
                    for t in range(grp * GROUP, (grp + 1) * GROUP):
                        residual(use, t, nh, None)
                        use += 1
                        if nh == 1:
                            tile_stats(n * TILES + t, t, use)
                            if t % GROUP:
                                shift(n * TILES + t - 1)
                    if nh == 1:
                        shift(n * TILES + t)
                    elif grp:
                        if lay == 0 and grp == NG - 1:
                            normed_transposes(0)
                        biases(n, grp - 1)
            downs(0, ALPHA)
            with dve.Fori(1, NFC - 1) as c:
                ups(c)
                downs(c)
            ups(NFC - 1)
            last_downs()

        gate(0)
        product_norm(0, GU_O, XTR[2], gated_group)
        mlp(0)
        for grp in range(NG):
            if grp == 2:
                biases(1, grp)
            if grp:
                normed_transposes(grp)

        nr = [0]
        for u in range(6):
            for t in range(TILES):
                n = u * TILES + t
                use = GU_KVQ + n
                dve.wait_ge(g_full, use + 1)
                if n >= 6:
                    dve.wait_ge(kv_out[n % 6], 16 * (n // 6))
                if u in (2, 3):
                    nc.vector.tensor_copy(kvs[:, n % 6, :], ps[:, use % 6, :]).then_inc(kv_done, 1)
                    dve.wait_ge(kv_done, n + 1)
                    dve.sem_inc(g_free, 1)
                    continue
                nc.vector.tensor_copy(kvs[:, n % 6, :], ps[:, use % 6, :]).then_inc(g_free, 1)
                dve.wait_ge(g_free, use + 1)
                v = kvs[:, n % 6, :].rearrange("p (g d) -> p g d", d=HD)
                x1, x2 = v[:, :, 0:ROT], v[:, :, ROT:2 * ROT]
                cos = cst[:, C_COS + t * ROT:C_COS + (t + 1) * ROT].unsqueeze(1).broadcast_to([P, 8, ROT])
                sin = cst[:, C_SIN + t * ROT:C_SIN + (t + 1) * ROT].unsqueeze(1).broadcast_to([P, 8, ROT])
                r = [rtmp[:, n % 2, i] for i in range(4)]
                for i, (x, tab) in enumerate(((x1, cos), (x2, sin), (x2, cos), (x1, sin))):
                    nc.vector.tensor_tensor(r[i], x, tab, ALU.mult).then_inc(rope, 1)
                nr[0] += 4
                dve.wait_ge(rope, nr[0])
                nc.vector.tensor_tensor(x1, r[0], r[1], ALU.subtract).then_inc(rope, 1)
                nr[0] += 1
                nc.vector.tensor_tensor(x2, r[2], r[3], ALU.add).then_inc(kv_done, 1)
                dve.wait_ge(rope, nr[0])
                dve.wait_ge(kv_done, n + 1)

        dve.wait_ge(lam_in, 16)
        dve.wait_ge(gnb_in, 16)
        for i in range(2):
            nc.vector.tensor_tensor(lamp[:, i, :], lamt[:, 2 * i, :], lamt[:, 2 * i + 1, :], ALU.mult).then_inc(dve_steps, 1)
        dve.wait_ge(dve_steps, 2)
        for i in range(2):
            nc.vector.reduce_sum(lam2[:, i:i + 1], lamp[:, i, :], AX.X).then_inc(lam_p, 1)
        nc.vector.tensor_scalar(gnb[:], gnb[:], 1.0 - LAMBDA_INIT, None, ALU.mult).then_inc(dve_steps, 1)
        dve.wait_ge(lam_e, 1)
        nc.vector.tensor_tensor(nlam, lam2[:, 1:2], lam2[:, 0:1], ALU.subtract).then_inc(dve_steps, 1)
        dve.wait_ge(dve_steps, 4)
        nc.vector.tensor_scalar(nlam, nlam, LAMBDA_INIT, None, ALU.subtract).then_inc(dve_steps, 1)
        dve.wait_ge(dve_steps, 5)
        nc.vector.scalar_tensor_tensor(sgl, cst[:, C_SG + 1:C_SG + 2], nlam, cst[:, C_SG:C_SG + 1],
                                       ALU.mult, ALU.add).then_inc(lambda_done, 1)

        def prepare(i):
            h, j = i // 8, i % 8
            dve.wait_ge(turned_hi, i + 1)
            c, part = j % 2, j % 4 // 2
            cols = slice(part * 512, (part + 1) * 512)
            if j < 4:
                nc.vector.tensor_tensor(KD[:, h % 2, 1, c, cols], ps[:, p_bank(i), :], KD[:, h % 2, 0, c, cols].bitcast(F32),
                                        ALU.subtract).then_inc(turned_free, 1)
            else:
                q = QS[HD:P, h % 2, c, cols]
                nc.vector.tensor_tensor(q, ps[HD:P, p_bank(i), :], q.bitcast(F32), ALU.subtract).then_inc(turned_free, 1)

        def maxima(s, c):
            w = (s % PT + 1) * P
            if s >= 2:
                dve.wait_ge(negmax_done, 2 * s - 3 + c)
            dve.wait_ge(s_full, 2 * s + c + 1)
            nc.vector.reduce_max(mx[:, s % 2, c:c + 1], ps[:, 2 * c:2 * c + 2, :].rearrange("p a n -> p (a n)")[:, 0:w],
                                 AX.X).then_inc(max_done, 1)
            dve.wait_ge(max_done, 2 * s + c + 1)
            nc.vector.tensor_scalar(nmx[:, s % 2, c:c + 1], mx[:, s % 2, c:c + 1], -float(HD) ** -0.5, None,
                                    ALU.mult).then_inc(negmax_done, 1)

        def combine(s):
            w = (s % PT + 1) * P
            dve.wait_ge(balance_done, s + 1)
            dve.wait_ge(exp_done, 2 * s + 2)
            nc.vector.scalar_tensor_tensor(PR[:, s % 4, 0, 0:w], PR[:, s % 4, 1, 0:w], gf[:, s % 4:s % 4 + 1],
                                           PR[:, s % 4, 0, 0:w], ALU.mult, ALU.add).then_inc(combined, 1)

        def weights_out(s):
            for bank, tiles, use in a_banks(s):
                if bank == 1:
                    dve.wait_ge(a_full[1], use + 1)
                    if s >= 2:
                        dve.wait_ge(o_full, s - 1)
                    n = len(tiles)
                    nc.vector.tensor_copy(AT[:, s % 2, tiles[0]:tiles[0] + n, :],
                                          ps[:, 6, 0:n * P].rearrange("p (k n) -> p k n", n=P)).then_inc(a_free[1], 1)

        def out_norm(s):
            dve.wait_ge(factor_done, s + 1)
            dve.wait_ge(o_free, s + 1)
            if s >= 2:
                dve.wait_ge(o_out[s % 2], 16 * (s // 2))
            nc.vector.scalar_tensor_tensor(osb[:, s % 2, :], oraw[:, s % 2, :], of[:, s % 4:s % 4 + 1], gnb[:],
                                           ALU.mult, ALU.mult).then_inc(out_normed, 1)

        for i in range(8):
            prepare(i)
        for s in range(-1, STEPS + 3):
            if s + 1 < STEPS:
                maxima(s + 1, 0)
            if 0 <= s - 1 < STEPS:
                weights_out(s - 1)
            if s + 1 < STEPS:
                maxima(s + 1, 1)
            if 0 <= s < STEPS:
                combine(s)
            if s + 9 < 8 * H_B:
                prepare(s + 9)
            if 0 <= s - 3:
                out_norm(s - 3)
        dve.wait_ge(out_normed, STEPS)
        dve.sem_inc(prompt_done, 1)

        for i in range(2):
            for z in range(2):
                dve.wait_ge(smp_qk_turned, 2 * i + z + 1)
                dst = (KTn, QTs)[i]
                nc.vector.tensor_copy(dst[:, 4 * z:4 * z + 4, :],
                                      ps[:, 2 * i + z, :].rearrange("p (k n) -> p k n", n=P)).then_inc(smp_qk_copied, 1)

        def cache_keys(w, hh):
            dve.wait_ge(cache_turned, 4 * w + hh + 1)
            if w >= 2:
                dve.wait_ge(smp_s_full, w - 1)
            nc.vector.tensor_copy(KTb[:, w % 2, hh, :], ps[:, 5, :]).then_inc(keys_copied1, 1)

        def maxima2(w):
            dve.wait_ge(smp_s_full, w + 1)
            nc.vector.reduce_max(mx[:, w % 2, 0:1], ps[:, w % 2, :], AX.X).then_inc(dve_steps, 1)
            nc.vector.reduce_max(mx[:, w % 2, 1:2], ps[:, 2, 0:16], AX.X).then_inc(dve_steps, 1)
            dve.wait_ge(dve_steps, 5 + 3 * w + 2)
            nc.vector.tensor_tensor(mx[:, w % 2, 0:1], mx[:, w % 2, 0:1], mx[:, w % 2, 1:2], ALU.max).then_inc(dve_steps, 1)
            dve.wait_ge(dve_steps, 5 + 3 * w + 3)
            nc.vector.tensor_scalar(nmx[:, w % 2, 0:1], mx[:, w % 2, 0:1], -float(HD) ** -0.5, None,
                                    ALU.mult).then_inc(smp_max, 1)

        def combination(w):
            dve.wait_ge(smp_coef, w + 1)
            if w >= 2:
                dve.wait_ge(smp_w_turned, w - 1)
            nc.vector.tensor_scalar(CM[:, w % 2, :], cst[:, C_SEL:C_SEL + P], coef[:, w % 2:w % 2 + 1], None,
                                    ALU.mult).then_inc(smp_select, 1)

        def outputs2(w):
            dve.wait_ge(smp_pv, w + 1)
            for hh in range(4):
                last = nc.vector.tensor_copy(oW[32 * hh:32 * hh + 32, w, :],
                                             ps[32 * hh:32 * hh + 32, 7, hh * P:(hh + 1) * P])
            last.then_inc(smp_out, 1)

        def sample_norm(w):
            dve.wait_ge(smp_rms, w + 1)
            nc.vector.scalar_tensor_tensor(oW[:, w, :], oW[:, w, :], rsS[:, w:w + 1], gnb[:],
                                           ALU.mult, ALU.mult).then_inc(smp_fin, 1)

        for hh in (1, 3):
            cache_keys(0, hh)
        for hh in (1, 3):
            cache_keys(1, hh)
        maxima2(0)
        for w in range(2 * STREAMS):
            if w + 2 < 2 * STREAMS:
                cache_keys(w + 2, 1)
            combination(w)
            if w + 2 < 2 * STREAMS:
                cache_keys(w + 2, 3)
            if w + 1 < 2 * STREAMS:
                maxima2(w + 1)
            if w:
                outputs2(w - 1)
            if w >= 3:
                sample_norm(w - 3)
        outputs2(2 * STREAMS - 1)
        for w in range(2 * STREAMS - 3, 2 * STREAMS):
            sample_norm(w)
        def attended_group(grp):
            for t in range(grp * GROUP, (grp + 1) * GROUP):
                for half in range(2):
                    lo_of(TU_O2 + 2 * t + half, XTR[0], t, half)

        product_norm(1, GU_O2, XTR[4], attended_group)
        mlp(1)
        biases(3, NG - 1)

    ctx.close()


_INS = ['x_prompt', 'x_sample', 'state_gla', 'cache_k', 'cache_v', 'w_in_a', 'w_gate_up_a', 'b_gate_a',
        'g_norm_a', 'w_o_a', 'w_kv', 'w_q_b', 'lam_b', 'g_norm_b', 'w_o_b', 'w_up', 'w_down', 'ln_g', 'ln_b']
_OUTS = [(1, 1024, 1024), (8, 16, 1024), (1, 1, 4, 128, 256), (1, 1024, 8, 2, 64), (1, 1024, 8, 128),
         (1, 8, 4, 128, 256), (8, 16, 8, 2, 64), (8, 16, 8, 128)]


def kernel(**inputs):
    import concourse.bacc as _bacc
    from concourse.bass_utils import run_bass_kernel_spmd as _run

    nc = _bacc.Bacc("TRN2", target_bir_lowering=False, num_devices=1)
    c, m = constants()
    arrays, args = {}, []
    inputs = dict(inputs, b_gate_a=np.asarray(inputs["b_gate_a"]).reshape(H_A, DK).T)
    for name, a in [(n, np.ascontiguousarray(inputs[n])) for n in _INS] + [("consts", c), ("maskrow", m)]:
        arrays[f"in_{name}"] = a
        args.append(nc.dram_tensor(f"in_{name}", a.shape, mybir.dt.from_np(a.dtype), kind="ExternalInput").ap())
    for i, shape in enumerate(_OUTS):
        args.append(nc.dram_tensor(f"out_{i}", shape, F32, kind="ExternalOutput").ap())
    encoder_step(nc, *args)
    r = _run(nc, [arrays], core_ids=[0])
    return tuple(r.results[0][f"out_{i}"] for i in range(len(_OUTS)))
```
